# Optimizing a Trainium2 kernel written in Bass

```python
import math
import jax, jax.numpy as jnp
from jax import lax
import numpy as np

D_MODEL = 1024
BATCH = 1
SEQ = 256
DEPTH = 1

N_META = 16
GRID_W = 64
Q_BLOCK = 128
HEAD_DIM = 64
ROPE_THETA = 10000.0
EPS = 1e-6
A_HEADS = 8
A_KV_HEADS = 2
A_GROUP = A_HEADS // A_KV_HEADS
A_WIDTH = A_HEADS * HEAD_DIM
A_KV_WIDTH = A_KV_HEADS * HEAD_DIM
B_HEADS = 4
B_VDIM = 2 * HEAD_DIM
B_WIDTH = B_HEADS * B_VDIM
MIX_WIDTH = A_WIDTH + B_WIDTH
IN_WIDTH = A_WIDTH + 2 * A_KV_WIDTH + 3 * B_WIDTH
D_FF = -(-8 * D_MODEL // (3 * 256)) * 256


def rms_norm(x, g):
    xf = x.astype(jnp.float32)
    y = xf * lax.rsqrt(jnp.mean(xf * xf, axis=-1, keepdims=True) + EPS)
    return (y * g.astype(jnp.float32)).astype(x.dtype)

def apply_rope(x, ang):
    xf = x.astype(jnp.float32).reshape(x.shape[:-1] + (x.shape[-1] // 2, 2))
    c = jnp.cos(ang)[None, :, None, :]
    s = jnp.sin(ang)[None, :, None, :]
    x1, x2 = xf[..., 0], xf[..., 1]
    out = jnp.stack([x1 * c - x2 * s, x1 * s + x2 * c], axis=-1)
    return out.reshape(x.shape).astype(x.dtype)

def rope_angles_1d(length):
    pos = jnp.arange(length, dtype=jnp.float32)
    inv = ROPE_THETA ** (-jnp.arange(0, HEAD_DIM, 2, dtype=jnp.float32) / HEAD_DIM)
    return pos[:, None] * inv[None, :]

def rope_angles_axial(n_tokens):
    rows = n_tokens // GRID_W
    r = jnp.repeat(jnp.arange(rows, dtype=jnp.float32), GRID_W)
    c = jnp.tile(jnp.arange(GRID_W, dtype=jnp.float32), rows)
    half = HEAD_DIM // 2
    inv = ROPE_THETA ** (-jnp.arange(0, half, 2, dtype=jnp.float32) / half)
    ang = jnp.concatenate([r[:, None] * inv[None, :], c[:, None] * inv[None, :]], axis=-1)
    meta = jnp.zeros((N_META, HEAD_DIM // 2), jnp.float32)
    return jnp.concatenate([meta, ang], axis=0)

def sweep_queries(fn, q):
    out_meta = fn(q[:, :N_META])
    real = q[:, N_META:]
    bsz, s = real.shape[0], real.shape[1]
    nb = s // Q_BLOCK
    blocks = jnp.moveaxis(real.reshape((bsz, nb, Q_BLOCK) + real.shape[2:]), 1, 0)
    out = lax.map(fn, blocks)
    out = jnp.moveaxis(out, 0, 1).reshape((bsz, s) + out.shape[3:])
    return jnp.concatenate([out_meta, out], axis=1)

def first_inputs(seed: int = 0) -> dict:
    key = jax.random.key(seed)
    ks = jax.random.split(key, 20)
    f32 = jnp.float32

    def gain(k, shape):
        return 1.0 + 0.1 * jax.random.normal(k, shape, f32)

    return {
        "x": jax.random.normal(ks[0], (BATCH, SEQ, D_MODEL), f32),
        "meta_tokens": jax.random.normal(ks[1], (N_META, D_MODEL), f32),
        "attn_norm_g": gain(ks[2], (DEPTH, D_MODEL)),
        "w_in": jax.random.normal(ks[3], (DEPTH, D_MODEL, IN_WIDTH), f32) * D_MODEL ** -0.5,
        "a_q_norm_g": gain(ks[4], (DEPTH, HEAD_DIM)),
        "a_k_norm_g": gain(ks[5], (DEPTH, HEAD_DIM)),
        "b_q_norm_g": gain(ks[6], (DEPTH, HEAD_DIM)),
        "b_k_norm_g": gain(ks[7], (DEPTH, HEAD_DIM)),
        "b_lambda_q1": 0.1 * jax.random.normal(ks[8], (DEPTH, HEAD_DIM), f32),
        "b_lambda_k1": 0.1 * jax.random.normal(ks[9], (DEPTH, HEAD_DIM), f32),
        "b_lambda_q2": 0.1 * jax.random.normal(ks[10], (DEPTH, HEAD_DIM), f32),
        "b_lambda_k2": 0.1 * jax.random.normal(ks[11], (DEPTH, HEAD_DIM), f32),
        "b_subln_g": gain(ks[12], (DEPTH, B_VDIM)),
        "w_out": jax.random.normal(ks[13], (DEPTH, MIX_WIDTH, D_MODEL), f32) * MIX_WIDTH ** -0.5,
        "ffn_norm_g": gain(ks[14], (DEPTH, D_MODEL)),
        "w_gate": jax.random.normal(ks[15], (DEPTH, D_MODEL, D_FF), f32) * D_MODEL ** -0.5,
        "w_up": jax.random.normal(ks[16], (DEPTH, D_MODEL, D_FF), f32) * D_MODEL ** -0.5,
        "w_down": jax.random.normal(ks[17], (DEPTH, D_FF, D_MODEL), f32) * D_FF ** -0.5,
    }

def first_block(x, meta_tokens, attn_norm_g, w_in, a_q_norm_g, a_k_norm_g, b_q_norm_g, b_k_norm_g,
              b_lambda_q1, b_lambda_k1, b_lambda_q2, b_lambda_k2, b_subln_g, w_out,
              ffn_norm_g, w_gate, w_up, w_down):
    bsz, s, _ = x.shape
    meta = jnp.broadcast_to(meta_tokens.astype(x.dtype)[None], (bsz, N_META, D_MODEL))
    x = jnp.concatenate([meta, x], axis=1)
    length = N_META + s

    ang_a = rope_angles_axial(s)
    ang_b = rope_angles_1d(length)
    scale = HEAD_DIM ** -0.5
    splits = np.cumsum([A_WIDTH, A_KV_WIDTH, A_KV_WIDTH, B_WIDTH, B_WIDTH]).tolist()

    for l in range(DEPTH):
        lam_init = 0.8 - 0.6 * math.exp(-0.3 * l)
        h = rms_norm(x, attn_norm_g[l])
        proj = jnp.einsum('bld,de->ble', h, w_in[l])
        qa, ka, va, qb, kb, vb = jnp.split(proj, splits, axis=-1)

        qa = apply_rope(rms_norm(qa.reshape(bsz, length, A_HEADS, HEAD_DIM), a_q_norm_g[l]), ang_a)
        ka = apply_rope(rms_norm(ka.reshape(bsz, length, A_KV_HEADS, HEAD_DIM), a_k_norm_g[l]), ang_a)
        va = va.reshape(bsz, length, A_KV_HEADS, HEAD_DIM)

        def gqa_block(q):
            nq = q.shape[1]
            qg = q.reshape(q.shape[0], nq, A_KV_HEADS, A_GROUP, HEAD_DIM)
            sc = jnp.einsum('bqkgd,blkd->bkgql', qg, ka).astype(jnp.float32) * scale
            p = jax.nn.softmax(sc, axis=-1).astype(va.dtype)
            o = jnp.einsum('bkgql,blkd->bqkgd', p, va)
            return o.reshape(q.shape[0], nq, A_WIDTH)

        out_a = sweep_queries(gqa_block, qa)

        qb = apply_rope(rms_norm(qb.reshape(bsz, length, 2 * B_HEADS, HEAD_DIM), b_q_norm_g[l]), ang_b)
        kb = apply_rope(rms_norm(kb.reshape(bsz, length, 2 * B_HEADS, HEAD_DIM), b_k_norm_g[l]), ang_b)
        qb = qb.reshape(bsz, length, B_HEADS, 2, HEAD_DIM)
        kb = kb.reshape(bsz, length, B_HEADS, 2, HEAD_DIM)
        vb = vb.reshape(bsz, length, B_HEADS, B_VDIM)
        lam = (jnp.exp(jnp.sum(b_lambda_q1[l].astype(jnp.float32) * b_lambda_k1[l].astype(jnp.float32)))
               - jnp.exp(jnp.sum(b_lambda_q2[l].astype(jnp.float32) * b_lambda_k2[l].astype(jnp.float32)))
               + lam_init)
        subln_g = b_subln_g[l]

        def diff_block(q):
            nq = q.shape[1]
            sc = jnp.einsum('bqhjd,blhjd->bhjql', q, kb).astype(jnp.float32) * scale
            p = jax.nn.softmax(sc, axis=-1)
            w = (p[:, :, 0] - lam * p[:, :, 1]).astype(vb.dtype)
            o = jnp.einsum('bhql,blhe->bqhe', w, vb)
            o = rms_norm(o, subln_g) * (1.0 - lam_init)
            return o.reshape(q.shape[0], nq, B_WIDTH)

        out_b = sweep_queries(diff_block, qb)

        mixed = jnp.concatenate([out_a, out_b], axis=-1)
        x = x + jnp.einsum('ble,ed->bld', mixed, w_out[l])

        h = rms_norm(x, ffn_norm_g[l])
        g = jnp.einsum('bld,df->blf', h, w_gate[l])
        u = jnp.einsum('bld,df->blf', h, w_up[l])
        x = x + jnp.einsum('blf,fd->bld', jax.nn.silu(g) * u, w_down[l])

    return x[:, N_META:]


GMLP_WIDTH = 512
GMLP_GROUPS = 4
GMLP_GROUP_DIM = GMLP_WIDTH // GMLP_GROUPS
CHUNK = 128

ATTN_PATTERNS = ((128, 1), (512, 4), (2048, 16))
N_ATTN_GROUPS = len(ATTN_PATTERNS)
HEADS_PER_GROUP = 4
HEAD_DIM_2 = 128
ATTN_GROUP_WIDTH = HEADS_PER_GROUP * HEAD_DIM_2
ATTN_WIDTH = N_ATTN_GROUPS * ATTN_GROUP_WIDTH
ROPE_DIM = HEAD_DIM_2 // 4
ROPE_THETA_2 = 500000.0

N_BRANCHES = 2
D_FF_2 = 4 * D_MODEL
D_IN = 2 * GMLP_WIDTH + 3 * ATTN_WIDTH + N_BRANCHES * D_MODEL
NORM_EPS = 1e-6
MASK_VALUE = -1e30


def rms_norm_2(x, gain):
    xf = x.astype(jnp.float32)
    y = xf * lax.rsqrt(jnp.mean(xf * xf, axis=-1, keepdims=True) + NORM_EPS)
    return (y * gain.astype(jnp.float32)).astype(x.dtype)

def layer_norm(x, gain, bias):
    xf = x.astype(jnp.float32)
    mu = jnp.mean(xf, axis=-1, keepdims=True)
    var = jnp.mean(jnp.square(xf - mu), axis=-1, keepdims=True)
    y = (xf - mu) * lax.rsqrt(var + NORM_EPS)
    return (y * gain.astype(jnp.float32) + bias.astype(jnp.float32)).astype(x.dtype)

def partial_rope(t):
    S = t.shape[1]
    half = ROPE_DIM // 2
    inv_freq = ROPE_THETA_2 ** (-jnp.arange(0, ROPE_DIM, 2, dtype=jnp.float32) / ROPE_DIM)
    ang = jnp.arange(S, dtype=jnp.float32)[:, None] * inv_freq[None, :]
    cos = jnp.cos(ang)[None, :, None, :]
    sin = jnp.sin(ang)[None, :, None, :]
    tf = t.astype(jnp.float32)
    x1, x2, rest = tf[..., :half], tf[..., half:ROPE_DIM], tf[..., ROPE_DIM:]
    out = jnp.concatenate([x1 * cos - x2 * sin, x2 * cos + x1 * sin, rest], axis=-1)
    return out.astype(t.dtype)

def dilated_window_attention(q, k, v, dilation, radius):
    B, S, H, Dh = q.shape
    L = S // dilation
    nb = -(-L // radius)
    Lp = nb * radius

    def strided(t):
        return t.astype(jnp.float32).reshape(B, L, dilation, H, Dh).transpose(0, 2, 1, 3, 4)

    qs, ks, vs = strided(q), strided(k), strided(v)
    qb = jnp.pad(qs, ((0, 0), (0, 0), (0, Lp - L), (0, 0), (0, 0))).reshape(B, dilation, nb, radius, H, Dh)

    def windows(t):
        tb = jnp.pad(t, ((0, 0), (0, 0), (radius, Lp - L + radius), (0, 0), (0, 0)))
        tb = tb.reshape(B, dilation, nb + 2, radius, H, Dh)
        return jnp.concatenate([tb[:, :, :-2], tb[:, :, 1:-1], tb[:, :, 2:]], axis=3)

    kw, vw = windows(ks), windows(vs)
    blk = jnp.arange(nb)[:, None, None]
    qpos = blk * radius + jnp.arange(radius)[None, :, None]
    kpos = blk * radius - radius + jnp.arange(3 * radius)[None, None, :]
    valid = (jnp.abs(qpos - kpos) <= radius) & (kpos >= 0) & (kpos < L)

    scale = 1.0 / math.sqrt(Dh)
    s = jnp.einsum('bdnqhe,bdnkhe->bdnhqk', qb, kw) * scale
    s = jnp.where(valid[None, None, :, None], s, MASK_VALUE)
    m = jnp.max(s, axis=-1, keepdims=True)
    p = jnp.exp(s - m)
    denom = jnp.sum(p, axis=-1, keepdims=True)
    o = jnp.einsum('bdnhqk,bdnkhe->bdnhqe', p, vw) / denom
    lse = (m + jnp.log(denom))[..., 0]

    o = o.transpose(0, 1, 2, 4, 3, 5).reshape(B, dilation, Lp, H, Dh)[:, :, :L]
    o = o.transpose(0, 2, 1, 3, 4).reshape(B, S, H, Dh)
    lse = lse.transpose(0, 1, 2, 4, 3).reshape(B, dilation, Lp, H)[:, :, :L]
    lse = lse.transpose(0, 2, 1, 3).reshape(B, S, H)
    return o, lse

def gmlp_spatial_gating(z, ln_gain, ln_bias, w_spatial, b_spatial):
    B, S, _ = z.shape
    u, v = z[..., :GMLP_WIDTH], z[..., GMLP_WIDTH:]
    v = layer_norm(v, ln_gain, ln_bias)
    v = v.reshape(B, S // CHUNK, CHUNK, GMLP_GROUPS, GMLP_GROUP_DIM)
    sv = jnp.einsum('bcsge,gts->bctge', v, w_spatial) + b_spatial.T[None, None, :, :, None]
    return u * sv.reshape(B, S, GMLP_WIDTH)

def second_inputs(seed: int = 0) -> dict:
    key = jax.random.key(seed)
    ks = jax.random.split(key, 17)
    f32 = jnp.float32

    def nrm(k, shape, scale):
        return jax.random.normal(k, shape, f32) * scale

    def gain(k, shape):
        return 1.0 + 0.05 * jax.random.normal(k, shape, f32)

    return {
        "x": jax.random.normal(ks[0], (BATCH, SEQ, D_MODEL), f32),
        "norm_mix_pre": gain(ks[1], (DEPTH, D_MODEL)),
        "w_in": nrm(ks[2], (DEPTH, D_MODEL, D_IN), D_MODEL ** -0.5),
        "b_gate": nrm(ks[3], (DEPTH, N_BRANCHES * D_MODEL), 0.02),
        "ln_v_gain": gain(ks[4], (DEPTH, GMLP_WIDTH)),
        "ln_v_bias": nrm(ks[5], (DEPTH, GMLP_WIDTH), 0.02),
        "w_spatial": nrm(ks[6], (DEPTH, GMLP_GROUPS, CHUNK, CHUNK), CHUNK ** -0.5),
        "b_spatial": gain(ks[7], (DEPTH, GMLP_GROUPS, CHUNK)),
        "w_branch_a": nrm(ks[8], (DEPTH, GMLP_WIDTH, D_MODEL), GMLP_WIDTH ** -0.5),
        "w_branch_b": nrm(ks[9], (DEPTH, ATTN_GROUP_WIDTH, D_MODEL), ATTN_GROUP_WIDTH ** -0.5),
        "w_out": nrm(ks[10], (DEPTH, D_MODEL, D_MODEL), D_MODEL ** -0.5),
        "norm_mix_post": gain(ks[11], (DEPTH, D_MODEL)),
        "norm_mlp_pre": gain(ks[12], (DEPTH, D_MODEL)),
        "w_up": nrm(ks[13], (DEPTH, D_MODEL, D_FF_2), D_MODEL ** -0.5),
        "w_down": nrm(ks[14], (DEPTH, D_FF_2, D_MODEL), D_FF_2 ** -0.5),
        "norm_mlp_post": gain(ks[15], (DEPTH, D_MODEL)),
    }

def second_block(x, norm_mix_pre, w_in, b_gate, ln_v_gain, ln_v_bias, w_spatial, b_spatial,
              w_branch_a, w_branch_b, w_out, norm_mix_post, norm_mlp_pre, w_up, w_down,
              norm_mlp_post):
    B, S, D = x.shape
    split_points = list(np.cumsum([GMLP_WIDTH * 2, ATTN_WIDTH, ATTN_WIDTH, ATTN_WIDTH])) 
    h = x
    for l in range(DEPTH):
        n = rms_norm_2(h, norm_mix_pre[l])
        proj = jnp.einsum('bsd,de->bse', n, w_in[l])
        z_gmlp, q, k, v, gates = jnp.split(proj, split_points, axis=-1)

        y_a = gmlp_spatial_gating(jax.nn.gelu(z_gmlp), ln_v_gain[l], ln_v_bias[l],
                                  w_spatial[l], b_spatial[l])

        n_heads = N_ATTN_GROUPS * HEADS_PER_GROUP
        q = partial_rope(q.reshape(B, S, n_heads, HEAD_DIM_2))
        k = partial_rope(k.reshape(B, S, n_heads, HEAD_DIM_2))
        v = v.reshape(B, S, n_heads, HEAD_DIM_2)
        outs, lses = [], []
        for g, (window, dilation) in enumerate(ATTN_PATTERNS):
            sl = slice(g * HEADS_PER_GROUP, (g + 1) * HEADS_PER_GROUP)
            o_g, lse_g = dilated_window_attention(q[:, :, sl], k[:, :, sl], v[:, :, sl],
                                                  dilation, window // (2 * dilation))
            outs.append(o_g)
            lses.append(lse_g)
        o_all = jnp.stack(outs, axis=0)
        w_mix = jax.nn.softmax(jnp.stack(lses, axis=0), axis=0)
        y_b = jnp.sum(w_mix[..., None] * o_all, axis=0).reshape(B, S, ATTN_GROUP_WIDTH).astype(h.dtype)

        g_all = jax.nn.sigmoid((gates + b_gate[l]).astype(jnp.float32)).astype(h.dtype)
        g_a, g_b = g_all[..., :D_MODEL], g_all[..., D_MODEL:]
        merged = (g_a * jnp.einsum('bse,ed->bsd', y_a, w_branch_a[l])
                  + g_b * jnp.einsum('bse,ed->bsd', y_b, w_branch_b[l]))
        mix_out = jnp.einsum('bsd,de->bse', merged, w_out[l])
        h = h + rms_norm_2(mix_out, norm_mix_post[l])

        n2 = rms_norm_2(h, norm_mlp_pre[l])
        hid = jnp.square(jax.nn.relu(jnp.einsum('bsd,df->bsf', n2, w_up[l])))
        mlp_out = jnp.einsum('bsf,fd->bsd', hid, w_down[l])
        h = h + rms_norm_2(mlp_out, norm_mlp_post[l])
    return h


def setup_inputs(seed=0):
    out = dict(first_inputs(seed))
    for name, value in second_inputs(seed + 1).items():
        if name != "x":
            out[name + "_2"] = value
    return out


def reference(
    x, meta_tokens, attn_norm_g, w_in, a_q_norm_g, a_k_norm_g, b_q_norm_g, b_k_norm_g,
    b_lambda_q1, b_lambda_k1, b_lambda_q2, b_lambda_k2, b_subln_g, w_out, ffn_norm_g, w_gate,
    w_up, w_down, norm_mix_pre_2, w_in_2, b_gate_2, ln_v_gain_2, ln_v_bias_2, w_spatial_2,
    b_spatial_2, w_branch_a_2, w_branch_b_2, w_out_2, norm_mix_post_2, norm_mlp_pre_2, w_up_2,
    w_down_2, norm_mlp_post_2,
):
    x = first_block(
        x, meta_tokens, attn_norm_g, w_in, a_q_norm_g, a_k_norm_g, b_q_norm_g, b_k_norm_g,
        b_lambda_q1, b_lambda_k1, b_lambda_q2, b_lambda_k2, b_subln_g, w_out, ffn_norm_g,
        w_gate, w_up, w_down,
    )
    return second_block(
        x, norm_mix_pre_2, w_in_2, b_gate_2, ln_v_gain_2, ln_v_bias_2, w_spatial_2, b_spatial_2,
        w_branch_a_2, w_branch_b_2, w_out_2, norm_mix_post_2, norm_mlp_pre_2, w_up_2, w_down_2,
        norm_mlp_post_2,
    )


_drawn_inputs = setup_inputs


def setup_inputs(seed=0):
    import zlib

    import numpy as np

    out = dict(_drawn_inputs(seed))
    spreads = {}
    factors = {'a_q_norm_g': 6.855,
     'a_k_norm_g': 6.075,
     'b_lambda_k1': 8.0,
     'b_lambda_q2': 8.0,
     'b_gate_2': 8.0,
     'ln_v_bias_2': 6.886,
     'b_spatial_2': 2.885}
    for name, (base, spread) in spreads.items():
        noise = np.random.default_rng([zlib.crc32(name.encode()), seed]).standard_normal(out[name].shape)
        drawn = base * np.exp(spread * noise) if base else spread * noise
        out[name] = __import__('jax').numpy.asarray(drawn.astype(out[name].dtype))
    for name, factor in factors.items():
        out[name] = (out[name] * factor).astype(out[name].dtype)
    return out
```

```python
import math
from contextlib import ExitStack

import numpy as np

import concourse.bass as bass
from concourse import mybir

F32 = mybir.dt.float32
F32R = mybir.dt.float32r
ALU = mybir.AluOpType
ACT = mybir.ActivationFunctionType
AX = mybir.AxisListType.X

P = 128
D = 1024
SEQ = 256
META = 16
TILES = SEQ // P
KC = D // P
KEYS = SEQ + META
EPS = 1e-6
WIDE = 512

HD = 64
A_HEADS, A_KV = 8, 2
B_HEADS, B_V = 4, 128
LAM_INIT = 0.8 - 0.6 * math.exp(-0.3 * 0)
D_FF = -(-8 * D // (3 * 256)) * 256

GMLP = 512
GROUPS = 4
PATTERNS = ((128, 1), (512, 4), (2048, 16))
NG = len(PATTERNS)
HD2 = 128
HEADS2 = 4
ROPE2 = HD2 // 4
D_FF2 = 4 * D
MASKED = -1e30

SLOTS = 8
RAW_SLOTS = 4
SLOT = 1024


def rope_tables():
    f = np.float32
    half = HD // 2
    inv_a = (f(10000.0) ** (-np.arange(0, half, 2, dtype=f) / f(half))).astype(f)
    t = np.arange(SEQ)
    ang_a = np.zeros((KEYS, half), f)
    ang_a[:SEQ] = np.concatenate([(t // 64).astype(f)[:, None] * inv_a, (t % 64).astype(f)[:, None] * inv_a], 1)
    inv_b = (f(10000.0) ** (-np.arange(0, HD, 2, dtype=f) / f(HD))).astype(f)
    pos = np.concatenate([META + t, np.arange(META)]).astype(f)
    ang_b = pos[:, None] * inv_b
    one = np.zeros((KEYS, 4, HD), f)
    for n, ang in ((0, ang_a), (2, ang_b)):
        one[:, n, :] = np.repeat(np.cos(ang), 2, axis=1)
        one[:, n + 1, 0::2] = -np.sin(ang)
        one[:, n + 1, 1::2] = np.sin(ang)
    inv_2 = (f(500000.0) ** (-np.arange(0, ROPE2, 2, dtype=f) / f(ROPE2))).astype(f)
    ang_2 = t.astype(f)[:, None] * inv_2
    two = np.zeros((SEQ, 2, ROPE2), f)
    two[:, 0, :] = np.concatenate([np.cos(ang_2), np.cos(ang_2)], 1)
    two[:, 1, :] = np.concatenate([-np.sin(ang_2), np.sin(ang_2)], 1)
    return one, two


def masks():
    q, k = np.arange(SEQ)[:, None], np.arange(SEQ)[None, :]
    out = np.full((SEQ, NG, SEQ), MASKED, np.float32)
    for g, (window, dilation) in enumerate(PATTERNS):
        seen = ((q - k) % dilation == 0) & (np.abs(q // dilation - k // dilation) <= window // (2 * dilation))
        out[:, g, :][seen] = 0.0
    return np.stack([out[0:P, 0], out[P:SEQ, 0], out[0:P, 1], out[0:P, 2]], axis=1)


class Mark:

    def __init__(self, line, n):
        self.line, self.n = line, n


class Line:

    every = []
    rounds = None
    floor = {}

    def __init__(self, nc, ctx, name):
        self.sem = ctx.enter_context(nc.semaphore(name))
        self.name, self.n, self.stride = name, 0, 0
        Line.every.append(self)

    def mark(self, ins, by=1):
        ins.then_inc(self.sem, by)
        self.n += by
        return Mark(self, self.n)


def wait(eng, *marks):
    latest = {}
    for m in marks:
        latest[m.line] = max(latest.get(m.line, 0), m.n)
    for line, n in latest.items():
        if Line.rounds is None:
            eng.wait_ge(line.sem, n)
        else:
            assert n > Line.floor[line], f"{line.name}: a mark from before the round ahead of the loop"
            eng.wait_ge(line.sem, Line.rounds * line.stride + n)


def run_steps(nc, step, n_steps, peeled_last=1):
    step(0, 0)
    before = {line: line.n for line in Line.every}
    step(1, 1)
    for line in Line.every:
        line.stride = line.n - before[line]
    last = n_steps - peeled_last
    start = {line: line.n for line in Line.every}
    for line in Line.every:
        line.loop_start = line.n
    with nc.Fori(0, last - 2) as i:
        Line.rounds, Line.floor = i, before
        step(i + 2, 2)
        Line.rounds = None
    more = last - 3
    for line in Line.every:
        assert line.n - start[line] == line.stride, (line.name, line.n - start[line], line.stride)
        line.n += line.stride * more
    return more


class Bank:

    def __init__(self, nc, ctx, name):
        self.t = ctx.enter_context(nc.psum_tensor(name, [P, WIDE], F32))
        self.free = ()


class Ring:

    def __init__(self, nc, ctx):
        self.nc = nc
        self.raw = ctx.enter_context(nc.sbuf_tensor("w_raw", [P, RAW_SLOTS, SLOT], F32))
        self.hi = ctx.enter_context(nc.sbuf_tensor("w_hi", [P, SLOTS, SLOT], F32R))
        self.lo = ctx.enter_context(nc.sbuf_tensor("w_lo", [P, SLOTS, SLOT], F32R))
        self.loaded = [Line(nc, ctx, f"w_loaded{r}") for r in range(RAW_SLOTS)]
        self.rounded = Line(nc, ctx, "w_hi_done")
        self.cut = Line(nc, ctx, "w_lo_done")
        self.used = Line(nc, ctx, "w_used")
        self.held = [False] * SLOTS
        self.raw_free = [() for _ in range(RAW_SLOTS)]
        self.ready = [None] * SLOTS
        self.free = [() for _ in range(SLOTS)]

    def fill(self, s, pieces, n=SLOT):
        nc, r = self.nc, s % RAW_SLOTS
        assert not self.held[s], "the slot's weights are still to be multiplied"
        self.held[s] = True
        raw = self.raw[:, r, :]
        wait(nc.sync, *self.raw_free[r])
        for view, src in pieces:
            full = self.loaded[r].mark(nc.sync.dma_start(view(raw), src), 16)
        wait(nc.scalar, full, *self.free[s])
        rounded = self.rounded.mark(nc.scalar.activation(self.hi[:, s, 0:n], raw[:, 0:n], ACT.Copy))
        wait(nc.vector, rounded)
        self.ready[s] = self.cut.mark(nc.vector.tensor_tensor(self.lo[:, s, 0:n], raw[:, 0:n], self.hi[:, s, 0:n],
                                                              ALU.subtract))
        self.raw_free[r] = (self.ready[s],)

    def done(self, s, ins):
        self.held[s] = False
        self.free[s] = (self.used.mark(ins),)
        return self.free[s][0]


class Slab:

    def __init__(self, ring, src, first, chunks, cols):
        self.ring, self.src, self.first, self.chunks, self.cols = ring, src, first, chunks, cols
        self.per = SLOT // max(cols, WIDE)
        self.n_slots = chunks // self.per

    def view(self, slot):
        return slot[:, 0:self.per * self.cols].rearrange("p (c n) -> p c n", c=self.per)

    def prepare(self):
        for j in range(self.n_slots):
            rows = self.src[j * self.per * P:(j + 1) * self.per * P, :].rearrange("(c p) n -> p c n", p=P)
            self.ring.fill(self.first + j, [(self.view, rows)], self.per * self.cols)

    def multiply(self, x_hi, x_lo, outs, x_ready=None, meta=None):
        ring, pe = self.ring, self.ring.nc.tensor
        width = min(self.cols, WIDE)
        for t in outs:
            for b in t:
                wait(pe, *b.free)
        if meta:
            wait(pe, *meta[1].free)
        for j in range(self.n_slots):
            s = self.first + j
            wait(pe, ring.ready[s])
            w_hi, w_lo = self.view(ring.hi[:, s, :]), self.view(ring.lo[:, s, :])
            for c in range(self.per):
                kc = j * self.per + c
                if x_ready:
                    wait(pe, x_ready[kc])
                first, last = kc == 0, kc == self.chunks - 1
                mm = three_passes(pe, x_hi, x_lo, w_hi[:, c, :], w_lo[:, c, :], kc, outs, width, first, last)
                if meta:
                    for n, w in enumerate((w_hi, w_lo)):
                        mm = pe.matmul(meta[1].t[:, 0:width], meta[0][:, kc, :], w[:, c, 0:width],
                                       start=first and n == 0, stop=last and n == 1)
            done = ring.done(s, mm)
        return done


def three_passes(pe, x_hi, x_lo, w_hi, w_lo, kc, outs, width, first, last):
    for t in range(TILES):
        for n, (x, w) in enumerate(((x_hi, w_hi), (x_hi, w_lo), (x_lo, w_hi))):
            for h, b in enumerate(outs[t]):
                mm = pe.matmul(b.t[:, 0:width], x[:, kc, t * P:(t + 1) * P], w[:, h * width:(h + 1) * width],
                               start=first and n == 0, stop=last and n == 2)
    return mm


def program(nc, a, out):
    with ExitStack() as ctx:
        Line.every = []
        build(nc, ctx, a, out)


def build(nc, ctx, a, out):
    pe, act, dve, pool, sp = nc.tensor, nc.scalar, nc.vector, nc.gpsimd, nc.sync

    def sb(name, shape, dt=F32, c=ctx):
        return c.enter_context(nc.sbuf_tensor(name, shape, dt))

    PE, AC, DV, PO = (Line(nc, ctx, n) for n in ("tensor_done", "scalar_done", "vector_done", "pool_done"))
    bank = [Bank(nc, ctx, f"bank{n}") for n in range(8)]
    MM = [bank[0:2], bank[2:4]]
    ring = Ring(nc, ctx)

    def per_tile(pair):
        return [[pair[0]], [pair[1]]]

    xload = Line(nc, ctx, "x_loaded")
    meta_load = Line(nc, ctx, "meta_and_gains_loaded")
    small = Line(nc, ctx, "small_loaded")
    post_load = [Line(nc, ctx, f"post_gain{n}_loaded") for n in range(2)]
    consts = Line(nc, ctx, "block2_loaded")
    x = sb("x", [P, TILES, D])
    tmp = sb("tmp", [P, TILES, D])
    ident = sb("ident", [P, P])
    gains = sb("gains", [P, 4, KC])
    stat = sb("stat", [P, 32])
    half_neg = sb("minus_half", [P, 8])
    h_hi = sb("h_hi", [P, KC, SEQ], F32R)
    h_lo = sb("h_lo", [P, KC, SEQ], F32R)

    one = ctx.enter_context(ExitStack())
    xm = sb("xm", [META, D], c=one)
    x_in = xload.mark(sp.dma_start(x[:], a["x"][0].rearrange("(t p) d -> p t d", p=P)), 16)
    meta_load.mark(act.dma_start(xm[:], a["meta_tokens"]), 16)
    meta_load.mark(act.dma_start(ident[:], a["ident"]), 16)
    for n, name in enumerate(("attn_norm_g", "ffn_norm_g", "norm_mix_pre_2", "norm_mlp_pre_2")):
        x_all = meta_load.mark(act.dma_start(gains[:, n, :], a[name][0].rearrange("(c p) -> p c", p=P),
                                         allow_slow_non_contiguous=True), 16)

    cuts = (("qa", A_HEADS * HD), ("kva", 2 * A_KV * HD), ("qb", 2 * B_HEADS * HD), ("kb", 2 * B_HEADS * HD),
            ("vb", B_HEADS * B_V))
    spans, o = {}, 0
    for name, n in cuts:
        spans[name] = (o, o + n)
        o += n
    slabs = {}
    for n, name in enumerate(("qb", "kb", "vb", "kva", "qa")):
        c0, c1 = spans[name]
        slabs[name] = Slab(ring, a["w_in"][0][:, c0:c1], 4 * (n % 2), KC, c1 - c0)
    for h in range(2):
        slabs[f"out{h}"] = Slab(ring, a["w_out"][0][:, h * WIDE:(h + 1) * WIDE], 4 * ((h + 1) % 2), KC, WIDE)

    rope1 = sb("rope1", [P, TILES, 4, HD], c=one)
    rope1m = sb("rope1m", [META, 4, HD], c=one)
    hg = sb("head_gains", [P, 4, HD], c=one)
    lamv = sb("lam_vectors", [P, 4, HD], c=one)
    subln = sb("subln", [P, 1], c=one)
    pool.dma_start(rope1[:], a["rope1"][0:SEQ].rearrange("(t p) k d -> p t k d", p=P)).then_inc(small.sem, 16)
    pool.dma_start(rope1m[:], a["rope1"][SEQ:KEYS]).then_inc(small.sem, 16)
    for n, name in enumerate(("a_q_norm_g", "a_k_norm_g", "b_q_norm_g", "b_k_norm_g")):
        pool.dma_start(hg[:, n, :], a[name][0:1, :].broadcast_to([P, HD])).then_inc(small.sem, 16)
    for n, name in enumerate(("b_lambda_q1", "b_lambda_k1", "b_lambda_q2", "b_lambda_k2")):
        pool.dma_start(lamv[:, n, :], a[name][0:1, :].broadcast_to([P, HD])).then_inc(small.sem, 16)
    small.n += 10 * 16
    small_in = small.mark(pool.dma_start(subln[:], a["b_subln_g"][0].rearrange("(p o) -> p o", o=1),
                                         allow_slow_non_contiguous=True), 16)

    half_ok = PO.mark(pool.memset(half_neg[:], -0.5))

    def inverse_root(v, scale, bias):
        rows, n = v.shape[0], v.shape[1]
        t = DV.mark(dve.tensor_scalar(v, v, scale, bias, ALU.mult, ALU.add))
        wait(pool, t, half_ok)
        return PO.mark(pool.tensor_tensor(v, v, half_neg[0:rows, 0:n], ALU.pow))

    def rms_scale(src, dst, ready, rows, k):
        ss = stat[0:rows, k:k + 1]
        wait(act, *ready)
        t = AC.mark(act.activation(dst, src, ACT.Square, accum_out=ss))
        wait(dve, t)
        t = inverse_root(ss, 1.0 / D, EPS)
        wait(dve, t)
        return DV.mark(dve.tensor_scalar(dst, src, ss, None, ALU.mult))

    def turn_and_cut(src, chunks, gain, ready, banks, out_hi=h_hi, out_lo=h_lo, free=(), at=0):
        marks = []
        wait(pe, *ready)
        wait(act, *free)
        for n, c0 in enumerate(range(0, chunks, 2)):
            b = banks[n % len(banks)]
            wait(pe, *b.free)
            for c in range(2):
                for t in range(TILES):
                    tr = pe.transpose(b.t[:, c * SEQ + t * P:c * SEQ + (t + 1) * P],
                                      src[:, t, (c0 + c) * P:(c0 + c + 1) * P], ident[:])
            wait(act, PE.mark(tr))
            if gain is None:
                d = slice(at + c0, at + c0 + 2)
                pair = b.t[:].rearrange("p (c n) -> p c n", c=2)
                wait(dve, AC.mark(act.activation(out_hi[:, d, :], pair, ACT.Copy)))
                t_lo = DV.mark(dve.tensor_tensor(out_lo[:, d, :], pair, out_hi[:, d, :], ALU.subtract))
                marks += [t_lo, t_lo]
            else:
                for c in range(2):
                    d = at + c0 + c
                    rounded = AC.mark(act.activation(out_hi[:, d, :], b.t[:, c * SEQ:(c + 1) * SEQ], ACT.Copy,
                                                     scale=gain(c0 + c)))
                wait(dve, rounded)
                for c in range(2):
                    d = at + c0 + c
                    t_lo = DV.mark(dve.scalar_tensor_tensor(out_lo[:, d, :], b.t[:, c * SEQ:(c + 1) * SEQ],
                                                            gain(c0 + c), out_hi[:, d, :], ALU.mult, ALU.subtract))
                    marks.append(t_lo)
            b.free = (t_lo,)
        return marks

    meta_stack = sb("meta_stack", [P, KC, P], F32R, c=one)
    meta_t = sb("meta_t", [P, KC, META], c=one)
    t_zero = PO.mark(pool.memset(meta_stack[:].bitcast(F32), 0.0))
    for t in range(TILES):
        normed = rms_scale(x[:, t, :], tmp[:, t, :], (x_in,), P, t)
    xm_sq = sb("xm_sq", [META, D], c=one)
    ss = stat[0:META, 2:3]
    wait(act, x_all)
    t = AC.mark(act.activation(xm_sq[:], xm[:], ACT.Square, accum_out=ss))
    wait(dve, t)
    t = inverse_root(ss, 1.0 / D, EPS)
    wait(dve, t)
    normed_m = DV.mark(dve.tensor_scalar(xm[:], xm[:], ss, None, ALU.mult))
    wait(pe, x_all)
    h1 = turn_and_cut(tmp, KC, lambda c: gains[:, 0, c:c + 1], (normed,), bank[4:7])
    wait(pe, normed_m)
    for c in range(KC):
        tr = pe.transpose(bank[7].t[:, c * META:(c + 1) * META], xm[:, c * P:(c + 1) * P], ident[0:META, 0:META])
    wait(dve, PE.mark(tr))
    t = DV.mark(dve.tensor_tensor(meta_t[:], bank[7].t[:, 0:KC * META].rearrange("p (c n) -> p c n", c=KC),
                                  gains[:, 0, :].unsqueeze(2).broadcast_to([P, KC, META]), ALU.mult))
    bank[7].free = (t,)
    wait(act, t, t_zero)
    wait(dve, t_zero)
    wait(dve, AC.mark(act.activation(meta_stack[:, :, 0:META], meta_t[:], ACT.Copy)))
    meta_ready = DV.mark(dve.tensor_tensor(meta_stack[:, :, 32:32 + META], meta_t[:], meta_stack[:, :, 0:META],
                                           ALU.subtract))
    slabs["qb"].prepare()

    lamp = sb("lam_products", [P, 2, HD], c=one)
    lam = sb("lam", [P, 4], c=one)
    lv = lamv[:].rearrange("p (j s) d -> p j s d", s=2)
    wait(dve, small_in)
    t = DV.mark(dve.tensor_tensor(lamp[:], lv[:, :, 0, :], lv[:, :, 1, :], ALU.mult))
    wait(dve, t)
    t = DV.mark(dve.tensor_reduce(lam[:, 0:2], lamp[:], AX, ALU.add))
    wait(act, t)
    t = AC.mark(act.activation(lam[:, 2:4], lam[:, 0:2], ACT.Exp))
    wait(dve, t)
    t = DV.mark(dve.tensor_tensor(lam[:, 0:1], lam[:, 3:4], lam[:, 2:3], ALU.subtract))
    wait(dve, t)
    lam_ok = DV.mark(dve.tensor_scalar(lam[:, 1:2], lam[:, 0:1], -LAM_INIT, None, ALU.add))
    subln_ok = DV.mark(dve.tensor_scalar(subln[:], subln[:], 1.0 - LAM_INIT, None, ALU.mult))

    rg = sb("rope_gain", [P, TILES, 4, 2, HD], c=one)
    rgm = sb("rope_gain_meta", [META, 4, 2, HD], c=one)
    wait(pool, small_in)
    for kind in range(4):
        base = 2 * (kind // 2)
        for dst, tab, g in [(rg[:, t, kind], rope1[:, t], hg[:, kind, :]) for t in range(TILES)] + \
                [(rgm[:, kind], rope1m[:], hg[0:META, kind, :])]:
            pool.tensor_tensor(dst[:, 0, :], tab[:, base, :], g, ALU.mult)
            for e in range(2):
                rg_done = PO.mark(pool.tensor_tensor(dst[:, 1, e::2], tab[:, base + 1, e::2], g[:, 1 - e::2],
                                                     ALU.mult))

    xn = sb("head_normed", [P, 2, WIDE], c=one)
    part = sb("rope_part", [P, 2, WIDE], c=one)
    mcopy = sb("meta_copy", [META, WIDE], c=one)
    msum = sb("meta_sum", [META, WIDE], c=one)
    xn_free = [(), ()]
    turn = [0]

    def by_head(v):
        return v.rearrange("p (h d) -> p h d", d=HD)

    def norm_and_rope(src, heads, table, is_q, ready, dsts, rows):
        u = turn[0] % 2
        turn[0] += 1
        n = heads * HD
        ss = stat[0:rows, 8 + 8 * u:8 + 8 * u + heads]
        x_t, p_t = xn[0:rows, u, 0:n], part[0:rows, u, 0:n]
        wait(act, *ready, *xn_free[u])
        t = AC.mark(act.activation(x_t, src, ACT.Square))
        wait(dve, t)
        t = DV.mark(dve.tensor_reduce(ss, by_head(x_t), AX, ALU.add))
        wait(dve, t)
        if is_q:
            t = inverse_root(ss, 1.0, HD * EPS)
        else:
            t = inverse_root(ss, 1.0 / HD, EPS)
        wait(dve, t)
        read = DV.mark(dve.tensor_tensor(by_head(x_t), by_head(src), ss.unsqueeze(2).broadcast_to([rows, heads, HD]),
                                         ALU.mult))
        wait(pool, read, rg_done, *xn_free[u])
        for e in range(2):
            swapped = PO.mark(pool.tensor_tensor(by_head(p_t)[:, :, e::2], by_head(x_t)[:, :, 1 - e::2],
                                                 table[:, 1, e::2].unsqueeze(1).broadcast_to([rows, heads, HD // 2]),
                                                 ALU.mult))
        wait(dve, read, swapped)
        t = DV.mark(dve.tensor_tensor(by_head(x_t), by_head(x_t),
                                      table[:, 0, :].unsqueeze(1).broadcast_to([rows, heads, HD]), ALU.mult))
        wait(dve, t)
        for d in dsts:
            done = DV.mark(dve.tensor_tensor(d, by_head(x_t), by_head(p_t), ALU.add))
        xn_free[u] = (done,)
        return read, done

    qn = sb("q_rows", [P, TILES, WIDE], c=one)
    kb = sb("kb", [P, TILES, WIDE], c=one)
    kbm = sb("kb_meta", [META, WIDE], c=one)
    vb = sb("vb", [P, TILES, WIDE], c=one)
    vbm = sb("vb_meta", [META, WIDE], c=one)
    kw = A_KV * HD
    ka = sb("ka", [P, TILES, 2 * kw], c=one)
    kam = sb("ka_meta", [META, 2 * kw], c=one)
    va = sb("va", [P, TILES, kw], c=one)
    vam = sb("va_meta", [META, kw], c=one)

    def add_meta(done, n, free=()):
        wait(act, done, *free)
        wait(dve, AC.mark(act.activation(mcopy[:, 0:n], bank[4].t[32:32 + META, 0:n], ACT.Copy)))
        t = DV.mark(dve.tensor_tensor(msum[:, 0:n], bank[4].t[0:META, 0:n], mcopy[:, 0:n], ALU.add))
        bank[4].free = (t,)
        return t

    def rope_tiles(pair, kind, is_q, dst, done, free=()):
        wait(dve, *free)
        for t in range(TILES):
            read, ok = norm_and_rope(pair[t].t[:], 8, rg[:, t, kind], is_q, (done,), [by_head(dst[:, t, :])], P)
            pair[t].free = (read,)
        return ok

    qT = sb("qT1", [P, 4, SEQ], c=one)
    kbT = sb("kbT", [P, 4, KEYS], c=one)
    kaT = sb("kaT", [P, 2, KEYS], c=one)

    def turn_heads(src, dst, chunks, ready, banks, free=(), metas=None):
        wait(pe, *ready)
        wait(act, *free)
        wait(dve, *free)
        marks = []
        for n, c0 in enumerate(range(0, chunks, 2)):
            b = banks[n % len(banks)]
            wait(pe, *b.free)
            for c in range(2):
                for t in range(TILES):
                    tr = pe.transpose(b.t[:, c * SEQ + t * P:c * SEQ + (t + 1) * P],
                                      src[:, t, (c0 + c) * P:(c0 + c + 1) * P], ident[:])
            pair, done = b.t[:].rearrange("p (c n) -> p c n", c=2), PE.mark(tr)
            if n % 2 == 0:
                wait(act, done)
                m = AC.mark(act.activation(dst[:, c0:c0 + 2, 0:SEQ], pair, ACT.Copy))
            else:
                wait(dve, done)
                m = DV.mark(dve.tensor_copy(dst[:, c0:c0 + 2, 0:SEQ], pair))
            b.free = (m,)
            marks.append(m)
        if metas is not None:
            b = banks[-1]
            wait(pe, *b.free)
            for c in range(chunks):
                tr = pe.transpose(b.t[:, c * META:(c + 1) * META], metas[:, c * P:(c + 1) * P], ident[0:META, 0:META])
            wait(dve, PE.mark(tr))
            m = DV.mark(dve.tensor_copy(dst[:, :, SEQ:KEYS],
                                        b.t[:, 0:chunks * META].rearrange("p (c n) -> p c n", c=chunks)))
            b.free = (m,)
            marks.append(m)
        return marks

    maps = sb("maps1", [P, TILES, 8, KEYS], c=one)
    den = sb("den1", [P, 2, TILES, 8], c=one)
    nmax = sb("nmax1", [P, 2, TILES, 8], c=one)
    rden = sb("rden1", [P, 2, TILES, 8], c=one)

    def scores(t, h, kT, k_chunk, which, b, free):
        p0 = HD * (h % 2)
        wait(pe, *b.free)
        wait(dve, PE.mark(pe.matmul(b.t[:, 0:KEYS], qT[p0:p0 + HD, h // 2, t * P:(t + 1) * P],
                                    kT[p0:p0 + HD, k_chunk, :], start=True, stop=True)))
        m = DV.mark(dve.tensor_reduce(nmax[:, which, t, h:h + 1], b.t[:, 0:KEYS], AX, ALU.max, negate=True))
        wait(act, m, *free)
        e = AC.mark(act.activation(maps[:, t, h, :], b.t[:, 0:KEYS], ACT.Exp, bias=nmax[:, which, t, h:h + 1],
                                   accum_out=den[:, which, t, h:h + 1]))
        b.free = (e,)
        return e

    pT = sb("pT", [P, 2, 2, SEQ], c=one)
    pTm = sb("pTm", [META, 2, SEQ], c=one)
    pT_free = [(), ()]

    def turn_map(h, buf, ready, b, bm):
        wait(pe, *ready, *b.free, *bm.free)
        for t in range(TILES):
            for c in range(2):
                pe.transpose(b.t[:, c * SEQ + t * P:c * SEQ + (t + 1) * P], maps[:, t, h, c * P:(c + 1) * P], ident[:])
            tr = pe.transpose(bm.t[0:META, t * P:(t + 1) * P], maps[:, t, h, SEQ:KEYS], ident[:])
        done = PE.mark(tr)
        wait(act, done, *pT_free[buf])
        wait(dve, done, *pT_free[buf])
        m1 = AC.mark(act.activation(pT[:, buf], b.t[:].rearrange("p (c n) -> p c n", c=2), ACT.Copy))
        m2 = DV.mark(dve.tensor_copy(pTm[:, buf, :], bm.t[0:META, 0:SEQ]))
        b.free, bm.free = (m1,), (m2,)
        return (m1, m2), done

    def weights_times_values(buf, ready, ob, v, vm, cols):
        n = cols.stop - cols.start
        wait(pe, *ready, *ob.free)
        for t in range(TILES):
            for c in range(2):
                pe.matmul(ob.t[:, t * n:(t + 1) * n], pT[:, buf, c, t * P:(t + 1) * P], v[:, c, cols],
                          start=(c == 0), stop=False)
            mm = pe.matmul(ob.t[:, t * n:(t + 1) * n], pTm[:, buf, t * P:(t + 1) * P], vm[:, cols],
                           start=False, stop=True)
        done = PE.mark(mm)
        pT_free[buf] = (done,)
        return done

    slabs["kb"].prepare()
    t_qb = slabs["qb"].multiply(h_hi, h_lo, per_tile(MM[0]), x_ready=h1)
    qb_ok = rope_tiles(MM[0], 2, True, qn, t_qb)
    wait(pe, meta_ready)
    slabs["vb"].prepare()
    t_kb = slabs["kb"].multiply(h_hi, h_lo, per_tile(MM[1]), meta=(meta_stack, bank[4]))
    qT_ok = turn_heads(qn, qT, 4, (qb_ok,), bank[5:7])
    kb_ok = rope_tiles(MM[1], 3, False, kb, t_kb)
    m = add_meta(t_kb, WIDE)
    wait(act, m)
    _, kbm_ok = norm_and_rope(msum[:], 8, rgm[:, 3], False, (m,), [by_head(kbm[:])], META)
    slabs["kva"].prepare()
    t_vb = slabs["vb"].multiply(h_hi, h_lo, per_tile(MM[0]), meta=(meta_stack, bank[4]))
    kbT_ok = turn_heads(kb, kbT, 4, (kb_ok, kbm_ok), bank[5:7], metas=kbm)
    wait(act, t_vb)
    wait(dve, t_vb)
    v0 = AC.mark(act.activation(vb[:, 0, :], MM[0][0].t[:], ACT.Copy))
    v1 = DV.mark(dve.tensor_copy(vb[:, 1, :], MM[0][1].t[:]))
    MM[0][0].free, MM[0][1].free = (v0,), (v1,)
    m = add_meta(t_vb, WIDE, (kbm_ok,))
    wait(dve, m)
    vb_ok = (v0, DV.mark(dve.tensor_copy(vbm[:], msum[:])))

    wait(pe, *qT_ok, *kbT_ok)
    exp_b = {}
    for n in range(8 * TILES):
        h, t = n // TILES, n % TILES
        exp_b[t, h] = scores(t, h, kbT, h // 2, 0, bank[5 + n % 3], ())
    b_scored = Mark(PE, PE.n)
    slabs["qa"].prepare()
    t_kva = slabs["kva"].multiply(h_hi, h_lo, per_tile(MM[1]), meta=(meta_stack, bank[4]))
    wait(dve, exp_b[1, 7], lam_ok)
    t = DV.mark(dve.reciprocal(rden[:, 0], den[:, 0]))
    wait(dve, t)
    rd = rden[:, 0].rearrange("p t (h j) -> p t h j", j=2)
    t = DV.mark(dve.tensor_scalar(rd[:, :, :, 1], rd[:, :, :, 1], lam[:, 1:2], None, ALU.mult))
    wait(dve, t)
    w_b = {}
    for h in range(B_HEADS):
        for t in range(TILES):
            e0, e1 = maps[:, t, 2 * h, :], maps[:, t, 2 * h + 1, :]
            u = DV.mark(dve.tensor_scalar(e1, e1, rden[:, 0, t, 2 * h + 1:2 * h + 2], None, ALU.mult))
            wait(dve, u)
            w_b[t, h] = DV.mark(dve.scalar_tensor_tensor(e0, e0, rden[:, 0, t, 2 * h:2 * h + 1], e1,
                                                         ALU.mult, ALU.add))
    for t in range(TILES):
        dup = ka[:, t, :].rearrange("p (h two d) -> p two h d", two=2, d=HD)
        wait(act, t_kva)
        va_ok = AC.mark(act.activation(va[:, t, :], MM[1][t].t[:, kw:2 * kw], ACT.Copy))
        read, ka_ok = norm_and_rope(MM[1][t].t[:, 0:kw], A_KV, rg[:, t, 1], False, (t_kva,), [dup[:, 0], dup[:, 1]], P)
        MM[1][t].free = (read, va_ok)
    m = add_meta(t_kva, 2 * kw, vb_ok)
    wait(dve, m)
    vam_ok = DV.mark(dve.tensor_copy(vam[:], msum[:, kw:2 * kw]))
    dup = kam[:].rearrange("p (h two d) -> p two h d", two=2, d=HD)
    _, kam_ok = norm_and_rope(msum[:, 0:kw], A_KV, rgm[:, 1], False, (m,), [dup[:, 0], dup[:, 1]], META)
    slabs["out0"].prepare()
    t_qa = slabs["qa"].multiply(h_hi, h_lo, per_tile(MM[0]))
    kaT_ok = turn_heads(ka, kaT, 2, (ka_ok, kam_ok), bank[5:7], metas=kam)
    qa_ok = rope_tiles(MM[0], 0, True, qn, t_qa, (qT_ok[0], qT_ok[1]))

    mixed = tmp
    b_turned, pv_b = {}, {}
    for h in range(B_HEADS):
        buf = h % 2
        ready, b_turned[h] = turn_map(2 * h, buf, (w_b[0, h], w_b[1, h]), bank[5 + buf], bank[7])
        ob = MM[1][h % 2]
        done = weights_times_values(buf, (*ready, *vb_ok), ob, vb, vbm, slice(h * B_V, (h + 1) * B_V))
        col = A_HEADS * HD + h * B_V
        wait(act, done, *([pv_b[1, h - 2]] if h > 1 else []))
        ss = stat[:, 24 + 2 * buf:26 + 2 * buf]
        for t in range(TILES):
            u = AC.mark(act.activation(mixed[:, t, col:col + B_V], ob.t[:, t * B_V:(t + 1) * B_V], ACT.Square,
                                       accum_out=ss[:, t:t + 1]))
        wait(dve, u)
        u = inverse_root(ss, 1.0 / B_V, EPS)
        wait(dve, u)
        for t in range(TILES):
            pv_b[t, h] = DV.mark(dve.tensor_scalar(mixed[:, t, col:col + B_V], ob.t[:, t * B_V:(t + 1) * B_V],
                                                   ss[:, t:t + 1], None, ALU.mult))
        ob.free = (pv_b[1, h],)

    qT_ok = turn_heads(qn, qT, 4, (qa_ok,), bank[2:4], free=(b_scored,))
    wait(pe, *qT_ok, *kaT_ok)
    exp_a = {}

    def attend_a(h):
        buf, kv = h % 2, h // (A_HEADS // A_KV)
        ready, _ = turn_map(h, buf, (exp_a[0, h], exp_a[1, h]), bank[6], bank[7])
        ob = bank[2 + buf]
        done = weights_times_values(buf, (*ready, va_ok, vam_ok), ob, va, vam, slice(kv * HD, (kv + 1) * HD))
        wait(dve, exp_a[0, h], exp_a[1, h])
        r = DV.mark(dve.reciprocal(rden[:, 1, :, h], den[:, 1, :, h]))
        wait(dve, r, done)
        for t in range(TILES):
            ok = DV.mark(dve.tensor_scalar(mixed[:, t, h * HD:(h + 1) * HD], ob.t[:, t * HD:(t + 1) * HD],
                                           rden[:, 1, t, h:h + 1], None, ALU.mult))
        ob.free = (ok,)
        return ok

    for h in range(A_HEADS + 2):
        if h < A_HEADS:
            for t in range(TILES):
                exp_a[t, h] = scores(t, h, kaT, h // 4, 1, (bank[0], bank[1], bank[4], bank[5])[(2 * h + t) % 4],
                                     (b_turned[h // 2], w_b[t, h // 2]))
        if h >= 2:
            pv_a = attend_a(h - 2)

    m_b = turn_and_cut(mixed[:, :, A_HEADS * HD:], 4, lambda c: subln[:], (pv_b[0, 3], pv_b[1, 3]), bank[4:6],
                       free=(t_qa, subln_ok), at=4)
    m_a = turn_and_cut(mixed, 4, None, (pv_a,), bank[6:8])
    slabs["out1"].prepare()
    t_o0 = slabs["out0"].multiply(h_hi, h_lo, per_tile(MM[0]), x_ready=m_a + m_b)

    def add_residual(pair, half, done):
        wait(dve, done)
        for t in range(TILES):
            cols = slice(half * WIDE, (half + 1) * WIDE)
            ok = DV.mark(dve.tensor_tensor(x[:, t, cols], x[:, t, cols], pair[t].t[:], ALU.add))
            pair[t].free = (ok,)
        return ok

    add_residual(MM[0], 0, t_o0)
    one.close()

    ffn_rows = sb("ffn_rows", [P, TILES, WIDE])
    f_hi = sb("ffn_hi", [P, 4, SEQ], F32R)
    f_lo = sb("ffn_lo", [P, 4, SEQ], F32R)
    f_line = {n: Line(nc, ctx, n) for n in ("ffn_up", "ffn_acted", "ffn_hidden", "ffn_turned", "ffn_hi_done",
                                            "ffn_lo_done")}

    def feed_forward(steps, up_pieces, down_piece, chunks, squared, x_ready, after):
        acc, up_banks = [bank[4:6], bank[6:8]], bank[0:2]
        L, n_hid = f_line, chunks * P
        state = {"rows_free": (), "cut_free": (), "cut": None}

        def fill_up(i):
            for s in range(4):
                ring.fill(s, up_pieces(i, s))

        def fill_down(i):
            for c in range(chunks):
                ring.fill(4 + c, [(lambda raw: raw, down_piece(i, c))])

        def down(first, last):
            if first:
                wait(pe, *(m for t in acc for b in t for m in b.free))
            for c in range(chunks):
                wait(pe, ring.ready[4 + c], state["cut"][c // 2])
                mm = three_passes(pe, f_hi, f_lo, ring.hi[:, 4 + c, :], ring.lo[:, 4 + c, :], c, acc, WIDE,
                                  first and c == 0, last and c == chunks - 1)
                done = ring.done(4 + c, mm)
            state["cut_free"] = (done,)
            return done

        def step(i, n, last=False):
            wait(pe, *(m for b in up_banks for m in b.free))
            for s in range(4):
                wait(pe, ring.ready[s])
                for c in range(2):
                    kc = 2 * s + c
                    if n == 0:
                        wait(pe, x_ready[kc])
                    mm = three_passes(pe, h_hi, h_lo, ring.hi[:, s, c * WIDE:(c + 1) * WIDE],
                                      ring.lo[:, s, c * WIDE:(c + 1) * WIDE], kc, per_tile(up_banks), WIDE,
                                      kc == 0, kc == KC - 1)
                up_done = ring.done(s, mm)
            if n > 0:
                fill_down(i - 1)
                down(first=(n == 1), last=False)
            if last:
                after()
            else:
                fill_up(i + 1)
            for t in range(TILES):
                b, rows = up_banks[t], ffn_rows[:, t, 0:n_hid]
                wait(act, up_done, *state["rows_free"])
                if squared:
                    acted = L["ffn_acted"].mark(act.activation(rows, b.t[:], ACT.Relu))
                    b.free = (acted,)
                    wait(pool, acted)
                    hidden = L["ffn_hidden"].mark(pool.tensor_tensor(rows, rows, rows, ALU.mult))
                else:
                    acted = L["ffn_acted"].mark(act.activation(rows, b.t[:, 0:n_hid], ACT.Silu))
                    wait(dve, acted)
                    hidden = L["ffn_hidden"].mark(dve.tensor_tensor(rows, rows, b.t[:, n_hid:2 * n_hid], ALU.mult))
                    b.free = (hidden,)
            state["cut"] = []
            wait(pe, hidden)
            for c0 in range(0, chunks, 2):
                b = bank[2 + c0 // 2]
                wait(pe, *b.free)
                for c in range(2):
                    for t in range(TILES):
                        tr = pe.transpose(b.t[:, c * SEQ + t * P:c * SEQ + (t + 1) * P],
                                          ffn_rows[:, t, (c0 + c) * P:(c0 + c + 1) * P], ident[:])
                turned = L["ffn_turned"].mark(tr)
                pair = b.t[:].rearrange("p (c n) -> p c n", c=2)
                wait(act, turned, *state["cut_free"])
                rounded = L["ffn_hi_done"].mark(act.activation(f_hi[:, c0:c0 + 2, :], pair, ACT.Copy))
                wait(dve, rounded)
                cut = L["ffn_lo_done"].mark(dve.tensor_tensor(f_lo[:, c0:c0 + 2, :], pair, f_hi[:, c0:c0 + 2, :],
                                                              ALU.subtract))
                b.free = (cut,)
                state["cut"].append(cut)
            state["rows_free"] = (turned,)

        more = run_steps(nc, step, steps)
        held = [m for f in (*ring.free, *ring.raw_free, state["rows_free"], state["cut_free"]) for m in f]
        held += [m for b in bank[0:4] for m in b.free] + list(ring.ready) + state["cut"]
        for m in {id(m): m for m in held if m is not None}.values():
            if m.n > m.line.loop_start:
                m.n += m.line.stride * more
        step(steps - 1, steps - 1, last=True)
        fill_down(steps - 1)
        return down(first=False, last=True)

    def up_slab1(i, s):
        n = D_FF // 11
        out = []
        for w, name in enumerate(("w_gate", "w_up")):
            src = a[name][0][2 * s * P:(2 * s + 2) * P, bass.ds(i * n, n)].rearrange("(c p) n -> p c n", p=P)
            out.append((lambda raw, w=w: raw.rearrange("p (c w n) -> p c w n", c=2, w=2)[:, :, w, :], src))
        return out

    def first_up(pieces):
        for s in range(4):
            ring.fill(s, pieces(0, s))

    t_o1 = slabs["out1"].multiply(h_hi, h_lo, per_tile(MM[1]))
    first_up(up_slab1)
    x_ok = add_residual(MM[1], 1, t_o1)

    bg = [sb(f"b_gate{h}", [P, D]) for h in range(2)]
    two = ctx.enter_context(ExitStack())
    ln = sb("ln_v", [P, 2, GMLP], c=two)
    mask = sb("mask", [P, 4, SEQ], c=two)
    rope2 = sb("rope2", [P, TILES, 2, ROPE2], c=two)
    pT2 = sb("pT2", [P, 2, NG * 2, P], c=two)
    wsp = pT2[:, 0, 0:GROUPS, :]
    wspT = sb("w_spatial_T", [P, GROUPS, P], c=two)
    bsp = sb("b_spatial", [P, GROUPS], c=two)
    wait(pool, t_o1)
    for dst, src in [(bg[h][:], a["b_gate_2"][0:1, h * D:(h + 1) * D].broadcast_to([P, D])) for h in range(2)] + [
            (ln[:, 0, :], a["ln_v_gain_2"][0:1, :].broadcast_to([P, GMLP])),
            (ln[:, 1, :], a["ln_v_bias_2"][0:1, :].broadcast_to([P, GMLP])),
            (mask[:], a["mask"]), (rope2[:], a["rope2"].rearrange("(t p) k d -> p t k d", p=P)),
            (wsp, a["w_spatial_2"][0].rearrange("g t s -> t g s")),
            (bsp[:], a["b_spatial_2"][0].rearrange("g t -> t g"))]:
        two_in = consts.mark(pool.dma_start(dst, src, allow_slow_non_contiguous=True), 16)

    n1 = [rms_scale(x[:, t, :], tmp[:, t, :], (x_ok,), P, t) for t in range(TILES)]
    h2 = turn_and_cut(tmp, KC, lambda c: gains[:, 1, c:c + 1], n1, bank[4:8], free=(t_o1,))

    win2 = a["w_in_2"][0]
    base = {"z": 0, "q": 2 * GMLP}
    base["k"] = base["q"] + NG * WIDE
    base["v"] = base["k"] + NG * WIDE
    base["g"] = base["v"] + NG * WIDE
    order2 = [("z", 1), ("z", 0)] + [(c, g) for g in range(NG) for c in "qkv"] + [("g", 0), ("g", 1), ("a", 0),
                                                                                  ("g", 2), ("g", 3), ("b", 0), ("o", 0), ("o", 1)]
    plan = []
    for n, (kind, j) in enumerate(order2):
        if kind in "ab":
            src, chunks, cols = a["w_branch_a_2" if kind == "a" else "w_branch_b_2"][0], 4, D
        elif kind == "o":
            src, chunks, cols = a["w_out_2"][0][:, j * WIDE:(j + 1) * WIDE], KC, WIDE
        else:
            c0 = base[kind] + j * WIDE
            src, chunks, cols = win2[:, c0:c0 + WIDE], KC, WIDE
        plan.append(Slab(ring, src, 4 * (n % 2), chunks, cols))
    at = {key: n for n, key in enumerate(order2)}

    ff1 = feed_forward(11, up_slab1, lambda i, c: a["w_down"][0][bass.ds((2 * i + c) * P, P), :], 2, False, h2,
                       plan[0].prepare)

    def add_acc(done):
        wait(dve, done)
        for t in range(TILES):
            for half in range(2):
                cols = slice(half * WIDE, (half + 1) * WIDE)
                b = bank[4 + 2 * t + half]
                ok = DV.mark(dve.tensor_tensor(x[:, t, cols], x[:, t, cols], b.t[:], ALU.add))
                b.free = (ok,)
        return ok

    x_ok = add_acc(ff1)

    n2 = [rms_scale(x[:, t, :], tmp[:, t, :], (x_ok,), P, t) for t in range(TILES)]
    h3 = turn_and_cut(tmp, KC, lambda c: gains[:, 2, c:c + 1], n2, bank[4:8], free=(ff1,))

    qk = {c: sb(f"{c}2_rows", [P, TILES, WIDE], c=two) for c in "qk"}
    u_rows = sb("u_rows", [P, TILES, GMLP], c=two)
    q2T = {c: sb(f"{c}2T", [P, HEADS2, SEQ], c=two) for c in "qk"}
    v2 = sb("v2", [P, NG, TILES, WIDE], c=two)
    sc = sb("scores2", [P, TILES, HEADS2, NG * SEQ], c=two)
    rot = sb("rope2_part", [P, 2, HEADS2, ROPE2], c=two)
    bn = sb("bn", [P, TILES, 8], c=two)
    smax = sb("smax2", [P, 3, TILES, HEADS2], c=two)

    def product(key, outs, ready=None):
        n = at[key]
        if n + 1 < len(plan):
            plan[n + 1].prepare()
        x_hi, x_lo = (f_hi, f_lo) if key[0] in "ab" else (h_hi, h_lo)
        return plan[n].multiply(x_hi, x_lo, outs, x_ready=ready)

    pair_of = lambda key: MM[at[key] % 2]

    key = ("z", 1)
    done = product(key, per_tile(pair_of(key)), ready=h3)
    v_rows = ffn_rows
    wait(act, done)
    v_ok = []
    for t in range(TILES):
        b = pair_of(key)[t]
        g = AC.mark(act.activation(v_rows[:, t, :], b.t[:], ACT.Gelu_apprx_tanh))
        b.free = (g,)
        wait(dve, g)
        s = DV.mark(dve.bn_stats(bn[:, t, 0:6], v_rows[:, t, :]))
        wait(dve, s)
        s = DV.mark(dve.bn_aggr(bn[:, t, 6:8], bn[:, t, 0:6]))
        wait(dve, s)
        s = inverse_root(bn[:, t, 7:8], 1.0, EPS)
        wait(dve, s)
        s = DV.mark(dve.tensor_scalar(v_rows[:, t, :], v_rows[:, t, :], bn[:, t, 6:7], bn[:, t, 7:8],
                                      ALU.subtract, ALU.mult))
        wait(pool, s, two_in)
        s = PO.mark(pool.tensor_tensor(v_rows[:, t, :], v_rows[:, t, :], ln[:, 0, :], ALU.mult))
        wait(pool, s)
        v_ok.append(PO.mark(pool.tensor_tensor(v_rows[:, t, :], v_rows[:, t, :], ln[:, 1, :], ALU.add)))
    wait(pe, two_in, *bank[4].free)
    for g in range(GROUPS):
        tr = pe.transpose(bank[4].t[:, g * P:(g + 1) * P], wsp[:, g, :], ident[:])
    wait(act, PE.mark(tr))
    wspT_ok = AC.mark(act.activation(wspT[:], bank[4].t[:].rearrange("p (g n) -> p g n", g=GROUPS), ACT.Copy))
    bank[4].free = (wspT_ok,)

    key = ("z", 0)
    done = product(key, per_tile(pair_of(key)))
    wait(act, done)
    for t in range(TILES):
        b = pair_of(key)[t]
        u_ok = AC.mark(act.activation(u_rows[:, t, :], b.t[:], ACT.Gelu_apprx_tanh))
        b.free = (u_ok,)

    def spatial():
        wait(pe, *v_ok, wspT_ok)
        wait(dve, u_ok, two_in)
        for t in range(TILES):
            b = bank[4 + t]
            wait(pe, *b.free)
            for g in range(GROUPS):
                mm = pe.matmul(b.t[:, g * P:(g + 1) * P], wspT[:, g, :], v_rows[:, t, g * P:(g + 1) * P],
                               start=True, stop=True)
            wait(dve, PE.mark(mm))
            for g in range(GROUPS):
                cols = slice(g * P, (g + 1) * P)
                ok = DV.mark(dve.scalar_tensor_tensor(u_rows[:, t, cols], b.t[:, cols], bsp[:, g:g + 1],
                                                      u_rows[:, t, cols], ALU.add, ALU.mult))
            b.free = (ok,)
        return ok

    qk_free = {"q": (), "k": ()}
    T_free = ()
    s_ok = {}

    def take_rows(kind, g, done):
        pair, rows = pair_of((kind, g)), qk[kind]
        for t in range(TILES):
            wait(act, done, *qk_free[kind])
            c = AC.mark(act.activation(rows[:, t, :], pair[t].t[:], ACT.Copy))
            pair[t].free = (c,)
            wait(dve, c, two_in)
            r = rows[:, t, :].rearrange("p (h d) -> p h d", d=HD2)
            half = ROPE2 // 2
            tab = lambda k, lo_, hi_: rope2[:, t, k, lo_:hi_].unsqueeze(1).broadcast_to([P, HEADS2, hi_ - lo_])
            dve.tensor_tensor(rot[:, 0], r[:, :, 0:ROPE2], tab(0, 0, ROPE2), ALU.mult)
            dve.tensor_tensor(rot[:, 1, :, 0:half], r[:, :, half:ROPE2], tab(1, 0, half), ALU.mult)
            s = DV.mark(dve.tensor_tensor(rot[:, 1, :, half:ROPE2], r[:, :, 0:half], tab(1, half, ROPE2), ALU.mult))
            wait(dve, s)
            ok = DV.mark(dve.tensor_tensor(r[:, :, 0:ROPE2], rot[:, 0], rot[:, 1], ALU.add))
            wait(dve, ok)
        return ok

    def turn2(kind, ok, banks):
        m = turn_heads(qk[kind], q2T[kind], HEADS2, (ok,), banks, free=T_free)
        qk_free[kind] = (Mark(PE, PE.n),)
        return m

    for g in range(NG):
        key = ("q", g)
        done = product(key, per_tile(pair_of(key)))
        q_ok = take_rows("q", g, done)
        if g == 0:
            ya_ok = spatial()
        key = ("k", g)
        done = product(key, per_tile(pair_of(key)))
        qT_ok = turn2("q", q_ok, bank[6:8])
        k_ok = take_rows("k", g, done)
        if g == 0:
            ya_cut = turn_and_cut(u_rows, 4, None, (ya_ok,), bank[4:6], out_hi=f_hi, out_lo=f_lo)
        key = ("v", g)
        done = product(key, per_tile(pair_of(key)))
        pair = pair_of(key)
        wait(act, done)
        wait(dve, done)
        v0 = AC.mark(act.activation(v2[:, g, 0, :], pair[0].t[:], ACT.Copy))
        v1 = DV.mark(dve.tensor_copy(v2[:, g, 1, :], pair[1].t[:]))
        pair[0].free, pair[1].free = (v0,), (v1,)
        kT_ok = turn2("k", k_ok, bank[6:8])
        wait(pe, *qT_ok, *kT_ok)
        for h in range(HEADS2):
            b = bank[4 + h % 2]
            wait(pe, *b.free)
            for t in range(TILES):
                mm = pe.matmul(b.t[:, t * SEQ:(t + 1) * SEQ], q2T["q"][:, h, t * P:(t + 1) * P], q2T["k"][:, h, :],
                               start=True, stop=True)
            T_free = (PE.mark(mm),)
            wait(dve, T_free[0])
            for t in range(TILES):
                m = mask[:, t if g == 0 else 1 + g, :]
                s_ok[g, h] = DV.mark(dve.scalar_tensor_tensor(sc[:, t, h, g * SEQ:(g + 1) * SEQ],
                                                              b.t[:, t * SEQ:(t + 1) * SEQ], HD2 ** -0.5, m,
                                                              ALU.mult, ALU.add))
            b.free = (s_ok[g, h],)
    v_all = (v0, v1)

    e2 = {}
    for t in range(TILES):
        wait(dve, *[s_ok[NG - 1, h] for h in range(HEADS2)])
        m = DV.mark(dve.tensor_reduce(smax[:, 0, t, :], sc[:, t], AX, ALU.max, negate=True))
        wait(act, m)
        for h in range(HEADS2):
            e2[t, h] = AC.mark(act.activation(sc[:, t, h, :], sc[:, t, h, :], ACT.Exp, bias=smax[:, 0, t, h:h + 1],
                                              accum_out=smax[:, 1, t, h:h + 1]))
        wait(dve, e2[t, HEADS2 - 1])
        rs_ok = DV.mark(dve.reciprocal(smax[:, 2, t, :], smax[:, 1, t, :]))

    yb = qk["q"]
    pT2_free = [(), ()]
    yb_ok = None

    def attend2(t, h, buf):
        wait(pe, e2[t, h])
        cps = []
        for n in range(2):
            b = bank[4 + n]
            wait(pe, *b.free)
            for c in range(3):
                kc = 3 * n + c
                tr = pe.transpose(b.t[:, c * P:(c + 1) * P], sc[:, t, h, kc * P:(kc + 1) * P], ident[:])
            done = PE.mark(tr)
            dst, src = pT2[:, buf, 3 * n:3 * n + 3, :], b.t[:, 0:3 * P].rearrange("p (c n) -> p c n", c=3)
            if n == 0:
                wait(act, done, *pT2_free[buf])
                cps.append(AC.mark(act.activation(dst, src, ACT.Copy)))
            else:
                wait(dve, done, *pT2_free[buf])
                cps.append(DV.mark(dve.tensor_copy(dst, src)))
            b.free = (cps[-1],)
        ob = bank[6 + buf]
        wait(pe, *cps, *v_all, *ob.free)
        for kc in range(2 * NG):
            mm = pe.matmul(ob.t[:, 0:HD2], pT2[:, buf, kc, :], v2[:, kc // 2, kc % 2, h * HD2:(h + 1) * HD2],
                           start=(kc == 0), stop=(kc == 2 * NG - 1))
        done = PE.mark(mm)
        pT2_free[buf] = (done,)
        wait(dve, done, rs_ok)
        ok = DV.mark(dve.tensor_scalar(yb[:, t, h * HD2:(h + 1) * HD2], ob.t[:, 0:HD2], smax[:, 2, t, h:h + 1], None,
                                       ALU.mult))
        ob.free = (ok,)
        return ok, done

    def gates(j, dst, done, free=()):
        pair = pair_of(("g", j))
        cols = slice((j % 2) * WIDE, (j % 2 + 1) * WIDE)
        for t in range(TILES):
            wait(dve, done, two_in, *free)
            s = DV.mark(dve.tensor_tensor(dst[:, t, cols], pair[t].t[:], bg[j // 2][:, cols], ALU.add))
            pair[t].free = (s,)
            wait(act, s)
            ok = AC.mark(act.activation(dst[:, t, cols], dst[:, t, cols], ACT.Sigmoid))
        return ok

    done = product(("g", 0), per_tile(pair_of(("g", 0))))
    g_a = tmp
    gates(0, g_a, done, free=(h3[-1],))
    for n in range(4):
        yb_ok, last_pv = attend2(n // 4, n % 4, n % 2)
    done = product(("g", 1), per_tile(pair_of(("g", 1))))
    ga_ok = gates(1, g_a, done)
    for n in range(4, 8):
        yb_ok, last_pv = attend2(n // 4, n % 4, n % 2)

    def branch(kind, ready):
        outs = [bank[0:2], bank[2:4]]
        return product((kind, 0), outs, ready=ready), outs

    done, outs = branch("a", ya_cut)
    wait(dve, done, ga_ok)
    for t in range(TILES):
        for half in range(2):
            cols, b = slice(half * WIDE, (half + 1) * WIDE), outs[t][half]
            m_ok = DV.mark(dve.tensor_tensor(tmp[:, t, cols], tmp[:, t, cols], b.t[:], ALU.mult))
            b.free = (m_ok,)
    yb_cut = turn_and_cut(yb, 4, None, (yb_ok,), bank[4:6], out_hi=f_hi, out_lo=f_lo, free=(done,))
    g_b = sc[:].rearrange("p t h n -> p (t h n)")[:, 0:TILES * D].rearrange("p (t n) -> p t n", t=TILES)
    for j in (2, 3):
        done = product(("g", j), per_tile(pair_of(("g", j))))
        gb_ok = gates(j, g_b, done, free=(last_pv,))
    h_read = done
    done, outs = branch("b", yb_cut)
    wait(dve, done, gb_ok, m_ok)
    for t in range(TILES):
        for half in range(2):
            cols, b = slice(half * WIDE, (half + 1) * WIDE), outs[t][half]
            s = DV.mark(dve.tensor_tensor(g_b[:, t, cols], g_b[:, t, cols], b.t[:], ALU.mult))
            b.free = (s,)
            wait(dve, s)
            m_ok = DV.mark(dve.tensor_tensor(tmp[:, t, cols], tmp[:, t, cols], g_b[:, t, cols], ALU.add))
    merged = turn_and_cut(tmp, KC, None, (m_ok,), bank[4:8], free=(h_read,))
    wait(pool, ga_ok)
    post_in = post_load[0].mark(pool.dma_start(bg[0][:], a["norm_mix_post_2"][0:1, :].broadcast_to([P, D])), 16)
    wait(pool, gb_ok)
    post2_in = post_load[1].mark(pool.dma_start(bg[1][:], a["norm_mlp_post_2"][0:1, :].broadcast_to([P, D])), 16)
    two.close()

    def up_slab2(i, s):
        src = a["w_up_2"][0][2 * s * P:(2 * s + 2) * P, bass.ds(i * WIDE, WIDE)].rearrange("(c p) n -> p c n", p=P)
        return [(lambda raw: raw.rearrange("p (c n) -> p c n", c=2), src)]

    m0, m1 = ("o", 0), ("o", 1)
    done0 = product(m0, per_tile(pair_of(m0)), ready=merged)
    done1 = product(m1, per_tile(pair_of(m1)))
    first_up(up_slab2)

    def post_norm(banks_of, dones, gain, gain_in, free):
        for t in range(TILES):
            ss = stat[:, 4 + 2 * t:6 + 2 * t]
            wait(act, *dones, *free)
            for half in range(2):
                cols = slice(half * WIDE, (half + 1) * WIDE)
                u = AC.mark(act.activation(tmp[:, t, cols], banks_of[t][half].t[:], ACT.Square,
                                           accum_out=ss[:, half:half + 1]))
            wait(dve, u)
            u = DV.mark(dve.tensor_tensor(ss[:, 0:1], ss[:, 0:1], ss[:, 1:2], ALU.add))
            wait(dve, u)
            u = inverse_root(ss[:, 0:1], 1.0 / D, EPS)
            wait(dve, u, gain_in)
            for half in range(2):
                cols, b = slice(half * WIDE, (half + 1) * WIDE), banks_of[t][half]
                u = DV.mark(dve.scalar_tensor_tensor(tmp[:, t, cols], b.t[:], ss[:, 0:1], gain[:, cols],
                                                     ALU.mult, ALU.mult))
                b.free = (u,)
            wait(dve, u)
            ok = DV.mark(dve.tensor_tensor(x[:, t, :], x[:, t, :], tmp[:, t, :], ALU.add))
            yield ok

    mix_banks = [[pair_of(m0)[t], pair_of(m1)[t]] for t in range(TILES)]
    x_marks = list(post_norm(mix_banks, (done0, done1), bg[0], post_in, (merged[-1],)))
    n3 = [rms_scale(x[:, t, :], tmp[:, t, :], (x_marks[t],), P, t) for t in range(TILES)]
    h4 = turn_and_cut(tmp, KC, lambda c: gains[:, 3, c:c + 1], n3, bank[4:8], free=(done1,))
    ff2 = feed_forward(8, up_slab2, lambda i, c: a["w_down_2"][0][bass.ds((4 * i + c) * P, P), :], 4, True, h4,
                       lambda: None)

    acc_banks = [bank[4:6], bank[6:8]]
    stored = [Line(nc, ctx, f"stored{t}") for t in range(TILES)]
    for t, ok in enumerate(post_norm(acc_banks, (ff2,), bg[1], post2_in, ())):
        wait(sp, ok)
        stored[t].mark(sp.dma_start(out[0, t * P:(t + 1) * P, :], x[:, t, :]), 16)
    wait(sp, *[Mark(line, line.n) for line in stored])


_INS = ["x", "meta_tokens", "attn_norm_g", "w_in", "a_q_norm_g", "a_k_norm_g", "b_q_norm_g", "b_k_norm_g",
        "b_lambda_q1", "b_lambda_k1", "b_lambda_q2", "b_lambda_k2", "b_subln_g", "w_out", "ffn_norm_g", "w_gate",
        "w_up", "w_down", "norm_mix_pre_2", "w_in_2", "b_gate_2", "ln_v_gain_2", "ln_v_bias_2", "w_spatial_2",
        "b_spatial_2", "w_branch_a_2", "w_branch_b_2", "w_out_2", "norm_mix_post_2", "norm_mlp_pre_2", "w_up_2",
        "w_down_2", "norm_mlp_post_2"]


def kernel(**inputs):
    import concourse.bacc as _bacc
    from concourse.bass_utils import run_bass_kernel_spmd as _run

    nc = _bacc.Bacc("TRN2", target_bir_lowering=False, num_devices=1)
    arrays = {name: np.ascontiguousarray(inputs[name]) for name in _INS}
    one, two = rope_tables()
    arrays.update(rope1=one, rope2=two, mask=masks(), ident=np.eye(P, dtype=np.float32))
    args = {n: nc.dram_tensor(f"in_{n}", v.shape, mybir.dt.from_np(v.dtype), kind="ExternalInput").ap()
            for n, v in arrays.items()}
    out = nc.dram_tensor("out_0", (1, SEQ, D), F32, kind="ExternalOutput").ap()
    program(nc, args, out)
    r = _run(nc, [{f"in_{n}": v for n, v in arrays.items()}], core_ids=[0])
    return r.results[0]["out_0"]
```

```python
import math
from contextlib import ExitStack

import numpy as np

import concourse.bass as bass
from concourse import mybir

F32 = mybir.dt.float32
F32R = mybir.dt.float32r
ALU = mybir.AluOpType
ACT = mybir.ActivationFunctionType
AX = mybir.AxisListType.X

P = 128
D = 1024
SEQ = 256
META = 16
TILES = SEQ // P
KC = D // P
KEYS = SEQ + META
EPS = 1e-6
WIDE = 512

HD = 64
A_HEADS, A_KV = 8, 2
B_HEADS, B_V = 4, 128
LAM_INIT = 0.8 - 0.6 * math.exp(-0.3 * 0)
D_FF = -(-8 * D // (3 * 256)) * 256

GMLP = 512
GROUPS = 4
PATTERNS = ((128, 1), (512, 4), (2048, 16))
NG = len(PATTERNS)
HD2 = 128
HEADS2 = 4
ROPE2 = HD2 // 4
D_FF2 = 4 * D
MASKED = -1e30

SLOTS = 8
RAW_SLOTS = 4
SLOT = 1024


def rope_tables():
    f = np.float32
    half = HD // 2
    inv_a = (f(10000.0) ** (-np.arange(0, half, 2, dtype=f) / f(half))).astype(f)
    t = np.arange(SEQ)
    ang_a = np.zeros((KEYS, half), f)
    ang_a[:SEQ] = np.concatenate([(t // 64).astype(f)[:, None] * inv_a, (t % 64).astype(f)[:, None] * inv_a], 1)
    inv_b = (f(10000.0) ** (-np.arange(0, HD, 2, dtype=f) / f(HD))).astype(f)
    pos = np.concatenate([META + t, np.arange(META)]).astype(f)
    ang_b = pos[:, None] * inv_b
    one = np.zeros((KEYS, 4, HD), f)
    for n, ang in ((0, ang_a), (2, ang_b)):
        one[:, n, :] = np.repeat(np.cos(ang), 2, axis=1)
        one[:, n + 1, 0::2] = -np.sin(ang)
        one[:, n + 1, 1::2] = np.sin(ang)
    inv_2 = (f(500000.0) ** (-np.arange(0, ROPE2, 2, dtype=f) / f(ROPE2))).astype(f)
    ang_2 = t.astype(f)[:, None] * inv_2
    two = np.zeros((SEQ, 2, ROPE2), f)
    two[:, 0, :] = np.concatenate([np.cos(ang_2), np.cos(ang_2)], 1)
    two[:, 1, :] = np.concatenate([-np.sin(ang_2), np.sin(ang_2)], 1)
    return one, two


def masks():
    q, k = np.arange(SEQ)[:, None], np.arange(SEQ)[None, :]
    out = np.full((SEQ, NG, SEQ), MASKED, np.float32)
    for g, (window, dilation) in enumerate(PATTERNS):
        seen = ((q - k) % dilation == 0) & (np.abs(q // dilation - k // dilation) <= window // (2 * dilation))
        out[:, g, :][seen] = 0.0
    return np.stack([out[0:P, 0], out[P:SEQ, 0], out[0:P, 1], out[0:P, 2]], axis=1)


class Mark:

    def __init__(self, line, n):
        self.line, self.n = line, n


class Line:

    every = []
    seen = {}
    rounds = None
    floor = {}

    def __init__(self, nc, ctx, name):
        self.sem = ctx.enter_context(nc.semaphore(name))
        self.name, self.n, self.stride = name, 0, 0
        Line.every.append(self)

    def mark(self, ins, by=1):
        ins.then_inc(self.sem, by)
        self.n += by
        return Mark(self, self.n)


def wait(eng, *marks):
    latest = {}
    for m in marks:
        latest[m.line] = max(latest.get(m.line, 0), m.n)
    for line, n in latest.items():
        if Line.rounds is None:
            seen = Line.seen.setdefault(eng.engine, {})
            if seen.get(line, 0) < n:
                eng.wait_ge(line.sem, n)
                seen[line] = n
        else:
            assert n > Line.floor[line], f"{line.name}: a mark from before the round ahead of the loop"
            eng.wait_ge(line.sem, Line.rounds * line.stride + n)


def run_steps(nc, step, n_steps, peeled_last=1):
    step(0, 0)
    step(1, 1)
    before = {line: line.n for line in Line.every}
    step(2, 2)
    for line in Line.every:
        line.stride = line.n - before[line]
    last = n_steps - peeled_last
    start = {line: line.n for line in Line.every}
    for line in Line.every:
        line.loop_start = line.n
    with nc.Fori(0, last - 3) as i:
        Line.rounds, Line.floor = i, before
        step(i + 3, 3)
        Line.rounds = None
    more = last - 4
    for line in Line.every:
        assert line.n - start[line] == line.stride, (line.name, line.n - start[line], line.stride)
        line.n += line.stride * more
    return more


class Bank:

    def __init__(self, nc, ctx, name):
        self.t = ctx.enter_context(nc.psum_tensor(name, [P, WIDE], F32))
        self.free = ()


class Ring:

    def __init__(self, nc, ctx):
        self.nc = nc
        self.raw = ctx.enter_context(nc.sbuf_tensor("w_raw", [P, RAW_SLOTS, SLOT], F32))
        self.hi = ctx.enter_context(nc.sbuf_tensor("w_hi", [P, SLOTS, SLOT], F32R))
        self.lo = ctx.enter_context(nc.sbuf_tensor("w_lo", [P, SLOTS, SLOT], F32R))
        self.loaded = [Line(nc, ctx, f"w_loaded{r}") for r in range(RAW_SLOTS)]
        self.rounded = Line(nc, ctx, "w_hi_done")
        self.cut = Line(nc, ctx, "w_lo_done")
        self.used = Line(nc, ctx, "w_used")
        self.held = [False] * SLOTS
        self.raw_free = [() for _ in range(RAW_SLOTS)]
        self.ready = [None] * SLOTS
        self.free = [() for _ in range(SLOTS)]

    def fill(self, s, pieces, n=SLOT):
        nc, r = self.nc, s % RAW_SLOTS
        assert not self.held[s], "the slot's weights are still to be multiplied"
        self.held[s] = True
        raw = self.raw[:, r, :]
        wait(nc.sync, *self.raw_free[r])
        for view, src in pieces:
            full = self.loaded[r].mark(nc.sync.dma_start(view(raw), src), 16)
        wait(nc.scalar, full, *self.free[s])
        rounded = self.rounded.mark(nc.scalar.activation(self.hi[:, s, 0:n], raw[:, 0:n], ACT.Copy))
        wait(nc.vector, rounded)
        self.ready[s] = self.cut.mark(nc.vector.tensor_tensor(self.lo[:, s, 0:n], raw[:, 0:n], self.hi[:, s, 0:n],
                                                              ALU.subtract))
        self.raw_free[r] = (self.ready[s],)

    def release(self, s, last_matmul):
        self.held[s] = False
        self.free[s] = (last_matmul,)

    def done(self, s, ins):
        self.release(s, self.used.mark(ins))
        return self.free[s][0]


class Slab:

    def __init__(self, ring, src, first, chunks, cols):
        self.ring, self.src, self.first, self.chunks, self.cols = ring, src, first, chunks, cols
        self.per = SLOT // max(cols, WIDE)
        self.n_slots = chunks // self.per

    def view(self, slot):
        return slot[:, 0:self.per * self.cols].rearrange("p (c n) -> p c n", c=self.per)

    def prepare(self, part=None):
        for j in part or range(self.n_slots):
            rows = self.src[j * self.per * P:(j + 1) * self.per * P, :].rearrange("(c p) n -> p c n", p=P)
            self.ring.fill(self.first + j, [(self.view, rows)], self.per * self.cols)

    def multiply(self, x_hi, x_lo, outs, x_ready=None, meta=None):
        ring, pe = self.ring, self.ring.nc.tensor
        width = min(self.cols, WIDE)
        for t in outs:
            for b in t:
                wait(pe, *b.free)
        if meta:
            wait(pe, *meta[1].free)
        for j in range(self.n_slots):
            s = self.first + j
            wait(pe, ring.ready[s])
            w_hi, w_lo = self.view(ring.hi[:, s, :]), self.view(ring.lo[:, s, :])
            for c in range(self.per):
                kc = j * self.per + c
                if x_ready:
                    wait(pe, x_ready[kc])
                first, last = kc == 0, kc == self.chunks - 1
                mm = three_passes(pe, x_hi, x_lo, w_hi[:, c, :], w_lo[:, c, :], kc, outs, width, first, last)
                if meta:
                    for n, w in enumerate((w_hi, w_lo)):
                        mm = pe.matmul(meta[1].t[:, 0:width], meta[0][:, kc, :], w[:, c, 0:width],
                                       start=first and n == 0, stop=last and n == 1)
            done = ring.done(s, mm)
        return done


    def multiply_by_bank(self, x_hi, x_lo, outs, x_ready=None):
        ring, pe = self.ring, self.ring.nc.tensor
        places = [(self.first + kc // self.per, kc % self.per, kc) for kc in range(self.chunks)]
        done = [[None] * len(t) for t in outs]
        for h in range(len(outs[0])):
            for t in range(TILES):
                b = outs[t][h]
                wait(pe, *b.free)
                for s, c, kc in places:
                    wait(pe, ring.ready[s])
                    if x_ready:
                        wait(pe, x_ready[kc])
                    w_hi, w_lo = self.view(ring.hi[:, s, :])[:, c, :], self.view(ring.lo[:, s, :])[:, c, :]
                    for n, (x, w) in enumerate(((x_hi, w_hi), (x_hi, w_lo), (x_lo, w_hi))):
                        mm = pe.matmul(b.t[:], x[:, kc, t * P:(t + 1) * P], w[:, h * WIDE:(h + 1) * WIDE],
                                       start=kc == 0 and n == 0, stop=kc == self.chunks - 1 and n == 2)
                done[t][h] = ring.used.mark(mm)
        for j in range(self.n_slots):
            ring.release(self.first + j, done[-1][-1])
        return done


def three_passes(pe, x_hi, x_lo, w_hi, w_lo, kc, outs, width, first, last):
    for t in range(TILES):
        for n, (x, w) in enumerate(((x_hi, w_hi), (x_hi, w_lo), (x_lo, w_hi))):
            for h, b in enumerate(outs[t]):
                mm = pe.matmul(b.t[:, 0:width], x[:, kc, t * P:(t + 1) * P], w[:, h * width:(h + 1) * width],
                               start=first and n == 0, stop=last and n == 2)
    return mm


def program(nc, a, out):
    with ExitStack() as ctx:
        Line.every, Line.seen = [], {}
        build(nc, ctx, a, out)


def build(nc, ctx, a, out):
    pe, act, dve, pool, sp = nc.tensor, nc.scalar, nc.vector, nc.gpsimd, nc.sync

    def sb(name, shape, dt=F32, c=ctx):
        return c.enter_context(nc.sbuf_tensor(name, shape, dt))

    PE, AC, DV, PO = (Line(nc, ctx, n) for n in ("tensor_done", "scalar_done", "vector_done", "pool_done"))
    bank = [Bank(nc, ctx, f"bank{n}") for n in range(8)]
    MM = [bank[0:2], bank[2:4]]
    ring = Ring(nc, ctx)

    def per_tile(pair):
        return [[pair[0]], [pair[1]]]

    x_line, x_in = [Line(nc, ctx, f"x{t}_loaded") for t in range(TILES)], []
    ident_load, gain_load, rest_load, meta_load = (Line(nc, ctx, n) for n in (
        "identity_loaded", "first_gain_loaded", "other_gains_loaded", "meta_loaded"))
    small = Line(nc, ctx, "small_loaded")
    post_load = [Line(nc, ctx, f"post_gain{n}_loaded") for n in range(2)]
    consts = Line(nc, ctx, "block2_loaded")
    x = sb("x", [P, TILES, D])
    tmp = sb("tmp", [P, TILES, D])
    ident = sb("ident", [P, P])
    gains = sb("gains", [P, 4, KC])
    stat = sb("stat", [P, 32])
    half_neg = sb("minus_half", [P, 2 * 8])
    row_scale = sb("row_scale", [P, 4, TILES])
    gain_rows = sb("gain_rows", [4 * KC, P])
    h_hi = sb("h_hi", [P, KC, SEQ], F32R)
    h_lo = sb("h_lo", [P, KC, SEQ], F32R)

    one = ctx.enter_context(ExitStack())
    xm = sb("xm", [META, D], c=one)
    for t in range(TILES):
        x_in.append(x_line[t].mark(sp.dma_start(x[:, t, :], a["x"][0, t * P:(t + 1) * P, :]), 16))
    ident_in = ident_load.mark(act.dma_start(ident[:], a["ident"]), 16)
    for n, name in enumerate(("attn_norm_g", "ffn_norm_g", "norm_mix_pre_2", "norm_mlp_pre_2")):
        rows = act.dma_start(gain_rows[n * KC:(n + 1) * KC, :], a[name][0].rearrange("(c p) -> c p", p=P))
        if n == 0:
            gain_in = gain_load.mark(rows, 16)
        else:
            gains_in = rest_load.mark(rows, 16)
    xm_in = meta_load.mark(act.dma_start(xm[:], a["meta_tokens"]), 16)

    cuts = (("qa", A_HEADS * HD), ("kva", 2 * A_KV * HD), ("qb", 2 * B_HEADS * HD), ("kb", 2 * B_HEADS * HD),
            ("vb", B_HEADS * B_V))
    spans, o = {}, 0
    for name, n in cuts:
        spans[name] = (o, o + n)
        o += n
    slabs = {}
    for n, name in enumerate(("qb", "kb", "vb", "kva", "qa")):
        c0, c1 = spans[name]
        slabs[name] = Slab(ring, a["w_in"][0][:, c0:c1], 4 * (n % 2), KC, c1 - c0)
    for h in range(2):
        slabs[f"out{h}"] = Slab(ring, a["w_out"][0][:, h * WIDE:(h + 1) * WIDE], 4 * h, KC, WIDE)

    rope1 = sb("rope1", [P, TILES, 4, HD], c=one)
    rope1m = sb("rope1m", [META, 4, HD], c=one)
    hg = sb("head_gains", [P, 4, HD], c=one)
    lamv = sb("lam_vectors", [P, 4, HD], c=one)
    subln = sb("subln", [P, 1], c=one)
    pool.dma_start(rope1[:], a["rope1"][0:SEQ].rearrange("(t p) k d -> p t k d", p=P)).then_inc(small.sem, 16)
    pool.dma_start(rope1m[:], a["rope1"][SEQ:KEYS]).then_inc(small.sem, 16)
    for n, name in enumerate(("a_q_norm_g", "a_k_norm_g", "b_q_norm_g", "b_k_norm_g")):
        pool.dma_start(hg[:, n, :], a[name][0:1, :].broadcast_to([P, HD])).then_inc(small.sem, 16)
    for n, name in enumerate(("b_lambda_q1", "b_lambda_k1", "b_lambda_q2", "b_lambda_k2")):
        pool.dma_start(lamv[:, n, :], a[name][0:1, :].broadcast_to([P, HD])).then_inc(small.sem, 16)
    small.n += 10 * 16
    small_in = small.mark(pool.dma_start(subln[:], a["b_subln_g"][0].rearrange("(p o) -> p o", o=1),
                                         allow_slow_non_contiguous=True), 16)

    half_ok = PO.mark(pool.memset(half_neg[:], -0.5))

    def inverse_root(v, scale, bias):
        rows, n = v.shape[0], v.shape[1]
        t = DV.mark(dve.tensor_scalar(v, v, scale, bias, ALU.mult, ALU.add))
        wait(pool, t, half_ok)
        return PO.mark(pool.tensor_tensor(v, v, half_neg[0:rows, 0:n], ALU.pow))

    def norm_scale(n, ready):
        for t in range(TILES):
            wait(act, *ready[t])
            m = AC.mark(act.activation(tmp[:, t, :], x[:, t, :], ACT.Square, accum_out=row_scale[:, n, t:t + 1]))
        wait(dve, m)
        return inverse_root(row_scale[:, n, :], 1.0 / D, EPS)

    def turn_and_cut(src, chunks, gain, ready, banks, out_hi=h_hi, out_lo=h_lo, free=(), at=0):
        marks = {}
        pairs = [chunks[n:n + 2] for n in range(0, len(chunks), 2)]
        for n0 in range(0, len(pairs), len(banks)):
            group = list(zip(pairs[n0:n0 + len(banks)], banks))
            turned = {}
            for t in range(TILES):
                wait(pe, *ready[t])
                for pair, b in group:
                    if t == 0:
                        wait(pe, *b.free)
                    for j, c in enumerate(pair):
                        tr = pe.transpose(b.t[:, j * SEQ + t * P:j * SEQ + (t + 1) * P], src[:, t, c * P:(c + 1) * P],
                                          ident[:])
                    turned[b] = PE.mark(tr)
            for pair, b in group:
                wait(act, turned[b], *free)
                if gain is None:
                    d = slice(pair[0] + at, pair[1] + at + 1)
                    both = b.t[:].rearrange("p (c n) -> p c n", c=2)
                    wait(dve, AC.mark(act.activation(out_hi[:, d, :], both, ACT.Copy)))
                    t_lo = DV.mark(dve.tensor_tensor(out_lo[:, d, :], both, out_hi[:, d, :], ALU.subtract))
                    marks[pair[0] + at] = marks[pair[1] + at] = t_lo
                else:
                    for j, c in enumerate(pair):
                        rounded = AC.mark(act.activation(out_hi[:, c + at, :], b.t[:, j * SEQ:(j + 1) * SEQ],
                                                         ACT.Copy, scale=gain(c)))
                    wait(dve, rounded)
                    for j, c in enumerate(pair):
                        t_lo = DV.mark(dve.scalar_tensor_tensor(out_lo[:, c + at, :], b.t[:, j * SEQ:(j + 1) * SEQ],
                                                                gain(c), out_hi[:, c + at, :], ALU.mult, ALU.subtract))
                        marks[c + at] = t_lo
                b.free = (t_lo,)
        return marks

    ALL, LEFT, RIGHT = range(KC), range(KC // 2), range(KC // 2, KC)

    meta_stack = sb("meta_stack", [P, KC, P], F32R, c=one)
    meta_t = sb("meta_t", [P, KC, META], c=one)
    t_zero = PO.mark(pool.memset(meta_stack[:].bitcast(F32), 0.0))
    wait(act, DV.mark(dve.memset(stat[:, 0:1], 0.0)))
    act.activation(stat[:, 1:2], stat[:, 0:1], ACT.Copy)
    wait(pe, ident_in, gain_in)
    wait(dve, PE.mark(pe.transpose(bank[7].t[:, 0:KC], gain_rows[0:KC, :], ident[0:KC, 0:KC])))
    gain_ok = DV.mark(dve.tensor_copy(gains[:, 0, :], bank[7].t[:, 0:KC]))
    bank[7].free = (gain_ok,)
    wait(act, gain_ok)
    first_gain = lambda c: gains[:, 0, c:c + 1]
    h1 = turn_and_cut(x, LEFT, first_gain, [(m,) for m in x_in], bank[3:5])
    slabs["qb"].prepare(range(0, 2))
    h1.update(turn_and_cut(x, RIGHT, first_gain, [(m,) for m in x_in], bank[5:7]))
    slabs["qb"].prepare(range(2, 4))
    xm_sq = sb("xm_sq", [META, D], c=one)
    r_meta = sb("row_scale_meta", [META, 1], c=one)
    wait(act, xm_in)
    wait(dve, AC.mark(act.activation(xm_sq[:], xm[:], ACT.Square, accum_out=r_meta[:])))
    rm_ok = inverse_root(r_meta[:], 1.0 / D, EPS)
    r1_ok = norm_scale(0, [(m,) for m in x_in])

    lamp = sb("lam_products", [P, 2, HD], c=one)
    lam = sb("lam", [P, 4], c=one)
    lv = lamv[:].rearrange("p (j s) d -> p j s d", s=2)
    wait(dve, small_in)
    t = DV.mark(dve.tensor_tensor(lamp[:], lv[:, :, 0, :], lv[:, :, 1, :], ALU.mult))
    wait(dve, t)
    t = DV.mark(dve.tensor_reduce(lam[:, 0:2], lamp[:], AX, ALU.add))
    wait(act, t)
    t = AC.mark(act.activation(lam[:, 2:4], lam[:, 0:2], ACT.Exp))
    wait(dve, t)
    t = DV.mark(dve.tensor_tensor(lam[:, 0:1], lam[:, 3:4], lam[:, 2:3], ALU.subtract))
    wait(dve, t)
    lam_ok = DV.mark(dve.tensor_scalar(lam[:, 1:2], lam[:, 0:1], -LAM_INIT, None, ALU.add))
    subln_ok = DV.mark(dve.tensor_scalar(subln[:], subln[:], 1.0 - LAM_INIT, None, ALU.mult))

    rg = sb("rope_gain", [P, TILES, 4, 2, HD], c=one)
    rgm = sb("rope_gain_meta", [META, 4, 2, HD], c=one)
    wait(pool, small_in)
    for kind in range(4):
        base = 2 * (kind // 2)
        for dst, tab, g in [(rg[:, t, kind], rope1[:, t], hg[:, kind, :]) for t in range(TILES)] + \
                [(rgm[:, kind], rope1m[:], hg[0:META, kind, :])]:
            pool.tensor_tensor(dst[:, 0, :], tab[:, base, :], g, ALU.mult)
            for e in range(2):
                rg_done = PO.mark(pool.tensor_tensor(dst[:, 1, e::2], tab[:, base + 1, e::2], g[:, 1 - e::2],
                                                     ALU.mult))

    xn = sb("head_normed", [P, 2, WIDE], c=one)
    part = sb("rope_part", [P, 2, WIDE], c=one)
    mcopy = sb("meta_copy", [META, WIDE], c=one)
    msum = sb("meta_sum", [META, WIDE], c=one)
    xn_free = []

    def by_head(v):
        return v.rearrange("p (h d) -> p h d", d=HD)

    def norm_and_rope(srcs, heads, tables, scales, is_q, ready, dsts):
        rows, n, count = srcs[0].shape[0], heads * HD, len(srcs)
        ss = stat[0:rows, 8:8 + count * heads]
        ss_of = [ss[:, i * heads:(i + 1) * heads] for i in range(count)]
        x_t = [xn[0:rows, i, 0:n] for i in range(count)]
        p_t = [part[0:rows, i, 0:n] for i in range(count)]
        wait(act, *ready, *xn_free)
        for i in range(count):
            m = AC.mark(act.activation(x_t[i], srcs[i], ACT.Square, scale=scales[i]))
            wait(dve, m)
            m = DV.mark(dve.tensor_reduce(ss_of[i], by_head(x_t[i]), AX, ALU.add))
        wait(dve, m)
        m = inverse_root(ss, 1.0, HD * EPS) if is_q else inverse_root(ss, 1.0 / HD, EPS)
        wait(dve, m)
        for i in range(count):
            m = DV.mark(dve.tensor_scalar(ss_of[i], ss_of[i], scales[i], None, ALU.mult))
        wait(dve, m)
        read = []
        for i in range(count):
            read.append(DV.mark(dve.tensor_tensor(by_head(x_t[i]), by_head(srcs[i]),
                                                  ss_of[i].unsqueeze(2).broadcast_to([rows, heads, HD]), ALU.mult)))
        swapped, turned = [], []
        for i in range(count):
            eng, line = (pool, PO) if i == 0 and count > 1 else (dve, DV)
            wait(eng, read[i], rg_done, *xn_free)
            for e in range(2):
                m = line.mark(eng.tensor_tensor(by_head(p_t[i])[:, :, e::2], by_head(x_t[i])[:, :, 1 - e::2],
                                                tables[i][:, 1, e::2].unsqueeze(1).broadcast_to([rows, heads, HD // 2]),
                                                ALU.mult))
            swapped.append(m)
        for i in reversed(range(count)):
            wait(dve, swapped[i])
            m = DV.mark(dve.tensor_tensor(by_head(x_t[i]), by_head(x_t[i]),
                                          tables[i][:, 0, :].unsqueeze(1).broadcast_to([rows, heads, HD]), ALU.mult))
            wait(dve, m)
            for d in dsts[i]:
                done = DV.mark(dve.tensor_tensor(d, by_head(x_t[i]), by_head(p_t[i]), ALU.add))
        xn_free[:] = [done]
        return read, done

    qn = sb("q_rows", [P, TILES, WIDE], c=one)
    kb = sb("kb", [P, TILES, WIDE], c=one)
    kbm = sb("kb_meta", [META, WIDE], c=one)
    vb = sb("vb", [P, TILES, WIDE], c=one)
    vbm = sb("vb_meta", [META, WIDE], c=one)
    kw = A_KV * HD
    ka = sb("ka", [P, TILES, 2 * kw], c=one)
    kam = sb("ka_meta", [META, 2 * kw], c=one)
    va = sb("va", [P, TILES, kw], c=one)
    vam = sb("va_meta", [META, kw], c=one)

    def add_meta(done, n, b, free=()):
        wait(act, done, rm_ok, *free)
        wait(dve, AC.mark(act.activation(mcopy[:, 0:n], b.t[32:32 + META, 0:n], ACT.Copy, scale=r_meta[:])))
        t = DV.mark(dve.scalar_tensor_tensor(msum[:, 0:n], b.t[0:META, 0:n], r_meta[:], mcopy[:, 0:n],
                                             ALU.mult, ALU.add))
        b.free = (t,)
        return t

    def rope_tiles(pair, kind, is_q, dst, done, free=()):
        wait(dve, *free)
        wait(act, r1_ok)
        read, ok = norm_and_rope([b.t[:] for b in pair], 8, [rg[:, t, kind] for t in range(TILES)],
                                 [row_scale[:, 0, t:t + 1] for t in range(TILES)], is_q, (done,),
                                 [[by_head(dst[:, t, :])] for t in range(TILES)])
        for t in range(TILES):
            pair[t].free = (read[t],)
        return ok

    one_scale = sb("one_scale", [META, 1], c=one)
    one_ok = PO.mark(pool.memset(one_scale[:], 1.0))

    qT = sb("qT1", [P, 4, SEQ], c=one)
    kbT = sb("kbT", [P, 4, KEYS], c=one)
    kaT = sb("kaT", [P, 2, KEYS], c=one)

    def turn_heads(src, dst, chunks, ready, banks, free=(), metas=None):
        wait(pe, *ready)
        wait(act, *free)
        wait(dve, *free)
        marks = []
        for n, c0 in enumerate(range(0, chunks, 2)):
            b = banks[n % len(banks)]
            wait(pe, *b.free)
            for c in range(2):
                for t in range(TILES):
                    tr = pe.transpose(b.t[:, c * SEQ + t * P:c * SEQ + (t + 1) * P],
                                      src[:, t, (c0 + c) * P:(c0 + c + 1) * P], ident[:])
            pair, done = b.t[:].rearrange("p (c n) -> p c n", c=2), PE.mark(tr)
            if n % 2 == 0:
                wait(act, done)
                m = AC.mark(act.activation(dst[:, c0:c0 + 2, 0:SEQ], pair, ACT.Copy))
            else:
                wait(dve, done)
                m = DV.mark(dve.tensor_copy(dst[:, c0:c0 + 2, 0:SEQ], pair))
            b.free = (m,)
            marks.append(m)
        if metas is not None:
            b = banks[-1]
            wait(pe, *b.free)
            for c in range(chunks):
                tr = pe.transpose(b.t[:, c * META:(c + 1) * META], metas[:, c * P:(c + 1) * P], ident[0:META, 0:META])
            wait(dve, PE.mark(tr))
            m = DV.mark(dve.tensor_copy(dst[:, :, SEQ:KEYS],
                                        b.t[:, 0:chunks * META].rearrange("p (c n) -> p c n", c=chunks)))
            b.free = (m,)
            marks.append(m)
        return marks

    maps = sb("maps1", [P, TILES, 8, KEYS], c=one)
    den = sb("den1", [P, 2, TILES, 8], c=one)
    nmax = sb("nmax1", [P, 2, TILES, 8], c=one)
    rden = sb("rden1", [P, 2, TILES, 8], c=one)

    def scores(t, h, kT, k_chunk, which, b, free):
        p0 = HD * (h % 2)
        wait(pe, *b.free)
        wait(dve, PE.mark(pe.matmul(b.t[:, 0:KEYS], qT[p0:p0 + HD, h // 2, t * P:(t + 1) * P],
                                    kT[p0:p0 + HD, k_chunk, :], start=True, stop=True)))
        m = DV.mark(dve.tensor_reduce(nmax[:, which, t, h:h + 1], b.t[:, 0:KEYS], AX, ALU.max, negate=True))
        wait(act, m, *free)
        e = AC.mark(act.activation(maps[:, t, h, :], b.t[:, 0:KEYS], ACT.Exp, bias=nmax[:, which, t, h:h + 1],
                                   accum_out=den[:, which, t, h:h + 1]))
        b.free = (e,)
        return e

    pT = sb("pT", [P, 2, 2, SEQ], c=one)
    pTm = sb("pTm", [META, 2, SEQ], c=one)
    pT_free = [(), ()]

    def turn_map(h, buf, ready, b, ob, by_act=False):
        wait(pe, *ready, *b.free, *ob.free)
        for t in range(TILES):
            for c in range(2):
                pe.transpose(b.t[:, c * SEQ + t * P:c * SEQ + (t + 1) * P], maps[:, t, h, c * P:(c + 1) * P], ident[:])
            tr = pe.transpose(ob.t[0:META, SEQ + t * P:SEQ + (t + 1) * P], maps[:, t, h, SEQ:KEYS], ident[:])
        done = PE.mark(tr)
        wait(act, done, *pT_free[buf])
        m1 = AC.mark(act.activation(pT[:, buf], b.t[:].rearrange("p (c n) -> p c n", c=2), ACT.Copy))
        if by_act:
            m2 = AC.mark(act.activation(pTm[:, buf, :], ob.t[0:META, SEQ:2 * SEQ], ACT.Copy))
        else:
            wait(dve, done, *pT_free[buf])
            m2 = DV.mark(dve.tensor_copy(pTm[:, buf, :], ob.t[0:META, SEQ:2 * SEQ]))
        b.free, ob.free = (m1,), (m2,)
        return (m1, m2), done

    def weights_times_values(buf, ready, ob, v, vm, cols):
        n = cols.stop - cols.start
        wait(pe, *ready)
        for t in range(TILES):
            for c in range(2):
                pe.matmul(ob.t[:, t * n:(t + 1) * n], pT[:, buf, c, t * P:(t + 1) * P], v[:, c, cols],
                          start=(c == 0), stop=False)
            mm = pe.matmul(ob.t[:, t * n:(t + 1) * n], pTm[:, buf, t * P:(t + 1) * P], vm[:, cols],
                           start=False, stop=True)
        done = PE.mark(mm)
        pT_free[buf] = (done,)
        return done

    slabs["kb"].prepare()
    t_qb = slabs["qb"].multiply(h_hi, h_lo, per_tile(MM[0]), x_ready=h1)
    wait(pe, gains_in, *bank[7].free)
    wait(dve, PE.mark(pe.transpose(bank[7].t[:, 0:4 * KC], gain_rows[:], ident[0:4 * KC, 0:4 * KC])))
    gains_ok = DV.mark(dve.tensor_copy(gains[:, 1:4, :].rearrange("p n c -> p (n c)"), bank[7].t[:, KC:4 * KC]))
    bank[7].free = (gains_ok,)
    wait(act, gains_ok)
    wait(pe, xm_in, *bank[7].free)
    for c in range(KC):
        tr = pe.transpose(bank[7].t[:, c * META:(c + 1) * META], xm[:, c * P:(c + 1) * P], ident[0:META, 0:META])
    wait(dve, PE.mark(tr))
    t = DV.mark(dve.tensor_tensor(meta_t[:], bank[7].t[:, 0:KC * META].rearrange("p (c n) -> p c n", c=KC),
                                  gains[:, 0, :].unsqueeze(2).broadcast_to([P, KC, META]), ALU.mult))
    bank[7].free = (t,)
    wait(act, t, t_zero)
    wait(dve, t_zero)
    wait(dve, AC.mark(act.activation(meta_stack[:, :, 0:META], meta_t[:], ACT.Copy)))
    meta_ready = DV.mark(dve.tensor_tensor(meta_stack[:, :, 32:32 + META], meta_t[:], meta_stack[:, :, 0:META],
                                           ALU.subtract))
    slabs["vb"].prepare()
    qb_ok = rope_tiles(MM[0], 2, True, qn, t_qb)
    wait(pe, meta_ready)
    t_kb = slabs["kb"].multiply(h_hi, h_lo, per_tile(MM[1]), meta=(meta_stack, bank[4]))
    slabs["kva"].prepare()
    kb_ok = rope_tiles(MM[1], 3, False, kb, t_kb)
    m = add_meta(t_kb, WIDE, bank[4])
    wait(act, m, one_ok)
    _, kbm_ok = norm_and_rope([msum[:]], 8, [rgm[:, 3]], [one_scale[:]], False, (m,), [[by_head(kbm[:])]])
    t_vb = slabs["vb"].multiply(h_hi, h_lo, per_tile(MM[0]), meta=(meta_stack, bank[7]))
    qT_ok = turn_heads(qn, qT, 4, (qb_ok,), bank[5:7])
    wait(act, t_vb)
    wait(dve, t_vb)
    v0 = AC.mark(act.activation(vb[:, 0, :], MM[0][0].t[:], ACT.Copy, scale=row_scale[:, 0, 0:1]))
    v1 = DV.mark(dve.tensor_scalar(vb[:, 1, :], MM[0][1].t[:], row_scale[:, 0, 1:2], None, ALU.mult))
    MM[0][0].free, MM[0][1].free = (v0,), (v1,)
    m = add_meta(t_vb, WIDE, bank[7], (kbm_ok,))
    wait(dve, m)
    vb_ok = (v0, DV.mark(dve.tensor_copy(vbm[:], msum[:])))

    t_kva = slabs["kva"].multiply(h_hi, h_lo, per_tile(MM[1]), meta=(meta_stack, bank[4]))
    kbT_ok = turn_heads(kb, kbT, 4, (kb_ok, kbm_ok), bank[5:7], metas=kbm)
    slabs["qa"].prepare()
    wait(pe, *qT_ok, *kbT_ok)
    exp_b = {}
    for n in range(8 * TILES):
        h, t = n // TILES, n % TILES
        exp_b[t, h] = scores(t, h, kbT, h // 2, 0, bank[5 + n % 3], ())
    b_scored = Mark(PE, PE.n)
    t_qa = slabs["qa"].multiply(h_hi, h_lo, per_tile(MM[0]))
    m = add_meta(t_kva, 2 * kw, bank[4], vb_ok)
    wait(act, t_kva)
    for t in range(TILES):
        va_ok = AC.mark(act.activation(va[:, t, :], MM[1][t].t[:, kw:2 * kw], ACT.Copy, scale=row_scale[:, 0, t:t + 1]))
    dups = [v.rearrange("p (h two d) -> p two h d", two=2, d=HD) for v in (ka[:, 0, :], ka[:, 1, :], kam[:])]
    read, ka_ok = norm_and_rope([b.t[:, 0:kw] for b in MM[1]], A_KV, [rg[:, t, 1] for t in range(TILES)],
                                [row_scale[:, 0, t:t + 1] for t in range(TILES)], False, (t_kva,),
                                [[d[:, 0], d[:, 1]] for d in dups[0:2]])
    for t in range(TILES):
        MM[1][t].free = (read[t], va_ok)
    wait(dve, m)
    vam_ok = DV.mark(dve.tensor_copy(vam[:], msum[:, kw:2 * kw]))
    wait(act, m)
    _, kam_ok = norm_and_rope([msum[:, 0:kw]], A_KV, [rgm[:, 1]], [one_scale[:]], False, (m,),
                              [[dups[2][:, 0], dups[2][:, 1]]])
    wait(dve, exp_b[1, 7], lam_ok)
    t = DV.mark(dve.reciprocal(rden[:, 0], den[:, 0]))
    wait(dve, t)
    rd = rden[:, 0].rearrange("p t (h j) -> p t h j", j=2)
    t = DV.mark(dve.tensor_scalar(rd[:, :, :, 1], rd[:, :, :, 1], lam[:, 1:2], None, ALU.mult))
    wait(dve, t)
    w_b = {}
    for h in range(B_HEADS):
        for t in range(TILES):
            e0, e1 = maps[:, t, 2 * h, :], maps[:, t, 2 * h + 1, :]
            u = DV.mark(dve.tensor_scalar(e1, e1, rden[:, 0, t, 2 * h + 1:2 * h + 2], None, ALU.mult))
            wait(dve, u)
            w_b[t, h] = DV.mark(dve.scalar_tensor_tensor(e0, e0, rden[:, 0, t, 2 * h:2 * h + 1], e1,
                                                         ALU.mult, ALU.add))

    mixed = tmp
    b_turned, pv_b, b_ready, b_root = {}, {}, {}, {}
    b_sums = (bank[7], bank[4], bank[2], bank[3])
    b_ss = sb("b_square_sums", [P, 2 * B_HEADS], c=one)
    wait(act, r1_ok)
    wait(dve, r1_ok)

    def turn_b(h):
        b_ready[h], b_turned[h] = turn_map(2 * h, h % 2, (w_b[0, h], w_b[1, h]), bank[5 + h % 2], b_sums[h], by_act=True)

    def attend_b(h):
        buf, ob = h % 2, b_sums[h]
        done = weights_times_values(buf, (*b_ready[h], *vb_ok), ob, vb, vbm, slice(h * B_V, (h + 1) * B_V))
        col = A_HEADS * HD + h * B_V
        wait(act, done)
        ss = b_ss[:, 2 * h:2 * h + 2]
        for t in range(TILES):
            u = AC.mark(act.activation(mixed[:, t, col:col + B_V], ob.t[:, t * B_V:(t + 1) * B_V], ACT.Square,
                                       accum_out=ss[:, t:t + 1]))
        wait(pool, u, half_ok)
        u = PO.mark(pool.tensor_scalar(ss, ss, 1.0 / B_V, EPS, ALU.mult, ALU.add))
        wait(pool, u)
        b_root[h] = PO.mark(pool.tensor_tensor(ss, ss, half_neg[:, 0:TILES], ALU.pow))

    def scale_b(h):
        ob, col, ss = b_sums[h], A_HEADS * HD + h * B_V, b_ss[:, 2 * h:2 * h + 2]
        wait(act, b_root[h])
        for t in range(TILES):
            pv_b[t, h] = AC.mark(act.activation(mixed[:, t, col:col + B_V], ob.t[:, t * B_V:(t + 1) * B_V],
                                                ACT.Copy, scale=ss[:, t:t + 1]))
        ob.free = (pv_b[1, h],)

    turn_b(0)
    turn_b(1)
    attend_b(0)
    turn_b(2)
    qa_ok = rope_tiles(MM[0], 0, True, qn, t_qa, (qT_ok[0], qT_ok[1]))
    attend_b(1)
    turn_b(3)
    scale_b(0)
    scale_b(1)
    attend_b(2)
    attend_b(3)
    scale_b(2)
    scale_b(3)
    qT_ok = turn_heads(qn, qT, 4, (qa_ok,), bank[5:7], free=(b_scored,))
    kaT_ok = turn_heads(ka, kaT, 2, (ka_ok, kam_ok), bank[5:7], metas=kam)

    wait(pe, *qT_ok, *kaT_ok)
    exp_a, a_ready = {}, {}

    def score_a(h):
        for t in range(TILES):
            exp_a[t, h] = scores(t, h, kaT, h // 4, 1, bank[(2 * h + t) % 4], (b_turned[h // 2], w_b[t, h // 2]))

    def turn_a(h):
        a_ready[h], _ = turn_map(h, h % 2, (exp_a[0, h], exp_a[1, h]), bank[4 + h % 2], bank[6 + h % 2])

    for h in range(2):
        score_a(h)
    turn_a(0)
    for h in range(A_HEADS):
        slabs[f"out{h // 4}"].prepare((h % 4,))
        if h + 2 < A_HEADS:
            score_a(h + 2)
        if h + 1 < A_HEADS:
            turn_a(h + 1)
        kv, ob = h // (A_HEADS // A_KV), bank[6 + h % 2]
        done = weights_times_values(h % 2, (*a_ready[h], va_ok, vam_ok), ob, va, vam, slice(kv * HD, (kv + 1) * HD))
        wait(dve, exp_a[0, h], exp_a[1, h])
        r = DV.mark(dve.reciprocal(rden[:, 1, :, h], den[:, 1, :, h]))
        wait(dve, r, done)
        for t in range(TILES):
            pv_a = DV.mark(dve.tensor_scalar(mixed[:, t, h * HD:(h + 1) * HD], ob.t[:, t * HD:(t + 1) * HD],
                                             rden[:, 1, t, h:h + 1], None, ALU.mult))
        ob.free = (pv_a,)

    m_ok = turn_and_cut(mixed, RIGHT, lambda c: subln[:], [(pv_b[0, 3],), (pv_b[1, 3],)], bank[4:6],
                        free=(t_qa, subln_ok))
    m_ok.update(turn_and_cut(mixed, LEFT, None, [(pv_a,), ()], bank[0:2]))
    t_o0 = slabs["out0"].multiply(h_hi, h_lo, per_tile(MM[1]), x_ready=m_ok)

    def add_residual(pair, half, dones):
        oks = []
        for t in range(TILES):
            cols = slice(half * WIDE, (half + 1) * WIDE)
            wait(dve, dones[t])
            oks.append(DV.mark(dve.tensor_tensor(x[:, t, cols], x[:, t, cols], pair[t].t[:], ALU.add)))
            pair[t].free = (oks[t],)
        return oks

    x_left = add_residual(MM[1], 0, (t_o0, t_o0))
    one.close()

    ffn_rows = sb("ffn_rows", [P, TILES, WIDE])
    f_hi = sb("ffn_hi", [P, 4, SEQ], F32R)
    f_lo = sb("ffn_lo", [P, 4, SEQ], F32R)
    f_line = {n: Line(nc, ctx, n) for n in ("ffn_up", "ffn_acted", "ffn_hidden", "ffn_turned", "ffn_hi_done",
                                            "ffn_lo_done")}

    def feed_forward(steps, up_pieces, down_piece, chunks, squared, x_ready, scale, up_at, last_at, after):
        down_at = 4 - up_at
        acc = [bank[4:6], bank[6:8]]
        L, n_hid = f_line, chunks * P
        state = {"rows_free": (), "cut_free": (), "cut": None}

        def fill_up(i):
            for s in range(4):
                ring.fill(up_at + s, up_pieces(i, s))

        def fill_down(i, first_slot=down_at):
            for c in range(chunks):
                ring.fill(first_slot + c, [(lambda raw: raw, down_piece(i, c))])

        def down(first, last):
            if first:
                wait(pe, *(m for t in acc for b in t for m in b.free))
            for c in range(chunks):
                s = down_at + c
                wait(pe, ring.ready[s], state["cut"][c // 2])
                mm = three_passes(pe, f_hi, f_lo, ring.hi[:, s, :], ring.lo[:, s, :], c, acc, WIDE,
                                  first and c == 0, last and c == chunks - 1)
                done = ring.done(s, mm)
            state["cut_free"] = (done,)
            return done

        def turn_hidden():
            wait(pe, state["hidden"])
            state["cut"] = []
            for c0 in range(0, chunks, 2):
                b = bank[2 + c0 // 2]
                wait(pe, *b.free)
                for c in range(2):
                    for t in range(TILES):
                        tr = pe.transpose(b.t[:, c * SEQ + t * P:c * SEQ + (t + 1) * P],
                                          ffn_rows[:, t, (c0 + c) * P:(c0 + c + 1) * P], ident[:])
                turned = L["ffn_turned"].mark(tr)
                pair = b.t[:].rearrange("p (c n) -> p c n", c=2)
                wait(act, turned, *state["cut_free"])
                rounded = L["ffn_hi_done"].mark(act.activation(f_hi[:, c0:c0 + 2, :], pair, ACT.Copy))
                wait(dve, rounded)
                cut = L["ffn_lo_done"].mark(dve.tensor_tensor(f_lo[:, c0:c0 + 2, :], pair, f_hi[:, c0:c0 + 2, :],
                                                              ALU.subtract))
                b.free = (cut,)
                state["cut"].append(cut)
            state["rows_free"] = (turned,)

        def step(i, n, last=False):
            up_banks = bank[6:8] if n == 0 else bank[0:2]
            wait(pe, *(m for b in up_banks for m in b.free))
            for s in range(4):
                wait(pe, ring.ready[up_at + s])
                for c in range(2):
                    kc = 2 * s + c
                    if n == 0:
                        wait(pe, x_ready[kc])
                    w = slice(c * WIDE, (c + 1) * WIDE)
                    mm = three_passes(pe, h_hi, h_lo, ring.hi[:, up_at + s, w], ring.lo[:, up_at + s, w], kc,
                                      per_tile(up_banks), WIDE, kc == 0, kc == KC - 1)
                up_done = ring.done(up_at + s, mm)
                if n == 1 and s == 1:
                    turn_hidden()
            if n > 0:
                fill_down(i - 1)
                down(first=(n == 1), last=False)
            if last:
                fill_down(i, last_at)
            else:
                fill_up(i + 1)
            for t in range(TILES):
                b, rows = up_banks[t], ffn_rows[:, t, 0:n_hid]
                wait(act, up_done, *state["rows_free"])
                if squared:
                    acted = L["ffn_acted"].mark(act.activation(rows, b.t[:], ACT.Relu, scale=scale[:, t:t + 1]))
                    b.free = (acted,)
                    wait(pool, acted)
                    state["hidden"] = L["ffn_hidden"].mark(pool.tensor_tensor(rows, rows, rows, ALU.mult))
                else:
                    acted = L["ffn_acted"].mark(act.activation(rows, b.t[:, 0:n_hid], ACT.Silu,
                                                               scale=scale[:, t:t + 1]))
                    wait(dve, acted)
                    hidden = L["ffn_hidden"].mark(dve.scalar_tensor_tensor(rows, b.t[:, n_hid:2 * n_hid],
                                                                           scale[:, t:t + 1], rows, ALU.mult,
                                                                           ALU.mult))
                    b.free = (hidden,)
                    state["hidden"] = hidden
            if n > 0:
                turn_hidden()

        more = run_steps(nc, step, steps)
        held = [m for f in (*ring.free, *ring.raw_free, state["rows_free"], state["cut_free"], (state["hidden"],)) for m in f]
        held += [m for b in bank[0:4] for m in b.free] + list(ring.ready) + state["cut"]
        for m in {id(m): m for m in held if m is not None}.values():
            if m.n > m.line.loop_start:
                m.n += m.line.stride * more
        step(steps - 1, steps - 1, last=True)
        after()
        done = [[None, None], [None, None]]
        for h in range(2):
            for t in range(TILES):
                for c in range(chunks):
                    s = last_at + c
                    wait(pe, ring.ready[s], state["cut"][c // 2])
                    cols = slice(h * WIDE, (h + 1) * WIDE)
                    for n, (xx, w) in enumerate(((f_hi, ring.hi), (f_hi, ring.lo), (f_lo, ring.hi))):
                        mm = pe.matmul(acc[t][h].t[:], xx[:, c, t * P:(t + 1) * P], w[:, s, cols],
                                       start=False, stop=c == chunks - 1 and n == 2)
                done[t][h] = ring.used.mark(mm)
        for c in range(chunks):
            ring.release(last_at + c, done[1][1])
        return done

    def up_slab1(i, s):
        n = D_FF // 11
        out = []
        for w, name in enumerate(("w_gate", "w_up")):
            src = a[name][0][2 * s * P:(2 * s + 2) * P, bass.ds(i * n, n)].rearrange("(c p) n -> p c n", p=P)
            out.append((lambda raw, w=w: raw.rearrange("p (c w n) -> p c w n", c=2, w=2)[:, :, w, :], src))
        return out

    def first_up(pieces, up_at):
        for s in range(4):
            ring.fill(up_at + s, pieces(0, s))

    first_up(up_slab1, 0)
    t_o1 = slabs["out1"].multiply_by_bank(h_hi, h_lo, per_tile(MM[0]))
    x_right = add_residual(MM[0], 1, (t_o1[0][0], t_o1[1][0]))
    t_o1 = t_o1[1][0]

    bg = [sb(f"b_gate{h}", [P, D]) for h in range(2)]
    two = ctx.enter_context(ExitStack())
    ln = sb("ln_v", [P, 2, GMLP], c=two)
    mask = sb("mask", [P, 4, SEQ], c=two)
    rope2 = sb("rope2", [P, TILES, 2, ROPE2], c=two)
    pT2 = sb("pT2", [P, 2, NG * 2, P], c=two)
    wsp = pT2[:, 0, 0:GROUPS, :]
    wspT = sb("w_spatial_T", [P, GROUPS, P], c=two)
    bsp = sb("b_spatial", [P, GROUPS], c=two)
    wait(pool, t_o1)
    for dst, src in [(bg[h][:], a["b_gate_2"][0:1, h * D:(h + 1) * D].broadcast_to([P, D])) for h in range(2)] + [
            (ln[:, 0, :], a["ln_v_gain_2"][0:1, :].broadcast_to([P, GMLP])),
            (ln[:, 1, :], a["ln_v_bias_2"][0:1, :].broadcast_to([P, GMLP])),
            (mask[:], a["mask"]), (rope2[:], a["rope2"].rearrange("(t p) k d -> p t k d", p=P)),
            (wsp, a["w_spatial_2"][0].rearrange("g t s -> t g s")),
            (bsp[:], a["b_spatial_2"][0].rearrange("g t -> t g"))]:
        two_in = consts.mark(pool.dma_start(dst, src, allow_slow_non_contiguous=True), 16)

    h2 = turn_and_cut(x, LEFT, lambda c: gains[:, 1, c:c + 1], [(m,) for m in x_left], bank[4:6], free=(t_o1,))
    h2.update(turn_and_cut(x, RIGHT, lambda c: gains[:, 1, c:c + 1], [(m,) for m in x_right], bank[6:8]))
    r2_ok = norm_scale(1, [(m,) for m in x_right])

    win2 = a["w_in_2"][0]
    base = {"z": 0, "q": 2 * GMLP}
    base["k"] = base["q"] + NG * WIDE
    base["v"] = base["k"] + NG * WIDE
    base["g"] = base["v"] + NG * WIDE
    order2 = [("z", 1), ("z", 0)] + [(c, g) for g in range(NG) for c in "qkv"] + [("g", 0), ("g", 1), ("a", 0),
                                                                                  ("g", 2), ("g", 3), ("b", 0), ("o", 0), ("o", 1)]
    plan = []
    for n, (kind, j) in enumerate(order2):
        if kind in "ab":
            src, chunks, cols = a["w_branch_a_2" if kind == "a" else "w_branch_b_2"][0], 4, D
        elif kind == "o":
            src, chunks, cols = a["w_out_2"][0][:, j * WIDE:(j + 1) * WIDE], KC, WIDE
        else:
            c0 = base[kind] + j * WIDE
            src, chunks, cols = win2[:, c0:c0 + WIDE], KC, WIDE
        plan.append(Slab(ring, src, 4 * (n % 2), chunks, cols))
    at = {key: n for n, key in enumerate(order2)}

    wait(act, r2_ok)
    wait(dve, r2_ok)
    ff1 = feed_forward(11, up_slab1, lambda i, c: a["w_down"][0][bass.ds((2 * i + c) * P, P), :], 2, False, h2,
                       row_scale[:, 1, :], 0, 6, plan[0].prepare)

    used_up = ff1[1][1]
    x_left = add_residual([bank[4], bank[6]], 0, [ff1[t][0] for t in range(TILES)])
    x_right = add_residual([bank[5], bank[7]], 1, [ff1[t][1] for t in range(TILES)])

    h_free = (used_up,)
    h3 = turn_and_cut(x, LEFT, lambda c: gains[:, 2, c:c + 1], [(m,) for m in x_left], bank[0:2], free=h_free)
    h3.update(turn_and_cut(x, RIGHT, lambda c: gains[:, 2, c:c + 1], [(m,) for m in x_right], bank[2:4]))
    r3_ok = norm_scale(2, [(m,) for m in x_right])
    r3 = [row_scale[:, 2, t:t + 1] for t in range(TILES)]

    qk = {c: sb(f"{c}2_rows", [P, TILES, WIDE], c=two) for c in "qk"}
    u_rows = sb("u_rows", [P, TILES, GMLP], c=two)
    q2T = {c: sb(f"{c}2T", [P, HEADS2, SEQ], c=two) for c in "qk"}
    v2 = sb("v2", [P, NG, TILES, WIDE], c=two)
    sc = sb("scores2", [P, TILES, HEADS2, NG * SEQ], c=two)
    rot = sb("rope2_part", [P, 2, HEADS2, ROPE2], c=two)
    bn = sb("bn", [P, TILES, 8], c=two)
    gmax = sb("pattern_max2", [P, NG, TILES, HEADS2], c=two)
    gmax_ok = [None] * TILES
    smax = sb("smax2", [P, 3, TILES, HEADS2], c=two)

    def product(key, outs, ready=None, by_bank=False):
        n = at[key]
        if n + 1 < len(plan):
            plan[n + 1].prepare()
        x_hi, x_lo = (f_hi, f_lo) if key[0] in "ab" else (h_hi, h_lo)
        if by_bank:
            return plan[n].multiply_by_bank(x_hi, x_lo, outs, x_ready=ready)
        return plan[n].multiply(x_hi, x_lo, outs, x_ready=ready)

    pair_of = lambda key: MM[at[key] % 2]

    key = ("z", 1)
    done = product(key, per_tile(pair_of(key)), ready=h3)
    v_rows = ffn_rows
    wait(act, done, r3_ok)
    wait(dve, r3_ok)
    v_ok = []
    for t in range(TILES):
        b = pair_of(key)[t]
        g = AC.mark(act.activation(v_rows[:, t, :], b.t[:], ACT.Gelu_apprx_tanh, scale=r3[t]))
        b.free = (g,)
        wait(dve, g)
        s = DV.mark(dve.bn_stats(bn[:, t, 0:6], v_rows[:, t, :]))
        wait(dve, s)
        s = DV.mark(dve.bn_aggr(bn[:, t, 6:8], bn[:, t, 0:6]))
        wait(dve, s)
        s = inverse_root(bn[:, t, 7:8], 1.0, EPS)
        wait(dve, s)
        s = DV.mark(dve.tensor_scalar(v_rows[:, t, :], v_rows[:, t, :], bn[:, t, 6:7], bn[:, t, 7:8],
                                      ALU.subtract, ALU.mult))
        wait(pool, s, two_in)
        s = PO.mark(pool.tensor_tensor(v_rows[:, t, :], v_rows[:, t, :], ln[:, 0, :], ALU.mult))
        wait(pool, s)
        v_ok.append(PO.mark(pool.tensor_tensor(v_rows[:, t, :], v_rows[:, t, :], ln[:, 1, :], ALU.add)))
    wait(pe, two_in, *bank[4].free)
    for g in range(GROUPS):
        tr = pe.transpose(bank[4].t[:, g * P:(g + 1) * P], wsp[:, g, :], ident[:])
    wait(act, PE.mark(tr))
    wspT_ok = AC.mark(act.activation(wspT[:], bank[4].t[:].rearrange("p (g n) -> p g n", g=GROUPS), ACT.Copy))
    bank[4].free = (wspT_ok,)

    key = ("z", 0)
    done = product(key, per_tile(pair_of(key)))
    wait(act, done)
    for t in range(TILES):
        b = pair_of(key)[t]
        u_ok = AC.mark(act.activation(u_rows[:, t, :], b.t[:], ACT.Gelu_apprx_tanh, scale=r3[t]))
        b.free = (u_ok,)

    def spatial():
        wait(pe, *v_ok, wspT_ok)
        wait(dve, u_ok, two_in)
        for t in range(TILES):
            b = bank[4 + t]
            wait(pe, *b.free)
            for g in range(GROUPS):
                mm = pe.matmul(b.t[:, g * P:(g + 1) * P], wspT[:, g, :], v_rows[:, t, g * P:(g + 1) * P],
                               start=True, stop=True)
            wait(dve, PE.mark(mm))
            for g in range(GROUPS):
                cols = slice(g * P, (g + 1) * P)
                ok = DV.mark(dve.scalar_tensor_tensor(u_rows[:, t, cols], b.t[:, cols], bsp[:, g:g + 1],
                                                      u_rows[:, t, cols], ALU.add, ALU.mult))
            b.free = (ok,)
        return ok

    qk_free = {"q": (), "k": ()}
    T_free = ()
    s_ok = {}

    def take_rows(kind, g, done):
        pair, rows = pair_of((kind, g)), qk[kind]
        for t in range(TILES):
            wait(act, done, *qk_free[kind])
            c = AC.mark(act.activation(rows[:, t, :], pair[t].t[:], ACT.Copy, scale=r3[t]))
            pair[t].free = (c,)
            wait(dve, c, two_in)
            r = rows[:, t, :].rearrange("p (h d) -> p h d", d=HD2)
            half = ROPE2 // 2
            tab = lambda k, lo_, hi_: rope2[:, t, k, lo_:hi_].unsqueeze(1).broadcast_to([P, HEADS2, hi_ - lo_])
            dve.tensor_tensor(rot[:, 0], r[:, :, 0:ROPE2], tab(0, 0, ROPE2), ALU.mult)
            dve.tensor_tensor(rot[:, 1, :, 0:half], r[:, :, half:ROPE2], tab(1, 0, half), ALU.mult)
            s = DV.mark(dve.tensor_tensor(rot[:, 1, :, half:ROPE2], r[:, :, 0:half], tab(1, half, ROPE2), ALU.mult))
            wait(dve, s)
            ok = DV.mark(dve.tensor_tensor(r[:, :, 0:ROPE2], rot[:, 0], rot[:, 1], ALU.add))
            wait(dve, ok)
        return ok

    def turn2(kind, ok, banks):
        m = turn_heads(qk[kind], q2T[kind], HEADS2, (ok,), banks, free=T_free)
        qk_free[kind] = (Mark(PE, PE.n),)
        return m

    def raw_scores(g, qT_ok, kT_ok):
        wait(pe, *qT_ok, *kT_ok)
        for h in range(HEADS2):
            b = bank[4 + h % 2]
            wait(pe, *b.free)
            for t in range(TILES):
                mm = pe.matmul(b.t[:, t * SEQ:(t + 1) * SEQ], q2T["q"][:, h, t * P:(t + 1) * P], q2T["k"][:, h, :],
                               start=True, stop=True)
            scored = PE.mark(mm)
            wait(dve, scored)
            for t in range(TILES):
                m = mask[:, t if g == 0 else 1 + g, :]
                s_ok[g, h] = DV.mark(dve.scalar_tensor_tensor(sc[:, t, h, g * SEQ:(g + 1) * SEQ],
                                                              b.t[:, t * SEQ:(t + 1) * SEQ], HD2 ** -0.5, m,
                                                              ALU.mult, ALU.add))
            b.free = (s_ok[g, h],)
        wait(dve, s_ok[g, HEADS2 - 1])
        for t in range(TILES):
            gmax_ok[t] = DV.mark(dve.tensor_reduce(gmax[:, g, t, :], sc[:, t, :, g * SEQ:(g + 1) * SEQ], AX, ALU.max,
                                                   negate=True))
        return scored

    for g in range(NG):
        key = ("q", g)
        done = product(key, per_tile(pair_of(key)))
        if g > 0:
            T_free = (raw_scores(g - 1, qT_ok, kT_ok),)
        q_ok = take_rows("q", g, done)
        if g == 0:
            ya_ok = spatial()
        key = ("k", g)
        done = product(key, per_tile(pair_of(key)))
        qT_ok = turn2("q", q_ok, bank[6:8])
        k_ok = take_rows("k", g, done)
        if g == 0:
            ya_cut = turn_and_cut(u_rows, LEFT, None, [(ya_ok,), ()], bank[4:6], out_hi=f_hi, out_lo=f_lo)
        key = ("v", g)
        done = product(key, per_tile(pair_of(key)))
        pair = pair_of(key)
        wait(act, done)
        wait(dve, done)
        v0 = AC.mark(act.activation(v2[:, g, 0, :], pair[0].t[:], ACT.Copy, scale=r3[0]))
        v1 = DV.mark(dve.tensor_scalar(v2[:, g, 1, :], pair[1].t[:], r3[1], None, ALU.mult))
        pair[0].free, pair[1].free = (v0,), (v1,)
        kT_ok = turn2("k", k_ok, bank[6:8])
    done_g0 = product(("g", 0), per_tile(pair_of(("g", 0))))
    raw_scores(NG - 1, qT_ok, kT_ok)
    v_all = (v0, v1)

    e2 = {}
    for t in range(TILES):
        wait(dve, gmax_ok[t])
        m = DV.mark(dve.tensor_tensor(smax[:, 0, t, :], gmax[:, 0, t, :], gmax[:, 1, t, :], ALU.min))
        wait(dve, m)
        m = DV.mark(dve.tensor_tensor(smax[:, 0, t, :], smax[:, 0, t, :], gmax[:, 2, t, :], ALU.min))
        wait(act, m)
        for h in range(HEADS2):
            e2[t, h] = AC.mark(act.activation(sc[:, t, h, :], sc[:, t, h, :], ACT.Exp, bias=smax[:, 0, t, h:h + 1],
                                              accum_out=smax[:, 1, t, h:h + 1]))
        wait(dve, e2[t, HEADS2 - 1])
        rs_ok = DV.mark(dve.reciprocal(smax[:, 2, t, :], smax[:, 1, t, :]))

    yb = qk["q"]
    pT2_free = [(), ()]
    yb_ok = None

    def turn2_map(n):
        t, h, buf = n // HEADS2, n % HEADS2, n % 2
        wait(pe, e2[t, h])
        cps = []
        for j in range(2):
            b = bank[4 + 2 * buf + j]
            wait(pe, *b.free)
            for c in range(3):
                kc = 3 * j + c
                tr = pe.transpose(b.t[:, c * P:(c + 1) * P], sc[:, t, h, kc * P:(kc + 1) * P], ident[:])
            done = PE.mark(tr)
            dst, src = pT2[:, buf, 3 * j:3 * j + 3, :], b.t[:, 0:3 * P].rearrange("p (c n) -> p c n", c=3)
            if j == 0:
                wait(act, done, *pT2_free[buf])
                cps.append(AC.mark(act.activation(dst, src, ACT.Copy)))
            else:
                wait(dve, done, *pT2_free[buf])
                cps.append(DV.mark(dve.tensor_copy(dst, src)))
            b.free = (cps[-1],)
        return cps

    def attend2(n, cps):
        t, h, buf = n // HEADS2, n % HEADS2, n % 2
        ob = bank[n % 4]
        sums = ob.t[:, 0:P]
        wait(pe, *cps, *v_all, *ob.free)
        for kc in range(2 * NG):
            mm = pe.matmul(sums, pT2[:, buf, kc, :], v2[:, kc // 2, kc % 2, h * HD2:(h + 1) * HD2],
                           start=(kc == 0), stop=(kc == 2 * NG - 1))
        done = PE.mark(mm)
        pT2_free[buf] = (done,)
        wait(dve, done, rs_ok)
        ok = DV.mark(dve.tensor_scalar(yb[:, t, h * HD2:(h + 1) * HD2], sums, smax[:, 2, t, h:h + 1], None, ALU.mult))
        ob.free = (ok,)
        return ok, done

    def gates(j, dst, done, free=()):
        pair = pair_of(("g", j))
        cols = slice((j % 2) * WIDE, (j % 2 + 1) * WIDE)
        for t in range(TILES):
            wait(dve, done, two_in, *free)
            s = DV.mark(dve.scalar_tensor_tensor(dst[:, t, cols], pair[t].t[:], r3[t], bg[j // 2][:, cols],
                                                 ALU.mult, ALU.add))
            pair[t].free = (s,)
            wait(act, s)
            ok = AC.mark(act.activation(dst[:, t, cols], dst[:, t, cols], ACT.Sigmoid))
        return ok

    done_g1 = product(("g", 1), per_tile(pair_of(("g", 1))))
    g_a = tmp
    gates(0, g_a, done_g0, free=(r3_ok,))
    ga_ok = gates(1, g_a, done_g1)
    cps = turn2_map(0)
    for n in range(TILES * HEADS2):
        ahead = turn2_map(n + 1) if n + 1 < TILES * HEADS2 else None
        yb_ok, last_pv = attend2(n, cps)
        cps = ahead

    outs = [bank[0:2], bank[2:4]]
    done = product(("a", 0), outs, ready=ya_cut)
    for t in range(TILES):
        for half in range(2):
            cols, b = slice(half * WIDE, (half + 1) * WIDE), outs[t][half]
            wait(dve, done, ga_ok)
            m_ok = DV.mark(dve.tensor_tensor(tmp[:, t, cols], tmp[:, t, cols], b.t[:], ALU.mult))
            b.free = (m_ok,)
    yb_cut = turn_and_cut(yb, LEFT, None, [(yb_ok,), ()], bank[4:6], out_hi=f_hi, out_lo=f_lo, free=(done,))
    g_b = sc[:].rearrange("p t h n -> p (t h n)")[:, 0:TILES * D].rearrange("p (t n) -> p t n", t=TILES)
    for j in (2, 3):
        done = product(("g", j), per_tile(pair_of(("g", j))))
        gb_ok = gates(j, g_b, done, free=(last_pv,))
    h_read = done
    done = product(("b", 0), outs, ready=yb_cut, by_bank=True)
    m_half = []
    for half in range(2):
        for t in range(TILES):
            cols, b = slice(half * WIDE, (half + 1) * WIDE), outs[t][half]
            wait(dve, done[t][half], gb_ok, m_ok)
            s = DV.mark(dve.tensor_tensor(g_b[:, t, cols], g_b[:, t, cols], b.t[:], ALU.mult))
            b.free = (s,)
            wait(dve, s)
            s = DV.mark(dve.tensor_tensor(tmp[:, t, cols], tmp[:, t, cols], g_b[:, t, cols], ALU.add))
            m_half.append((s,))
    merged = turn_and_cut(tmp, LEFT, None, m_half[0:2], bank[4:6], free=(h_read,))
    merged.update(turn_and_cut(tmp, RIGHT, None, m_half[2:4], bank[6:8]))
    wait(pool, ga_ok)
    post_in = post_load[0].mark(pool.dma_start(bg[0][:], a["norm_mix_post_2"][0:1, :].broadcast_to([P, D])), 16)
    wait(pool, gb_ok)
    post2_in = post_load[1].mark(pool.dma_start(bg[1][:], a["norm_mlp_post_2"][0:1, :].broadcast_to([P, D])), 16)
    two.close()

    def up_slab2(i, s):
        src = a["w_up_2"][0][2 * s * P:(2 * s + 2) * P, bass.ds(i * WIDE, WIDE)].rearrange("(c p) n -> p c n", p=P)
        return [(lambda raw: raw.rearrange("p (c n) -> p c n", c=2), src)]

    m0, m1 = ("o", 0), ("o", 1)
    done0 = product(m0, per_tile(pair_of(m0)), ready=merged)
    first_up(up_slab2, 4)
    done1 = product(m1, per_tile(pair_of(m1)), by_bank=True)

    def post_norm(banks_of, dones, gain, gain_in, free):
        for t in range(TILES):
            ss = stat[:, 4 + 2 * t:6 + 2 * t]
            wait(act, *free)
            for half in range(2):
                wait(act, dones[t][half])
                cols = slice(half * WIDE, (half + 1) * WIDE)
                u = AC.mark(act.activation(tmp[:, t, cols], banks_of[t][half].t[:], ACT.Square,
                                           accum_out=ss[:, half:half + 1]))
            wait(dve, u)
            u = DV.mark(dve.tensor_tensor(ss[:, 0:1], ss[:, 0:1], ss[:, 1:2], ALU.add))
            wait(dve, u)
            u = inverse_root(ss[:, 0:1], 1.0 / D, EPS)
            wait(dve, u, gain_in)
            for half in range(2):
                cols, b = slice(half * WIDE, (half + 1) * WIDE), banks_of[t][half]
                u = DV.mark(dve.scalar_tensor_tensor(tmp[:, t, cols], b.t[:], ss[:, 0:1], gain[:, cols],
                                                     ALU.mult, ALU.mult))
                b.free = (u,)
            wait(dve, u)
            yield DV.mark(dve.tensor_tensor(x[:, t, :], x[:, t, :], tmp[:, t, :], ALU.add))

    mix_banks = [[pair_of(m0)[t], pair_of(m1)[t]] for t in range(TILES)]
    x_marks = list(post_norm(mix_banks, [(done0, done1[t][0]) for t in range(TILES)], bg[0], post_in,
                             tuple(merged.values())))
    done1 = done1[1][0]
    h4 = turn_and_cut(x, ALL, lambda c: gains[:, 3, c:c + 1], [(m,) for m in x_marks], bank[4:8], free=(done1,))
    r4_ok = norm_scale(3, [(m,) for m in x_marks])
    wait(act, r4_ok)
    wait(dve, r4_ok)
    ff2 = feed_forward(8, up_slab2, lambda i, c: a["w_down_2"][0][bass.ds((4 * i + c) * P, P), :], 4, True, h4,
                       row_scale[:, 3, :], 4, 4, lambda: None)

    acc_banks = [bank[4:6], bank[6:8]]
    stored = [Line(nc, ctx, f"stored{t}") for t in range(TILES)]
    for t, ok in enumerate(post_norm(acc_banks, ff2, bg[1], post2_in, ())):
        wait(sp, ok)
        stored[t].mark(sp.dma_start(out[0, t * P:(t + 1) * P, :], x[:, t, :]), 16)
    wait(sp, *[Mark(line, line.n) for line in stored])


_INS = ["x", "meta_tokens", "attn_norm_g", "w_in", "a_q_norm_g", "a_k_norm_g", "b_q_norm_g", "b_k_norm_g",
        "b_lambda_q1", "b_lambda_k1", "b_lambda_q2", "b_lambda_k2", "b_subln_g", "w_out", "ffn_norm_g", "w_gate",
        "w_up", "w_down", "norm_mix_pre_2", "w_in_2", "b_gate_2", "ln_v_gain_2", "ln_v_bias_2", "w_spatial_2",
        "b_spatial_2", "w_branch_a_2", "w_branch_b_2", "w_out_2", "norm_mix_post_2", "norm_mlp_pre_2", "w_up_2",
        "w_down_2", "norm_mlp_post_2"]


def kernel(**inputs):
    import concourse.bacc as _bacc
    from concourse.bass_utils import run_bass_kernel_spmd as _run

    nc = _bacc.Bacc("TRN2", target_bir_lowering=False, num_devices=1)
    arrays = {name: np.ascontiguousarray(inputs[name]) for name in _INS}
    one, two = rope_tables()
    arrays.update(rope1=one, rope2=two, mask=masks(), ident=np.eye(P, dtype=np.float32))
    args = {n: nc.dram_tensor(f"in_{n}", v.shape, mybir.dt.from_np(v.dtype), kind="ExternalInput").ap()
            for n, v in arrays.items()}
    out = nc.dram_tensor("out_0", (1, SEQ, D), F32, kind="ExternalOutput").ap()
    program(nc, args, out)
    r = _run(nc, [{f"in_{n}": v for n, v in arrays.items()}], core_ids=[0])
    return r.results[0]["out_0"]
```

```python
import math
from contextlib import ExitStack

import numpy as np

import concourse.bass as bass
from concourse import mybir

F32 = mybir.dt.float32
F32R = mybir.dt.float32r
ALU = mybir.AluOpType
ACT = mybir.ActivationFunctionType
AX = mybir.AxisListType.X

P = 128
D = 1024
SEQ = 256
META = 16
TILES = SEQ // P
KC = D // P
KEYS = SEQ + META
EPS = 1e-6
WIDE = 512

HD = 64
A_HEADS, A_KV = 8, 2
B_HEADS, B_V = 4, 128
LAM_INIT = 0.8 - 0.6 * math.exp(-0.3 * 0)
D_FF = -(-8 * D // (3 * 256)) * 256

GMLP = 512
GROUPS = 4
PATTERNS = ((128, 1), (512, 4), (2048, 16))
NG = len(PATTERNS)
HD2 = 128
HEADS2 = 4
ROPE2 = HD2 // 4
D_FF2 = 4 * D
MASKED = -1e30

SLOTS = 8
RAW_SLOTS = 4
SLOT = 1024


def rope_tables():
    f = np.float32
    half = HD // 2
    inv_a = (f(10000.0) ** (-np.arange(0, half, 2, dtype=f) / f(half))).astype(f)
    t = np.arange(SEQ)
    ang_a = np.zeros((KEYS, half), f)
    ang_a[:SEQ] = np.concatenate([(t // 64).astype(f)[:, None] * inv_a, (t % 64).astype(f)[:, None] * inv_a], 1)
    inv_b = (f(10000.0) ** (-np.arange(0, HD, 2, dtype=f) / f(HD))).astype(f)
    pos = np.concatenate([META + t, np.arange(META)]).astype(f)
    ang_b = pos[:, None] * inv_b
    one = np.zeros((KEYS, 4, HD), f)
    for n, ang in ((0, ang_a), (2, ang_b)):
        one[:, n, :] = np.repeat(np.cos(ang), 2, axis=1)
        one[:, n + 1, 0::2] = -np.sin(ang)
        one[:, n + 1, 1::2] = np.sin(ang)
    inv_2 = (f(500000.0) ** (-np.arange(0, ROPE2, 2, dtype=f) / f(ROPE2))).astype(f)
    ang_2 = t.astype(f)[:, None] * inv_2
    two = np.zeros((SEQ, 2, ROPE2), f)
    two[:, 0, :] = np.concatenate([np.cos(ang_2), np.cos(ang_2)], 1)
    two[:, 1, :] = np.concatenate([-np.sin(ang_2), np.sin(ang_2)], 1)
    return one, two


def masks():
    q, k = np.arange(SEQ)[:, None], np.arange(SEQ)[None, :]
    out = np.full((SEQ, NG, SEQ), MASKED, np.float32)
    for g, (window, dilation) in enumerate(PATTERNS):
        seen = ((q - k) % dilation == 0) & (np.abs(q // dilation - k // dilation) <= window // (2 * dilation))
        out[:, g, :][seen] = 0.0
    return np.stack([out[0:P, 0], out[P:SEQ, 0], out[0:P, 1], out[0:P, 2]], axis=1)


class Mark:

    def __init__(self, line, n):
        self.line, self.n = line, n


class Line:

    every = []
    seen = {}
    rounds = None
    floor = {}

    def __init__(self, nc, ctx, name):
        self.sem = ctx.enter_context(nc.semaphore(name))
        self.name, self.n, self.stride = name, 0, 0
        Line.every.append(self)

    def mark(self, ins, by=1):
        ins.then_inc(self.sem, by)
        self.n += by
        return Mark(self, self.n)


def wait(eng, *marks):
    latest = {}
    for m in marks:
        latest[m.line] = max(latest.get(m.line, 0), m.n)
    for line, n in latest.items():
        if Line.rounds is None:
            seen = Line.seen.setdefault(eng.engine, {})
            if seen.get(line, 0) < n:
                eng.wait_ge(line.sem, n)
                seen[line] = n
        else:
            assert n > Line.floor[line], f"{line.name}: a mark from before the round ahead of the loop"
            eng.wait_ge(line.sem, Line.rounds * line.stride + n)


def run_steps(nc, step, n_steps, peeled_last=1):
    step(0, 0)
    step(1, 1)
    before = {line: line.n for line in Line.every}
    step(2, 2)
    for line in Line.every:
        line.stride = line.n - before[line]
    last = n_steps - peeled_last
    start = {line: line.n for line in Line.every}
    for line in Line.every:
        line.loop_start = line.n
    with nc.Fori(0, last - 3) as i:
        Line.rounds, Line.floor = i, before
        step(i + 3, 3)
        Line.rounds = None
    more = last - 4
    for line in Line.every:
        assert line.n - start[line] == line.stride, (line.name, line.n - start[line], line.stride)
        line.n += line.stride * more
    return more


class Bank:

    def __init__(self, nc, ctx, name):
        self.t = ctx.enter_context(nc.psum_tensor(name, [P, WIDE], F32))
        self.free = ()


class Ring:

    def __init__(self, nc, ctx):
        self.nc = nc
        self.raw = ctx.enter_context(nc.sbuf_tensor("w_raw", [P, RAW_SLOTS, SLOT], F32))
        self.hi = ctx.enter_context(nc.sbuf_tensor("w_hi", [P, SLOTS, SLOT], F32R))
        self.lo = ctx.enter_context(nc.sbuf_tensor("w_lo", [P, SLOTS, SLOT], F32R))
        self.loaded = [Line(nc, ctx, f"w_loaded{r}") for r in range(RAW_SLOTS)]
        self.rounded = Line(nc, ctx, "w_hi_done")
        self.cut = Line(nc, ctx, "w_lo_done")
        self.cut_by_pool = Line(nc, ctx, "w_lo_done_by_pool")
        self.used = Line(nc, ctx, "w_used")
        self.held = [False] * SLOTS
        self.raw_free = [() for _ in range(RAW_SLOTS)]
        self.ready = [None] * SLOTS
        self.free = [() for _ in range(SLOTS)]

    def fill(self, s, pieces, n=SLOT, by_pool=False):
        nc, r = self.nc, s % RAW_SLOTS
        assert not self.held[s], "the slot's weights are still to be multiplied"
        self.held[s] = True
        raw = self.raw[:, r, :]
        wait(nc.sync, *self.raw_free[r])
        for view, src in pieces:
            full = self.loaded[r].mark(nc.sync.dma_start(view(raw), src), 16)
        wait(nc.scalar, full, *self.free[s])
        rounded = self.rounded.mark(nc.scalar.activation(self.hi[:, s, 0:n], raw[:, 0:n], ACT.Copy))
        eng, line = (nc.gpsimd, self.cut_by_pool) if by_pool else (nc.vector, self.cut)
        wait(eng, rounded)
        self.ready[s] = line.mark(eng.tensor_tensor(self.lo[:, s, 0:n], raw[:, 0:n], self.hi[:, s, 0:n],
                                                    ALU.subtract))
        self.raw_free[r] = (self.ready[s],)

    def release(self, s, last_matmul):
        self.held[s] = False
        self.free[s] = (last_matmul,)

    def done(self, s, ins):
        self.release(s, self.used.mark(ins))
        return self.free[s][0]


class Slab:

    def __init__(self, ring, src, first, chunks, cols):
        self.ring, self.src, self.first, self.chunks, self.cols = ring, src, first, chunks, cols
        self.per = SLOT // max(cols, WIDE)
        self.n_slots = chunks // self.per

    def view(self, slot):
        return slot[:, 0:self.per * self.cols].rearrange("p (c n) -> p c n", c=self.per)

    def prepare(self, part=None, by_pool=False):
        for j in part or range(self.n_slots):
            rows = self.src[j * self.per * P:(j + 1) * self.per * P, :].rearrange("(c p) n -> p c n", p=P)
            self.ring.fill(self.first + j, [(self.view, rows)], self.per * self.cols, by_pool)

    def multiply(self, x_hi, x_lo, outs, x_ready=None, meta=None, midway=None):
        ring, pe = self.ring, self.ring.nc.tensor
        width = min(self.cols, WIDE)
        for t in outs:
            for b in t:
                wait(pe, *b.free)
        if meta:
            wait(pe, *meta[1].free)
        for j in range(self.n_slots):
            s = self.first + j
            wait(pe, ring.ready[s])
            w_hi, w_lo = self.view(ring.hi[:, s, :]), self.view(ring.lo[:, s, :])
            for c in range(self.per):
                kc = j * self.per + c
                if x_ready:
                    wait(pe, x_ready[kc])
                first, last = kc == 0, kc == self.chunks - 1
                mm = three_passes(pe, x_hi, x_lo, w_hi[:, c, :], w_lo[:, c, :], kc, outs, width, first, last)
            if meta:
                wait(pe, *meta[2])
                for c in range(self.per):
                    kc = j * self.per + c
                    for n, w in enumerate((w_hi, w_lo)):
                        mm = pe.matmul(meta[1].t[:, 0:width], meta[0][:, kc, :], w[:, c, 0:width],
                                       start=kc == 0 and n == 0, stop=kc == self.chunks - 1 and n == 1)
            done = ring.done(s, mm)
            if midway and j == self.n_slots // 2 - 1:
                midway()
        return done

    def multiply_by_bank(self, x_hi, x_lo, outs, x_ready=None):
        ring, pe = self.ring, self.ring.nc.tensor
        places = [(self.first + kc // self.per, kc % self.per, kc) for kc in range(self.chunks)]
        done = [[None] * len(t) for t in outs]
        for h in range(len(outs[0])):
            for t in range(TILES):
                b = outs[t][h]
                wait(pe, *b.free)
                for s, c, kc in places:
                    wait(pe, ring.ready[s])
                    if x_ready:
                        wait(pe, x_ready[kc])
                    w_hi, w_lo = self.view(ring.hi[:, s, :])[:, c, :], self.view(ring.lo[:, s, :])[:, c, :]
                    for n, (x, w) in enumerate(((x_hi, w_hi), (x_hi, w_lo), (x_lo, w_hi))):
                        mm = pe.matmul(b.t[:], x[:, kc, t * P:(t + 1) * P], w[:, h * WIDE:(h + 1) * WIDE],
                                       start=kc == 0 and n == 0, stop=kc == self.chunks - 1 and n == 2)
                done[t][h] = ring.used.mark(mm)
        for j in range(self.n_slots):
            ring.release(self.first + j, done[-1][-1])
        return done


def three_passes(pe, x_hi, x_lo, w_hi, w_lo, kc, outs, width, first, last):
    for t in range(TILES):
        for n, (x, w) in enumerate(((x_hi, w_hi), (x_hi, w_lo), (x_lo, w_hi))):
            for h, b in enumerate(outs[t]):
                mm = pe.matmul(b.t[:, 0:width], x[:, kc, t * P:(t + 1) * P], w[:, h * width:(h + 1) * width],
                               start=first and n == 0, stop=last and n == 2)
    return mm


def program(nc, a, out):
    with ExitStack() as ctx:
        Line.every, Line.seen = [], {}
        build(nc, ctx, a, out)


def build(nc, ctx, a, out):
    pe, act, dve, pool, sp = nc.tensor, nc.scalar, nc.vector, nc.gpsimd, nc.sync

    def sb(name, shape, dt=F32, c=ctx):
        return c.enter_context(nc.sbuf_tensor(name, shape, dt))

    PE, AC, DV, PO = (Line(nc, ctx, n) for n in ("tensor_done", "scalar_done", "vector_done", "pool_done"))
    bank = [Bank(nc, ctx, f"bank{n}") for n in range(8)]
    MM = [bank[0:2], bank[2:4]]
    ring = Ring(nc, ctx)

    def per_tile(pair):
        return [[pair[0]], [pair[1]]]

    x_line, x_in = [Line(nc, ctx, f"x{t}_loaded") for t in range(TILES)], []
    ident_load, gain_load, rest_load, meta_load = (Line(nc, ctx, n) for n in (
        "identity_loaded", "first_gain_loaded", "other_gains_loaded", "meta_loaded"))
    small = Line(nc, ctx, "small_loaded")
    post_load = [Line(nc, ctx, f"post_gain{n}_loaded") for n in range(2)]
    consts = Line(nc, ctx, "block2_loaded")
    x = sb("x", [P, TILES, D])
    tmp = sb("tmp", [P, TILES, D])
    ident = sb("ident", [P, P])
    gains = sb("gains", [P, 4, KC])
    stat = sb("stat", [P, 32])
    half_neg = sb("minus_half", [P, 2 * 8])
    row_scale = sb("row_scale", [P, 4, TILES])
    gain_rows = sb("gain_rows", [4 * KC, P])
    h_hi = sb("h_hi", [P, KC, SEQ], F32R)
    h_lo = sb("h_lo", [P, KC, SEQ], F32R)

    one = ctx.enter_context(ExitStack())
    xm = sb("xm", [META, D], c=one)
    for t in range(TILES):
        x_in.append(x_line[t].mark(sp.dma_start(x[:, t, :], a["x"][0, t * P:(t + 1) * P, :]), 16))
    ident_in = ident_load.mark(act.dma_start(ident[:], a["ident"]), 16)
    for n, name in enumerate(("attn_norm_g", "ffn_norm_g", "norm_mix_pre_2", "norm_mlp_pre_2")):
        rows = act.dma_start(gain_rows[n * KC:(n + 1) * KC, :], a[name][0].rearrange("(c p) -> c p", p=P))
        if n == 0:
            gain_in = gain_load.mark(rows, 16)
        else:
            gains_in = rest_load.mark(rows, 16)
    xm_in = meta_load.mark(act.dma_start(xm[:], a["meta_tokens"]), 16)

    cuts = (("qa", A_HEADS * HD), ("kva", 2 * A_KV * HD), ("qb", 2 * B_HEADS * HD), ("kb", 2 * B_HEADS * HD),
            ("vb", B_HEADS * B_V))
    spans, o = {}, 0
    for name, n in cuts:
        spans[name] = (o, o + n)
        o += n
    slabs = {}
    for n, name in enumerate(("qb", "kb", "vb", "kva", "qa")):
        c0, c1 = spans[name]
        slabs[name] = Slab(ring, a["w_in"][0][:, c0:c1], 4 * (n % 2), KC, c1 - c0)
    for h in range(2):
        slabs[f"out{h}"] = Slab(ring, a["w_out"][0][:, h * WIDE:(h + 1) * WIDE], 4 * h, KC, WIDE)

    rope1 = sb("rope1", [P, TILES, 4, HD], c=one)
    rope1m = sb("rope1m", [META, 4, HD], c=one)
    hg = sb("head_gains", [P, 4, HD], c=one)
    lamv = sb("lam_vectors", [P, 4, HD], c=one)
    subln = sb("subln", [P, 1], c=one)
    meta_stack = sb("meta_stack", [P, KC, P], F32R, c=one)
    half_ok = PO.mark(pool.memset(half_neg[:], -0.5))
    t_zero = PO.mark(pool.memset(meta_stack[:].bitcast(F32), 0.0))
    pool.dma_start(rope1[:], a["rope1"][0:SEQ].rearrange("(t p) k d -> p t k d", p=P)).then_inc(small.sem, 16)
    pool.dma_start(rope1m[:], a["rope1"][SEQ:KEYS]).then_inc(small.sem, 16)
    for n, name in enumerate(("a_q_norm_g", "a_k_norm_g", "b_q_norm_g", "b_k_norm_g")):
        pool.dma_start(hg[:, n, :], a[name][0:1, :].broadcast_to([P, HD])).then_inc(small.sem, 16)
    for n, name in enumerate(("b_lambda_q1", "b_lambda_k1", "b_lambda_q2", "b_lambda_k2")):
        pool.dma_start(lamv[:, n, :], a[name][0:1, :].broadcast_to([P, HD])).then_inc(small.sem, 16)
    small.n += 10 * 16
    small_in = small.mark(pool.dma_start(subln[:], a["b_subln_g"][0].rearrange("(p o) -> p o", o=1),
                                         allow_slow_non_contiguous=True), 16)

    def inverse_root(v, scale, bias):
        rows, n = v.shape[0], v.shape[1]
        t = DV.mark(dve.tensor_scalar(v, v, scale, bias, ALU.mult, ALU.add))
        wait(pool, t, half_ok)
        return PO.mark(pool.tensor_tensor(v, v, half_neg[0:rows, 0:n], ALU.pow))

    def norm_scale(n, ready):
        for t in range(TILES):
            wait(act, *ready[t])
            m = AC.mark(act.activation(tmp[:, t, :], x[:, t, :], ACT.Square, accum_out=row_scale[:, n, t:t + 1]))
        wait(dve, m)
        return inverse_root(row_scale[:, n, :], 1.0 / D, EPS)

    def turn_and_cut(src, chunks, gain, ready, banks, out_hi=h_hi, out_lo=h_lo, free=(), at=0):
        marks = {}
        pairs = [chunks[n:n + 2] for n in range(0, len(chunks), 2)]
        for n0 in range(0, len(pairs), len(banks)):
            group = list(zip(pairs[n0:n0 + len(banks)], banks))
            turned = {}
            for t in range(TILES):
                wait(pe, *ready[t])
                for pair, b in group:
                    if t == 0:
                        wait(pe, *b.free)
                    for j, c in enumerate(pair):
                        tr = pe.transpose(b.t[:, j * SEQ + t * P:j * SEQ + (t + 1) * P], src[:, t, c * P:(c + 1) * P],
                                          ident[:])
                    turned[b] = PE.mark(tr)
            for pair, b in group:
                wait(act, turned[b], *free)
                if gain is None:
                    d = slice(pair[0] + at, pair[1] + at + 1)
                    both = b.t[:].rearrange("p (c n) -> p c n", c=2)
                    wait(dve, AC.mark(act.activation(out_hi[:, d, :], both, ACT.Copy)))
                    t_lo = DV.mark(dve.tensor_tensor(out_lo[:, d, :], both, out_hi[:, d, :], ALU.subtract))
                    marks[pair[0] + at] = marks[pair[1] + at] = t_lo
                else:
                    for j, c in enumerate(pair):
                        rounded = AC.mark(act.activation(out_hi[:, c + at, :], b.t[:, j * SEQ:(j + 1) * SEQ],
                                                         ACT.Copy, scale=gain(c)))
                    wait(dve, rounded)
                    for j, c in enumerate(pair):
                        t_lo = DV.mark(dve.scalar_tensor_tensor(out_lo[:, c + at, :], b.t[:, j * SEQ:(j + 1) * SEQ],
                                                                gain(c), out_hi[:, c + at, :], ALU.mult, ALU.subtract))
                        marks[c + at] = t_lo
                b.free = (t_lo,)
        return marks

    ALL, LEFT, RIGHT = range(KC), range(KC // 2), range(KC // 2, KC)

    meta_t = sb("meta_t", [P, KC, META], c=one)
    wait(act, DV.mark(dve.memset(stat[:, 0:1], 0.0)))
    act.activation(stat[:, 1:2], stat[:, 0:1], ACT.Copy)
    wait(pe, ident_in, gain_in)
    wait(dve, PE.mark(pe.transpose(bank[7].t[:, 0:KC], gain_rows[0:KC, :], ident[0:KC, 0:KC])))
    gain_ok = DV.mark(dve.tensor_copy(gains[:, 0, :], bank[7].t[:, 0:KC]))
    bank[7].free = (gain_ok,)
    wait(act, gain_ok)
    first_gain = lambda c: gains[:, 0, c:c + 1]
    h1 = turn_and_cut(x, range(0, 2), first_gain, [(m,) for m in x_in], bank[3:4])
    slabs["qb"].prepare((0,))
    h1.update(turn_and_cut(x, range(2, 4), first_gain, [(m,) for m in x_in], bank[4:5]))
    slabs["qb"].prepare((1,))
    h1.update(turn_and_cut(x, RIGHT, first_gain, [(m,) for m in x_in], bank[5:7]))
    slabs["qb"].prepare((2, 3))
    xn = sb("head_normed", [P, 2, WIDE], c=one)
    xm_sq = xn[0:META].rearrange("p a b -> p (a b)")
    r_meta = sb("row_scale_meta", [META, 1], c=one)
    wait(act, xm_in)
    wait(dve, AC.mark(act.activation(xm_sq, xm[:], ACT.Square, accum_out=r_meta[:])))
    rm_ok = inverse_root(r_meta[:], 1.0 / D, EPS)
    r1_ok = norm_scale(0, [(m,) for m in x_in])

    lamp = sb("lam_products", [P, 2, HD], c=one)
    lam = sb("lam", [P, 4], c=one)
    lv = lamv[:].rearrange("p (j s) d -> p j s d", s=2)
    wait(dve, small_in)
    t = DV.mark(dve.tensor_tensor(lamp[:], lv[:, :, 0, :], lv[:, :, 1, :], ALU.mult))
    wait(dve, t)
    t = DV.mark(dve.tensor_reduce(lam[:, 0:2], lamp[:], AX, ALU.add))
    wait(act, t)
    t = AC.mark(act.activation(lam[:, 2:4], lam[:, 0:2], ACT.Exp))
    wait(dve, t)
    t = DV.mark(dve.tensor_tensor(lam[:, 0:1], lam[:, 3:4], lam[:, 2:3], ALU.subtract))
    wait(dve, t)
    lam_ok = DV.mark(dve.tensor_scalar(lam[:, 1:2], lam[:, 0:1], -LAM_INIT, None, ALU.add))
    subln_ok = DV.mark(dve.tensor_scalar(subln[:], subln[:], 1.0 - LAM_INIT, None, ALU.mult))

    rg = sb("rope_gain", [P, TILES, 4, 2, HD], c=one)
    rgm = sb("rope_gain_meta", [META, 4, 2, HD], c=one)
    wait(pool, small_in)
    for kind in range(4):
        base = 2 * (kind // 2)
        for dst, tab, g in [(rg[:, t, kind], rope1[:, t], hg[:, kind, :]) for t in range(TILES)] + \
                [(rgm[:, kind], rope1m[:], hg[0:META, kind, :])]:
            pool.tensor_tensor(dst[:, 0, :], tab[:, base, :], g, ALU.mult)
            for e in range(2):
                rg_done = PO.mark(pool.tensor_tensor(dst[:, 1, e::2], tab[:, base + 1, e::2], g[:, 1 - e::2],
                                                     ALU.mult))

    part = sb("rope_part", [P, 2, WIDE], c=one)
    mcopy, msum = xm[:, 0:WIDE], xm[:, WIDE:2 * WIDE]
    xn_free = []

    def by_head(v):
        return v.rearrange("p (h d) -> p h d", d=HD)

    def norm_and_rope(srcs, heads, tables, scales, is_q, ready, dsts, meanwhile=None):
        rows, n, count = srcs[0].shape[0], heads * HD, len(srcs)
        ss = stat[0:rows, 8:8 + count * heads]
        ss_of = [ss[:, i * heads:(i + 1) * heads] for i in range(count)]
        x_t = [xn[0:rows, i, 0:n] for i in range(count)]
        p_t = [part[0:rows, i, 0:n] for i in range(count)]
        wait(act, *ready, *xn_free)
        for i in range(count):
            m = AC.mark(act.activation(x_t[i], srcs[i], ACT.Square, scale=scales[i]))
            wait(dve, m)
            m = DV.mark(dve.tensor_reduce(ss_of[i], by_head(x_t[i]), AX, ALU.add))
        wait(dve, m)
        m = inverse_root(ss, 1.0, HD * EPS) if is_q else inverse_root(ss, 1.0 / HD, EPS)
        if meanwhile:
            meanwhile()
        wait(dve, m)
        for i in range(count):
            m = DV.mark(dve.tensor_scalar(ss_of[i], ss_of[i], scales[i], None, ALU.mult))
        wait(dve, m)
        read = []
        for i in range(count):
            read.append(DV.mark(dve.tensor_tensor(by_head(x_t[i]), by_head(srcs[i]),
                                                  ss_of[i].unsqueeze(2).broadcast_to([rows, heads, HD]), ALU.mult)))
        swapped, turned = [], []
        for i in range(count):
            eng, line = (pool, PO) if i == 0 and count > 1 else (dve, DV)
            wait(eng, read[i], rg_done, *xn_free)
            for e in range(2):
                m = line.mark(eng.tensor_tensor(by_head(p_t[i])[:, :, e::2], by_head(x_t[i])[:, :, 1 - e::2],
                                                tables[i][:, 1, e::2].unsqueeze(1).broadcast_to([rows, heads, HD // 2]),
                                                ALU.mult))
            swapped.append(m)
        for i in reversed(range(count)):
            wait(dve, swapped[i])
            m = DV.mark(dve.tensor_tensor(by_head(x_t[i]), by_head(x_t[i]),
                                          tables[i][:, 0, :].unsqueeze(1).broadcast_to([rows, heads, HD]), ALU.mult))
            wait(dve, m)
            for d in dsts[i]:
                done = DV.mark(dve.tensor_tensor(d, by_head(x_t[i]), by_head(p_t[i]), ALU.add))
        xn_free[:] = [done]
        return read, done

    qn = sb("q_rows", [P, TILES, WIDE], c=one)
    kb = sb("kb", [P, TILES, WIDE], c=one)
    kbm = sb("kb_meta", [META, WIDE], c=one)
    vb = sb("vb", [P, TILES, WIDE], c=one)
    vbm = sb("vb_meta", [META, WIDE], c=one)
    kw = A_KV * HD
    ka = sb("ka", [P, TILES, 2 * kw], c=one)
    kam = sb("ka_meta", [META, 2 * kw], c=one)
    va = sb("va", [P, TILES, kw], c=one)
    vam = sb("va_meta", [META, kw], c=one)

    def add_meta(done, n, b, free=()):
        wait(act, done, rm_ok, *free)
        wait(dve, AC.mark(act.activation(mcopy[:, 0:n], b.t[32:32 + META, 0:n], ACT.Copy, scale=r_meta[:])))
        t = DV.mark(dve.scalar_tensor_tensor(msum[:, 0:n], b.t[0:META, 0:n], r_meta[:], mcopy[:, 0:n],
                                             ALU.mult, ALU.add))
        b.free = (t,)
        return t

    def rope_tiles(pair, kind, is_q, dst, done, free=(), meanwhile=None):
        wait(dve, *free)
        wait(act, r1_ok)
        read, ok = norm_and_rope([b.t[:] for b in pair], 8, [rg[:, t, kind] for t in range(TILES)],
                                 [row_scale[:, 0, t:t + 1] for t in range(TILES)], is_q, (done,),
                                 [[by_head(dst[:, t, :])] for t in range(TILES)], meanwhile)
        for t in range(TILES):
            pair[t].free = (read[t],)
        return ok

    one_scale = sb("one_scale", [META, 1], c=one)
    one_ok = PO.mark(pool.memset(one_scale[:], 1.0))

    qT = sb("qT1", [P, 4, SEQ], F32R, c=one)
    kbT = sb("kbT", [P, 4, KEYS], F32R, c=one)
    kaT = sb("kaT", [P, 2, KEYS], F32R, c=one)
    qT_lo = sb("qT1_lo", [P, 4, SEQ], F32R, c=one)
    kT_lo = sb("kT1_lo", [P, 4, KEYS], F32R, c=one)

    def turn_heads(src, hi, lo, chunks, ready, banks, free=(), metas=None):
        wait(pe, *ready)
        pairs, marks = [], []
        for n, c0 in enumerate(range(0, chunks, 2)):
            wait(pe, *banks[n].free)
            for c in range(2):
                for t in range(TILES):
                    tr = pe.transpose(banks[n].t[:, c * SEQ + t * P:c * SEQ + (t + 1) * P],
                                      src[:, t, (c0 + c) * P:(c0 + c + 1) * P], ident[:])
            pairs.append((banks[n], banks[n].t[:].rearrange("p (c n) -> p c n", c=2), slice(c0, c0 + 2),
                          slice(0, SEQ), PE.mark(tr)))
        if metas is not None:
            b = banks[-1]
            wait(pe, *b.free)
            for c in range(chunks):
                tr = pe.transpose(b.t[:, c * META:(c + 1) * META], metas[:, c * P:(c + 1) * P], ident[0:META, 0:META])
            pairs.append((b, b.t[:, 0:chunks * META].rearrange("p (c n) -> p c n", c=chunks), slice(0, chunks),
                          slice(SEQ, KEYS), PE.mark(tr)))
        for b, turned, c, n, done in pairs:
            wait(act, done, *free)
            rounded = AC.mark(act.activation(hi[:, c, n], turned, ACT.Copy))
            wait(dve, rounded, *free)
            b.free = (DV.mark(dve.tensor_tensor(lo[:, c, n], turned, hi[:, c, n], ALU.subtract)),)
            marks.append(b.free[0])
        return marks

    maps = sb("maps1", [P, TILES, 8, KEYS], c=one)
    den = sb("den1", [P, 2, TILES, 8], c=one)
    nmax = sb("nmax1", [P, 2, TILES, 8], c=one)
    rden = sb("rden1", [P, 2, TILES, 8], c=one)

    def scores(t, h, q, k, k_chunk, which, b, free):
        p0 = HD * (h % 2)
        wait(pe, *b.free)
        for n, (x, y) in enumerate(((q[0], k[0]), (q[0], k[1]), (q[1], k[0]))):
            mm = pe.matmul(b.t[:, 0:KEYS], x[p0:p0 + HD, h // 2, t * P:(t + 1) * P], y[p0:p0 + HD, k_chunk, :],
                           start=n == 0, stop=n == 2)
        wait(dve, PE.mark(mm))
        m = DV.mark(dve.tensor_reduce(nmax[:, which, t, h:h + 1], b.t[:, 0:KEYS], AX, ALU.max, negate=True))
        wait(act, m, *free)
        e = AC.mark(act.activation(maps[:, t, h, :], b.t[:, 0:KEYS], ACT.Exp, bias=nmax[:, which, t, h:h + 1],
                                   accum_out=den[:, which, t, h:h + 1]))
        b.free = (e,)
        return e

    pT = sb("pT", [P, 2, 2, SEQ], c=one)
    pTm = sb("pTm", [META, 2, SEQ], c=one)
    pT_free = [(), ()]

    def turn_map(h, buf, ready, b, ob, by_act=False):
        wait(pe, *ready, *b.free, *ob.free)
        for t in range(TILES):
            for c in range(2):
                pe.transpose(b.t[:, c * SEQ + t * P:c * SEQ + (t + 1) * P], maps[:, t, h, c * P:(c + 1) * P], ident[:])
            tr = pe.transpose(ob.t[0:META, SEQ + t * P:SEQ + (t + 1) * P], maps[:, t, h, SEQ:KEYS], ident[:])
        done = PE.mark(tr)
        wait(act, done, *pT_free[buf])
        m1 = AC.mark(act.activation(pT[:, buf], b.t[:].rearrange("p (c n) -> p c n", c=2), ACT.Copy))
        if by_act:
            m2 = AC.mark(act.activation(pTm[:, buf, :], ob.t[0:META, SEQ:2 * SEQ], ACT.Copy))
        else:
            wait(dve, done, *pT_free[buf])
            m2 = DV.mark(dve.tensor_copy(pTm[:, buf, :], ob.t[0:META, SEQ:2 * SEQ]))
        b.free, ob.free = (m1,), (m2,)
        return (m1, m2), done

    def weights_times_values(buf, ready, ob, v, vm, cols):
        n = cols.stop - cols.start
        wait(pe, *ready)
        for t in range(TILES):
            for c in range(2):
                pe.matmul(ob.t[:, t * n:(t + 1) * n], pT[:, buf, c, t * P:(t + 1) * P], v[:, c, cols],
                          start=(c == 0), stop=False)
            mm = pe.matmul(ob.t[:, t * n:(t + 1) * n], pTm[:, buf, t * P:(t + 1) * P], vm[:, cols],
                           start=False, stop=True)
        done = PE.mark(mm)
        pT_free[buf] = (done,)
        return done

    slabs["kb"].prepare()
    meta_ready = []

    def gains_and_meta():
        wait(pe, gains_in, *bank[7].free)
        wait(dve, PE.mark(pe.transpose(bank[7].t[:, 0:4 * KC], gain_rows[:], ident[0:4 * KC, 0:4 * KC])))
        gains_ok = DV.mark(dve.tensor_copy(gains[:, 1:4, :].rearrange("p n c -> p (n c)"), bank[7].t[:, KC:4 * KC]))
        bank[7].free = (gains_ok,)
        wait(act, gains_ok)
        wait(pe, xm_in, *bank[5].free)
        for c in range(KC):
            tr = pe.transpose(bank[5].t[:, c * META:(c + 1) * META], xm[:, c * P:(c + 1) * P], ident[0:META, 0:META])
        wait(dve, PE.mark(tr))
        t = DV.mark(dve.tensor_tensor(meta_t[:], bank[5].t[:, 0:KC * META].rearrange("p (c n) -> p c n", c=KC),
                                      gains[:, 0, :].unsqueeze(2).broadcast_to([P, KC, META]), ALU.mult))
        bank[5].free = (t,)
        wait(act, t, t_zero)
        wait(dve, t_zero)
        wait(dve, AC.mark(act.activation(meta_stack[:, :, 0:META], meta_t[:], ACT.Copy)))
        ready = DV.mark(dve.tensor_tensor(meta_stack[:, :, 32:32 + META], meta_t[:], meta_stack[:, :, 0:META],
                                               ALU.subtract))
        meta_ready.append(ready)

    t_qb = slabs["qb"].multiply(h_hi, h_lo, per_tile(MM[0]), x_ready=h1, midway=gains_and_meta)
    slabs["vb"].prepare()
    qb_ok = rope_tiles(MM[0], 2, True, qn, t_qb)
    t_kb = slabs["kb"].multiply(h_hi, h_lo, per_tile(MM[1]), meta=(meta_stack, bank[4], meta_ready))
    slabs["kva"].prepare()
    kb_ok = rope_tiles(MM[1], 3, False, kb, t_kb)
    m = add_meta(t_kb, WIDE, bank[4])
    wait(act, m, one_ok)
    _, kbm_ok = norm_and_rope([msum[:]], 8, [rgm[:, 3]], [one_scale[:]], False, (m,), [[by_head(kbm[:])]])
    t_vb = slabs["vb"].multiply(h_hi, h_lo, per_tile(MM[0]), meta=(meta_stack, bank[7], meta_ready))
    slabs["qa"].prepare(by_pool=True)
    qT_ok = turn_heads(qn, qT, qT_lo, 4, (qb_ok,), bank[5:7])
    wait(act, t_vb)
    wait(dve, t_vb)
    v0 = AC.mark(act.activation(vb[:, 0, :], MM[0][0].t[:], ACT.Copy, scale=row_scale[:, 0, 0:1]))
    v1 = DV.mark(dve.tensor_scalar(vb[:, 1, :], MM[0][1].t[:], row_scale[:, 0, 1:2], None, ALU.mult))
    MM[0][0].free, MM[0][1].free = (v0,), (v1,)
    m = add_meta(t_vb, WIDE, bank[7], (kbm_ok,))
    wait(dve, m)
    vb_ok = (v0, DV.mark(dve.tensor_copy(vbm[:], msum[:])))

    t_kva = slabs["kva"].multiply(h_hi, h_lo, per_tile(MM[1]), meta=(meta_stack, bank[4], meta_ready))
    kbT_ok = turn_heads(kb, kbT, kT_lo, 4, (kb_ok, kbm_ok), bank[5:8], metas=kbm)
    wait(pe, kbT_ok[2])
    exp_b = {}
    for n in range(8 * TILES):
        h, t = n // TILES, n % TILES
        wait(pe, qT_ok[h // 4], kbT_ok[h // 4])
        exp_b[t, h] = scores(t, h, (qT, qT_lo), (kbT, kT_lo), h // 2, 0, (bank[5], bank[6], bank[7], bank[0], bank[1])[n % 5], ())
    b_scored = Mark(PE, PE.n)
    t_qa = slabs["qa"].multiply(h_hi, h_lo, per_tile(MM[0]))
    m = add_meta(t_kva, 2 * kw, bank[4], vb_ok)
    wait(act, t_kva)
    for t in range(TILES):
        va_ok = AC.mark(act.activation(va[:, t, :], MM[1][t].t[:, kw:2 * kw], ACT.Copy, scale=row_scale[:, 0, t:t + 1]))
    dups = [v.rearrange("p (h two d) -> p two h d", two=2, d=HD) for v in (ka[:, 0, :], ka[:, 1, :], kam[:])]
    read, ka_ok = norm_and_rope([b.t[:, 0:kw] for b in MM[1]], A_KV, [rg[:, t, 1] for t in range(TILES)],
                                [row_scale[:, 0, t:t + 1] for t in range(TILES)], False, (t_kva,),
                                [[d[:, 0], d[:, 1]] for d in dups[0:2]])
    for t in range(TILES):
        MM[1][t].free = (read[t], va_ok)
    wait(dve, m)
    vam_ok = DV.mark(dve.tensor_copy(vam[:], msum[:, kw:2 * kw]))
    wait(act, m)
    _, kam_ok = norm_and_rope([msum[:, 0:kw]], A_KV, [rgm[:, 1]], [one_scale[:]], False, (m,),
                              [[dups[2][:, 0], dups[2][:, 1]]])
    wait(dve, exp_b[1, 7], lam_ok)
    t = DV.mark(dve.reciprocal(rden[:, 0], den[:, 0]))
    wait(dve, t)
    rd = rden[:, 0].rearrange("p t (h j) -> p t h j", j=2)
    t = DV.mark(dve.tensor_scalar(rd[:, :, :, 1], rd[:, :, :, 1], lam[:, 1:2], None, ALU.mult))
    wait(dve, t)
    w_b = {}

    def weights_b(h):
        for t in range(TILES):
            e0, e1 = maps[:, t, 2 * h, :], maps[:, t, 2 * h + 1, :]
            u = DV.mark(dve.tensor_scalar(e1, e1, rden[:, 0, t, 2 * h + 1:2 * h + 2], None, ALU.mult))
            wait(dve, u)
            w_b[t, h] = DV.mark(dve.scalar_tensor_tensor(e0, e0, rden[:, 0, t, 2 * h:2 * h + 1], e1,
                                                         ALU.mult, ALU.add))

    def last_weights_b():
        weights_b(2)
        weights_b(3)

    weights_b(0)
    weights_b(1)
    qa_ok = rope_tiles(MM[0], 0, True, qn, t_qa, (qT_ok[0], qT_ok[1]), meanwhile=last_weights_b)

    mixed = tmp
    b_turned, pv_b, b_ready, b_root = {}, {}, {}, {}
    b_sums = (bank[7], bank[4], bank[2], bank[3])
    b_ss = sb("b_square_sums", [P, 2 * B_HEADS], c=one)
    wait(act, r1_ok)
    wait(dve, r1_ok)

    def turn_b(h):
        b_ready[h], b_turned[h] = turn_map(2 * h, h % 2, (w_b[0, h], w_b[1, h]), bank[5 + h % 2], b_sums[h], by_act=True)

    def attend_b(h):
        buf, ob = h % 2, b_sums[h]
        done = weights_times_values(buf, (*b_ready[h], *vb_ok), ob, vb, vbm, slice(h * B_V, (h + 1) * B_V))
        col = A_HEADS * HD + h * B_V
        wait(act, done)
        ss = b_ss[:, 2 * h:2 * h + 2]
        for t in range(TILES):
            u = AC.mark(act.activation(mixed[:, t, col:col + B_V], ob.t[:, t * B_V:(t + 1) * B_V], ACT.Square,
                                       accum_out=ss[:, t:t + 1]))
        wait(pool, u, half_ok)
        u = PO.mark(pool.tensor_scalar(ss, ss, 1.0 / B_V, EPS, ALU.mult, ALU.add))
        wait(pool, u)
        b_root[h] = PO.mark(pool.tensor_tensor(ss, ss, half_neg[:, 0:TILES], ALU.pow))

    def scale_b(h):
        ob, col, ss = b_sums[h], A_HEADS * HD + h * B_V, b_ss[:, 2 * h:2 * h + 2]
        wait(act, b_root[h])
        for t in range(TILES):
            pv_b[t, h] = AC.mark(act.activation(mixed[:, t, col:col + B_V], ob.t[:, t * B_V:(t + 1) * B_V],
                                                ACT.Copy, scale=ss[:, t:t + 1]))
        ob.free = (pv_b[1, h],)

    turn_b(0)
    turn_b(1)
    attend_b(0)
    turn_b(2)
    attend_b(1)
    turn_b(3)
    attend_b(2)
    scale_b(0)
    attend_b(3)
    kaT_ok = turn_heads(ka, kaT, kT_lo[:, 0:2, :], 2, (ka_ok, kam_ok), bank[0:2], free=(b_scored,), metas=kam)
    qT_ok = turn_heads(qn, qT, qT_lo, 4, (qa_ok,), bank[5:7], free=(b_scored,))
    for h in range(1, B_HEADS):
        scale_b(h)

    wait(pe, *kaT_ok)
    exp_a, w_a, a_ready, m_ok = {}, {}, {}, {}
    a_sums = (bank[7], bank[3])

    def score_a(h):
        wait(pe, qT_ok[h // 4])
        for t in range(TILES):
            exp_a[t, h] = scores(t, h, (qT, qT_lo), (kaT, kT_lo[:, 0:2, :]), h // 4, 1, bank[(2 * h + t) % 3],
                                 (b_turned[h // 2], w_b[t, h // 2]))

    def weights_a(h):
        wait(dve, exp_a[0, h], exp_a[1, h])
        wait(dve, DV.mark(dve.reciprocal(rden[:, 1, :, h], den[:, 1, :, h])))
        for t in range(TILES):
            w_a[h] = DV.mark(dve.tensor_scalar(maps[:, t, h, :], maps[:, t, h, :], rden[:, 1, t, h:h + 1], None,
                                               ALU.mult))

    def turn_a(h):
        a_ready[h], _ = turn_map(h, h % 2, (w_a[h],), bank[4 + h % 2], bank[6])

    def attend_a(h):
        kv, half, ob, buf = h // (A_HEADS // A_KV), h % 2, a_sums[h // 2 % 2], h % 2
        sums, cols = ob.t[half * HD:(half + 1) * HD, 0:SEQ], slice(kv * HD, (kv + 1) * HD)
        wait(pe, *a_ready[h], va_ok, vam_ok)
        if half == 0:
            wait(pe, *ob.free)
        for c in range(2):
            pe.matmul(sums, va[:, c, cols], pT[:, buf, c, :], start=c == 0, stop=False)
        done = PE.mark(pe.matmul(sums, vam[:, cols], pTm[:, buf, :], start=False, stop=True))
        pT_free[buf] = (done,)
        if half == 1:
            pair = h // 2
            wait(act, done, t_qa)
            wait(dve, AC.mark(act.activation(h_hi[:, pair, :], ob.t[:, 0:SEQ], ACT.Copy)))
            m_ok[pair] = DV.mark(dve.tensor_tensor(h_lo[:, pair, :], ob.t[:, 0:SEQ], h_hi[:, pair, :],
                                                   ALU.subtract))
            ob.free = (m_ok[pair],)

    score_a(0)
    score_a(1)
    weights_a(0)
    score_a(2)
    turn_a(0)
    weights_a(1)
    for h in range(A_HEADS):
        if h + 3 < A_HEADS:
            score_a(h + 3)
        if h + 1 < A_HEADS:
            turn_a(h + 1)
        if h + 2 < A_HEADS:
            weights_a(h + 2)
        attend_a(h)
        slabs[f"out{h // 4}"].prepare((h % 4,), by_pool=h != 7)

    m_ok.update(turn_and_cut(mixed, RIGHT, lambda c: subln[:], [(pv_b[0, 3],), (pv_b[1, 3],)], bank[4:6],
                             free=(t_qa, subln_ok)))
    t_o0 = slabs["out0"].multiply(h_hi, h_lo, per_tile(MM[1]), x_ready=m_ok)

    def add_residual(pair, half, dones):
        oks = []
        for t in range(TILES):
            cols = slice(half * WIDE, (half + 1) * WIDE)
            wait(dve, dones[t])
            oks.append(DV.mark(dve.tensor_tensor(x[:, t, cols], x[:, t, cols], pair[t].t[:], ALU.add)))
            pair[t].free = (oks[t],)
        return oks

    x_left = add_residual(MM[1], 0, (t_o0, t_o0))
    one.close()

    ffn_rows = sb("ffn_rows", [P, TILES, WIDE])
    f_hi = sb("ffn_hi", [P, 4, SEQ], F32R)
    f_lo = sb("ffn_lo", [P, 4, SEQ], F32R)
    f_line = {n: Line(nc, ctx, n) for n in ("ffn_up", "ffn_acted", "ffn_hidden", "ffn_turned", "ffn_hi_done",
                                            "ffn_lo_done")}

    def feed_forward(steps, up_pieces, down_piece, chunks, squared, x_ready, scale, up_at, last_at, after):
        down_at = 4 - up_at
        acc = [bank[4:6], bank[6:8]]
        L, n_hid = f_line, chunks * P
        state = {"rows_free": (), "cut_free": (), "cut": None}

        def fill_up(i):
            for s in range(4):
                ring.fill(up_at + s, up_pieces(i, s))

        def fill_down(i, first_slot=down_at):
            for c in range(chunks):
                ring.fill(first_slot + c, [(lambda raw: raw, down_piece(i, c))])

        def down(first, last):
            if first:
                wait(pe, *(m for t in acc for b in t for m in b.free))
            for c in range(chunks):
                s = down_at + c
                wait(pe, ring.ready[s], state["cut"][c // 2])
                mm = three_passes(pe, f_hi, f_lo, ring.hi[:, s, :], ring.lo[:, s, :], c, acc, WIDE,
                                  first and c == 0, last and c == chunks - 1)
                done = ring.done(s, mm)
            state["cut_free"] = (done,)
            return done

        def turn_hidden():
            wait(pe, state["hidden"])
            state["cut"] = []
            for c0 in range(0, chunks, 2):
                b = bank[2 + c0 // 2]
                wait(pe, *b.free)
                for c in range(2):
                    for t in range(TILES):
                        tr = pe.transpose(b.t[:, c * SEQ + t * P:c * SEQ + (t + 1) * P],
                                          ffn_rows[:, t, (c0 + c) * P:(c0 + c + 1) * P], ident[:])
                turned = L["ffn_turned"].mark(tr)
                pair = b.t[:].rearrange("p (c n) -> p c n", c=2)
                wait(act, turned, *state["cut_free"])
                rounded = L["ffn_hi_done"].mark(act.activation(f_hi[:, c0:c0 + 2, :], pair, ACT.Copy))
                wait(dve, rounded)
                cut = L["ffn_lo_done"].mark(dve.tensor_tensor(f_lo[:, c0:c0 + 2, :], pair, f_hi[:, c0:c0 + 2, :],
                                                              ALU.subtract))
                b.free = (cut,)
                state["cut"].append(cut)
            state["rows_free"] = (turned,)

        def step(i, n, last=False):
            up_banks = bank[6:8] if n == 0 else bank[0:2]
            wait(pe, *(m for b in up_banks for m in b.free))
            for s in range(4):
                wait(pe, ring.ready[up_at + s])
                for c in range(2):
                    kc = 2 * s + c
                    if n == 0:
                        wait(pe, x_ready[kc])
                    w = slice(c * WIDE, (c + 1) * WIDE)
                    mm = three_passes(pe, h_hi, h_lo, ring.hi[:, up_at + s, w], ring.lo[:, up_at + s, w], kc,
                                      per_tile(up_banks), WIDE, kc == 0, kc == KC - 1)
                up_done = ring.done(up_at + s, mm)
                if n == 1 and s == 1:
                    turn_hidden()
            if n > 0:
                fill_down(i - 1)
                down(first=(n == 1), last=False)
            if last:
                fill_down(i, last_at)
            elif n != 1:
                fill_up(i + 1)
            for t in range(TILES):
                b, rows = up_banks[t], ffn_rows[:, t, 0:n_hid]
                wait(act, up_done, *state["rows_free"])
                if squared:
                    acted = L["ffn_acted"].mark(act.activation(rows, b.t[:], ACT.Relu, scale=scale[:, t:t + 1]))
                    b.free = (acted,)
                    wait(pool, acted)
                    state["hidden"] = L["ffn_hidden"].mark(pool.tensor_tensor(rows, rows, rows, ALU.mult))
                else:
                    acted = L["ffn_acted"].mark(act.activation(rows, b.t[:, 0:n_hid], ACT.Silu,
                                                               scale=scale[:, t:t + 1]))
                    wait(dve, acted)
                    hidden = L["ffn_hidden"].mark(dve.scalar_tensor_tensor(rows, b.t[:, n_hid:2 * n_hid],
                                                                           scale[:, t:t + 1], rows, ALU.mult,
                                                                           ALU.mult))
                    b.free = (hidden,)
                    state["hidden"] = hidden
            if n == 1:
                fill_up(i + 1)
            if n > 0:
                turn_hidden()

        more = run_steps(nc, step, steps)
        held = [m for f in (*ring.free, *ring.raw_free, state["rows_free"], state["cut_free"], (state["hidden"],)) for m in f]
        held += [m for b in bank[0:4] for m in b.free] + list(ring.ready) + state["cut"]
        for m in {id(m): m for m in held if m is not None}.values():
            if m.n > m.line.loop_start:
                m.n += m.line.stride * more
        step(steps - 1, steps - 1, last=True)
        after()
        done = [[None, None], [None, None]]
        for h in range(2):
            for t in range(TILES):
                for c in range(chunks):
                    s = last_at + c
                    wait(pe, ring.ready[s], state["cut"][c // 2])
                    cols = slice(h * WIDE, (h + 1) * WIDE)
                    for n, (xx, w) in enumerate(((f_hi, ring.hi), (f_hi, ring.lo), (f_lo, ring.hi))):
                        mm = pe.matmul(acc[t][h].t[:], xx[:, c, t * P:(t + 1) * P], w[:, s, cols],
                                       start=False, stop=c == chunks - 1 and n == 2)
                done[t][h] = ring.used.mark(mm)
        for c in range(chunks):
            ring.release(last_at + c, done[1][1])
        return done

    def up_slab1(i, s):
        n = D_FF // 11
        out = []
        for w, name in enumerate(("w_gate", "w_up")):
            src = a[name][0][2 * s * P:(2 * s + 2) * P, bass.ds(i * n, n)].rearrange("(c p) n -> p c n", p=P)
            out.append((lambda raw, w=w: raw.rearrange("p (c w n) -> p c w n", c=2, w=2)[:, :, w, :], src))
        return out

    def first_up(pieces, up_at):
        for s in range(4):
            ring.fill(up_at + s, pieces(0, s))

    first_up(up_slab1, 0)
    t_o1 = slabs["out1"].multiply_by_bank(h_hi, h_lo, per_tile(MM[0]))
    x_right = add_residual(MM[0], 1, (t_o1[0][0], t_o1[1][0]))
    t_o1 = t_o1[1][0]

    bg = [sb(f"b_gate{h}", [P, D]) for h in range(2)]
    two = ctx.enter_context(ExitStack())
    ln = sb("ln_v", [P, 2, GMLP], c=two)
    mask = sb("mask", [P, 4, SEQ], c=two)
    rope2 = sb("rope2", [P, TILES, 2, ROPE2], c=two)
    pT2 = sb("pT2", [P, 2, NG * 2, P], c=two)
    wsp = pT2[:, 0, 0:GROUPS, :]
    wspT = sb("w_spatial_T", [P, GROUPS, P], c=two)
    bsp = sb("b_spatial", [P, GROUPS], c=two)
    wait(pool, t_o1)
    for dst, src in [(bg[h][:], a["b_gate_2"][0:1, h * D:(h + 1) * D].broadcast_to([P, D])) for h in range(2)] + [
            (ln[:, 0, :], a["ln_v_gain_2"][0:1, :].broadcast_to([P, GMLP])),
            (ln[:, 1, :], a["ln_v_bias_2"][0:1, :].broadcast_to([P, GMLP])),
            (mask[:], a["mask"]), (rope2[:], a["rope2"].rearrange("(t p) k d -> p t k d", p=P)),
            (wsp, a["w_spatial_2"][0].rearrange("g t s -> t g s")),
            (bsp[:], a["b_spatial_2"][0].rearrange("g t -> t g"))]:
        two_in = consts.mark(pool.dma_start(dst, src, allow_slow_non_contiguous=True), 16)

    h2 = turn_and_cut(x, LEFT, lambda c: gains[:, 1, c:c + 1], [(m,) for m in x_left], bank[4:6], free=(t_o1,))
    h2.update(turn_and_cut(x, RIGHT, lambda c: gains[:, 1, c:c + 1], [(m,) for m in x_right], bank[2:4]))
    r2_ok = norm_scale(1, [(m,) for m in x_right])

    win2 = a["w_in_2"][0]
    base = {"z": 0, "q": 2 * GMLP}
    base["k"] = base["q"] + NG * WIDE
    base["v"] = base["k"] + NG * WIDE
    base["g"] = base["v"] + NG * WIDE
    order2 = [("z", 1), ("z", 0)] + [(c, g) for g in range(NG) for c in "qkv"] + [("g", 0), ("g", 1), ("a", 0),
                                                                                  ("g", 2), ("g", 3), ("b", 0), ("o", 0), ("o", 1)]
    plan = []
    for n, (kind, j) in enumerate(order2):
        if kind in "ab":
            src, chunks, cols = a["w_branch_a_2" if kind == "a" else "w_branch_b_2"][0], 4, D
        elif kind == "o":
            src, chunks, cols = a["w_out_2"][0][:, j * WIDE:(j + 1) * WIDE], KC, WIDE
        else:
            c0 = base[kind] + j * WIDE
            src, chunks, cols = win2[:, c0:c0 + WIDE], KC, WIDE
        plan.append(Slab(ring, src, 4 * (n % 2), chunks, cols))
    at = {key: n for n, key in enumerate(order2)}

    wait(act, r2_ok)
    wait(dve, r2_ok)
    ff1 = feed_forward(11, up_slab1, lambda i, c: a["w_down"][0][bass.ds((2 * i + c) * P, P), :], 2, False, h2,
                       row_scale[:, 1, :], 0, 6, plan[0].prepare)

    used_up = ff1[1][1]
    x_left = add_residual([bank[4], bank[6]], 0, [ff1[t][0] for t in range(TILES)])
    x_right = add_residual([bank[5], bank[7]], 1, [ff1[t][1] for t in range(TILES)])

    h_free = (used_up,)
    h3 = turn_and_cut(x, LEFT, lambda c: gains[:, 2, c:c + 1], [(m,) for m in x_left], bank[2:4], free=h_free)
    h3.update(turn_and_cut(x, RIGHT, lambda c: gains[:, 2, c:c + 1], [(m,) for m in x_right],
                           (bank[4], bank[6])))
    r3_ok = norm_scale(2, [(m,) for m in x_right])
    r3 = [row_scale[:, 2, t:t + 1] for t in range(TILES)]

    qk = {c: sb(f"{c}2_rows", [P, TILES, WIDE], c=two) for c in "qk"}
    u_rows = sb("u_rows", [P, TILES, GMLP], c=two)
    q2T = {c: sb(f"{c}2T", [P, HEADS2, SEQ], F32R, c=two) for c in "qk"}
    q2T_lo = {"q": f_hi, "k": f_lo}
    v2 = sb("v2", [P, NG, TILES, WIDE], c=two)
    sc = sb("scores2", [P, TILES, HEADS2, NG * SEQ], c=two)
    rot = sb("rope2_part", [P, 2, HEADS2, ROPE2], c=two)
    bn = sb("bn", [P, TILES, 8], c=two)
    gmax = sb("pattern_max2", [P, NG, TILES, HEADS2], c=two)
    gmax_ok = [None] * TILES
    smax = sb("smax2", [P, 3, TILES, HEADS2], c=two)

    def product(key, outs, ready=None, by_bank=False):
        n = at[key]
        if key == ("b", 0):
            plan[n + 1].prepare((0, 1))
            plan[n + 1].prepare((2, 3), by_pool=True)
        elif n + 1 < len(plan) and key != ("g", 1):
            plan[n + 1].prepare()
        x_hi, x_lo = (f_hi, f_lo) if key[0] in "ab" else (h_hi, h_lo)
        if by_bank:
            return plan[n].multiply_by_bank(x_hi, x_lo, outs, x_ready=ready)
        return plan[n].multiply(x_hi, x_lo, outs, x_ready=ready)

    pair_of = lambda key: MM[at[key] % 2]

    key = ("z", 1)
    done = product(key, per_tile(pair_of(key)), ready=h3)
    v_rows = ffn_rows
    wait(act, done, r3_ok)
    wait(dve, r3_ok)
    v_ok = []
    for t in range(TILES):
        b = pair_of(key)[t]
        g = AC.mark(act.activation(v_rows[:, t, :], b.t[:], ACT.Gelu_apprx_tanh, scale=r3[t]))
        b.free = (g,)
        wait(dve, g)
        s = DV.mark(dve.bn_stats(bn[:, t, 0:6], v_rows[:, t, :]))
        wait(dve, s)
        s = DV.mark(dve.bn_aggr(bn[:, t, 6:8], bn[:, t, 0:6]))
        wait(dve, s)
        s = inverse_root(bn[:, t, 7:8], 1.0, EPS)
        wait(dve, s)
        s = DV.mark(dve.tensor_scalar(v_rows[:, t, :], v_rows[:, t, :], bn[:, t, 6:7], bn[:, t, 7:8],
                                      ALU.subtract, ALU.mult))
        wait(pool, s, two_in)
        s = PO.mark(pool.tensor_tensor(v_rows[:, t, :], v_rows[:, t, :], ln[:, 0, :], ALU.mult))
        wait(pool, s)
        v_ok.append(PO.mark(pool.tensor_tensor(v_rows[:, t, :], v_rows[:, t, :], ln[:, 1, :], ALU.add)))
    wait(pe, two_in, *bank[4].free)
    for g in range(GROUPS):
        tr = pe.transpose(bank[4].t[:, g * P:(g + 1) * P], wsp[:, g, :], ident[:])
    wait(act, PE.mark(tr))
    wspT_ok = AC.mark(act.activation(wspT[:], bank[4].t[:].rearrange("p (g n) -> p g n", g=GROUPS), ACT.Copy))
    bank[4].free = (wspT_ok,)

    key = ("z", 0)
    done = product(key, per_tile(pair_of(key)))
    wait(act, done)
    for t in range(TILES):
        b = pair_of(key)[t]
        u_ok = AC.mark(act.activation(u_rows[:, t, :], b.t[:], ACT.Gelu_apprx_tanh, scale=r3[t]))
        b.free = (u_ok,)

    def spatial():
        wait(pe, *v_ok, wspT_ok)
        wait(dve, u_ok, two_in)
        for t in range(TILES):
            b = bank[4 + t]
            wait(pe, *b.free)
            for g in range(GROUPS):
                mm = pe.matmul(b.t[:, g * P:(g + 1) * P], wspT[:, g, :], v_rows[:, t, g * P:(g + 1) * P],
                               start=True, stop=True)
            wait(dve, PE.mark(mm))
            for g in range(GROUPS):
                cols = slice(g * P, (g + 1) * P)
                ok = DV.mark(dve.scalar_tensor_tensor(u_rows[:, t, cols], b.t[:, cols], bsp[:, g:g + 1],
                                                      u_rows[:, t, cols], ALU.add, ALU.mult))
            b.free = (ok,)
        return ok

    qk_free = {"q": (), "k": ()}
    T_free = ()
    s_ok = {}

    def take_rows(kind, g, done):
        pair, rows = pair_of((kind, g)), qk[kind]
        for t in range(TILES):
            wait(act, done, *qk_free[kind])
            c = AC.mark(act.activation(rows[:, t, :], pair[t].t[:], ACT.Copy, scale=r3[t]))
            pair[t].free = (c,)
            wait(dve, c, two_in)
            r = rows[:, t, :].rearrange("p (h d) -> p h d", d=HD2)
            half = ROPE2 // 2
            tab = lambda k, lo_, hi_: rope2[:, t, k, lo_:hi_].unsqueeze(1).broadcast_to([P, HEADS2, hi_ - lo_])
            dve.tensor_tensor(rot[:, 0], r[:, :, 0:ROPE2], tab(0, 0, ROPE2), ALU.mult)
            dve.tensor_tensor(rot[:, 1, :, 0:half], r[:, :, half:ROPE2], tab(1, 0, half), ALU.mult)
            s = DV.mark(dve.tensor_tensor(rot[:, 1, :, half:ROPE2], r[:, :, 0:half], tab(1, half, ROPE2), ALU.mult))
            wait(dve, s)
            ok = DV.mark(dve.tensor_tensor(r[:, :, 0:ROPE2], rot[:, 0], rot[:, 1], ALU.add))
            wait(dve, ok)
        return ok

    def turn2(kind, ok, banks):
        m = turn_heads(qk[kind], q2T[kind], q2T_lo[kind], HEADS2, (ok,), banks, free=T_free)
        qk_free[kind] = (Mark(PE, PE.n),)
        return m

    def raw_scores(g, qT_ok, kT_ok):
        wait(pe, *qT_ok, *kT_ok)
        for h in range(HEADS2):
            b = bank[4 + h % 2]
            wait(pe, *b.free)
            for t in range(TILES):
                for n, (x_, y) in enumerate(((q2T, q2T), (q2T, q2T_lo), (q2T_lo, q2T))):
                    mm = pe.matmul(b.t[:, t * SEQ:(t + 1) * SEQ], x_["q"][:, h, t * P:(t + 1) * P], y["k"][:, h, :],
                                   start=n == 0, stop=n == 2)
            scored = PE.mark(mm)
            wait(dve, scored)
            for t in range(TILES):
                m = mask[:, t if g == 0 else 1 + g, :]
                s_ok[g, h] = DV.mark(dve.scalar_tensor_tensor(sc[:, t, h, g * SEQ:(g + 1) * SEQ],
                                                              b.t[:, t * SEQ:(t + 1) * SEQ], HD2 ** -0.5, m,
                                                              ALU.mult, ALU.add))
            b.free = (s_ok[g, h],)
        wait(dve, s_ok[g, HEADS2 - 1])
        for t in range(TILES):
            gmax_ok[t] = DV.mark(dve.tensor_reduce(gmax[:, g, t, :], sc[:, t, :, g * SEQ:(g + 1) * SEQ], AX, ALU.max,
                                                   negate=True))
        return scored

    def gate_sums(j, dst, done, free=()):
        pair = pair_of(("g", j))
        cols = slice((j % 2) * WIDE, (j % 2 + 1) * WIDE)
        wait(dve, done, two_in, *free)
        for t in range(TILES):
            s = DV.mark(dve.scalar_tensor_tensor(dst[:, t, cols], pair[t].t[:], r3[t], bg[j // 2][:, cols],
                                                 ALU.mult, ALU.add))
            pair[t].free = (s,)
        return s

    def sigmoid(dst, ready):
        wait(act, ready)
        for t in range(TILES):
            ok = AC.mark(act.activation(dst[:, t, :], dst[:, t, :], ACT.Sigmoid))
        return ok

    for g in range(NG):
        key = ("q", g)
        done = product(key, per_tile(pair_of(key)))
        if g > 0:
            T_free = (raw_scores(g - 1, qT_ok, kT_ok),)
        q_ok = take_rows("q", g, done)
        if g == 0:
            ya_ok = spatial()
        key = ("k", g)
        done = product(key, per_tile(pair_of(key)))
        qT_ok = turn2("q", q_ok, bank[6:8])
        k_ok = take_rows("k", g, done)
        key = ("v", g)
        done = product(key, per_tile(pair_of(key)))
        pair = pair_of(key)
        wait(act, done)
        wait(dve, done)
        v0 = AC.mark(act.activation(v2[:, g, 0, :], pair[0].t[:], ACT.Copy, scale=r3[0]))
        v1 = DV.mark(dve.tensor_scalar(v2[:, g, 1, :], pair[1].t[:], r3[1], None, ALU.mult))
        pair[0].free, pair[1].free = (v0,), (v1,)
        kT_ok = turn2("k", k_ok, bank[6:8])
    done_g0 = product(("g", 0), per_tile(pair_of(("g", 0))))
    scored = raw_scores(NG - 1, qT_ok, kT_ok)
    g_a = tmp
    gate_sums(0, g_a, done_g0, free=(r3_ok,))
    v_all = (v0, v1)

    e2 = {}
    for t in range(TILES):
        wait(dve, gmax_ok[t])
        m = DV.mark(dve.tensor_tensor(smax[:, 0, t, :], gmax[:, 0, t, :], gmax[:, 1, t, :], ALU.min))
        wait(dve, m)
        smax_ok = DV.mark(dve.tensor_tensor(smax[:, 0, t, :], smax[:, 0, t, :], gmax[:, 2, t, :], ALU.min))

    def exp2(n):
        t, h = n // HEADS2, n % HEADS2
        wait(act, smax_ok)
        e2[t, h] = AC.mark(act.activation(sc[:, t, h, :], sc[:, t, h, :], ACT.Exp, bias=smax[:, 0, t, h:h + 1],
                                          accum_out=smax[:, 1, t, h:h + 1]))

    for n in range(HEADS2 + 1):
        exp2(n)

    yb = qk["q"]
    pT2_free = [(), ()]
    yb_ok = None

    def turn2_map(n):
        t, h, buf = n // HEADS2, n % HEADS2, n % 2
        wait(pe, e2[t, h])
        cps = []
        for j in range(2):
            b = bank[4 + 2 * buf + j]
            wait(pe, *b.free)
            for c in range(3):
                kc = 3 * j + c
                tr = pe.transpose(b.t[:, c * P:(c + 1) * P], sc[:, t, h, kc * P:(kc + 1) * P], ident[:])
            done = PE.mark(tr)
            dst, src = pT2[:, buf, 3 * j:3 * j + 3, :], b.t[:, 0:3 * P].rearrange("p (c n) -> p c n", c=3)
            if j == 0:
                wait(act, done, *pT2_free[buf])
                cps.append(AC.mark(act.activation(dst, src, ACT.Copy)))
            else:
                wait(dve, done, *pT2_free[buf])
                cps.append(DV.mark(dve.tensor_copy(dst, src)))
            b.free = (cps[-1],)
        return cps

    def attend2(n, cps):
        t, h, buf = n // HEADS2, n % HEADS2, n % 2
        ob = bank[n % 4]
        sums = ob.t[:, 0:P]
        wait(pe, *cps, *v_all, *ob.free)
        for kc in range(2 * NG):
            mm = pe.matmul(sums, pT2[:, buf, kc, :], v2[:, kc // 2, kc % 2, h * HD2:(h + 1) * HD2],
                           start=(kc == 0), stop=(kc == 2 * NG - 1))
        done = PE.mark(mm)
        pT2_free[buf] = (done,)
        if h == 0:
            wait(dve, e2[t, HEADS2 - 1])
            wait(dve, DV.mark(dve.reciprocal(smax[:, 2, t, :], smax[:, 1, t, :])))
        wait(dve, done)
        ok = DV.mark(dve.tensor_scalar(yb[:, t, h * HD2:(h + 1) * HD2], sums, smax[:, 2, t, h:h + 1], None, ALU.mult))
        ob.free = (ok,)
        return ok, done

    done_g1 = product(("g", 1), per_tile(pair_of(("g", 1))))
    ga_ok = gate_sums(1, g_a, done_g1)
    cps = turn2_map(0)
    ya_cut = turn_and_cut(u_rows, LEFT, None, [(ya_ok,), ()], bank[2:4], out_hi=f_hi, out_lo=f_lo, free=(scored,))
    for n in range(TILES * HEADS2):
        if n + 5 < TILES * HEADS2:
            exp2(n + 5)
        ahead = turn2_map(n + 1) if n + 1 < TILES * HEADS2 else None
        yb_ok, last_pv = attend2(n, cps)
        if n < 4:
            plan[at["a", 0]].prepare((n,))
        cps = ahead

    ga_ok = sigmoid(g_a, ga_ok)
    outs = [bank[0:2], bank[2:4]]
    done = product(("a", 0), outs, ready=ya_cut)
    for t in range(TILES):
        for half in range(2):
            cols, b = slice(half * WIDE, (half + 1) * WIDE), outs[t][half]
            wait(dve, done, ga_ok)
            m_ok = DV.mark(dve.tensor_tensor(tmp[:, t, cols], tmp[:, t, cols], b.t[:], ALU.mult))
            b.free = (m_ok,)
    yb_cut = turn_and_cut(yb, LEFT, None, [(yb_ok,), ()], bank[4:6], out_hi=f_hi, out_lo=f_lo, free=(done,))
    g_b = sc[:].rearrange("p t h n -> p (t h n)")[:, 0:TILES * D].rearrange("p (t n) -> p t n", t=TILES)
    for j in (2, 3):
        done = product(("g", j), per_tile(pair_of(("g", j))))
        gb_ok = gate_sums(j, g_b, done, free=(last_pv,))
    h_read = done
    gb_ok = sigmoid(g_b, gb_ok)
    done = product(("b", 0), outs, ready=yb_cut, by_bank=True)
    m_half = []
    for half in range(2):
        for t in range(TILES):
            cols, b = slice(half * WIDE, (half + 1) * WIDE), outs[t][half]
            wait(dve, done[t][half], gb_ok, m_ok)
            s = DV.mark(dve.tensor_tensor(g_b[:, t, cols], g_b[:, t, cols], b.t[:], ALU.mult))
            b.free = (s,)
            wait(dve, s)
            s = DV.mark(dve.tensor_tensor(tmp[:, t, cols], tmp[:, t, cols], g_b[:, t, cols], ALU.add))
            m_half.append((s,))
    merged = turn_and_cut(tmp, LEFT, None, m_half[0:2], bank[4:6], free=(h_read,))
    merged.update(turn_and_cut(tmp, RIGHT, None, m_half[2:4], bank[6:8]))
    wait(pool, ga_ok)
    post_in = post_load[0].mark(pool.dma_start(bg[0][:], a["norm_mix_post_2"][0:1, :].broadcast_to([P, D])), 16)
    wait(pool, gb_ok)
    post2_in = post_load[1].mark(pool.dma_start(bg[1][:], a["norm_mlp_post_2"][0:1, :].broadcast_to([P, D])), 16)
    two.close()

    def up_slab2(i, s):
        src = a["w_up_2"][0][2 * s * P:(2 * s + 2) * P, bass.ds(i * WIDE, WIDE)].rearrange("(c p) n -> p c n", p=P)
        return [(lambda raw: raw.rearrange("p (c n) -> p c n", c=2), src)]

    m0, m1 = ("o", 0), ("o", 1)
    done0 = product(m0, per_tile(pair_of(m0)), ready=merged)
    first_up(up_slab2, 4)
    done1 = product(m1, per_tile(pair_of(m1)), by_bank=True)

    def post_norm(banks_of, dones, gain, gain_in, free):
        for t in range(TILES):
            ss = stat[:, 4 + 2 * t:6 + 2 * t]
            halves = [(banks_of[t][half], slice(half * WIDE, (half + 1) * WIDE)) for half in range(2)]
            squared = []
            wait(act, *free)
            for half, (b, cols) in enumerate(halves):
                wait(act, dones[t][half], *squared)
                squared.append(AC.mark(act.activation(ffn_rows[:, t, :], b.t[:], ACT.Square,
                                                      accum_out=ss[:, half:half + 1])))
            wait(dve, gain_in, *free)
            for half, (b, cols) in enumerate(halves):
                wait(dve, squared[half])
                if half == 1:
                    u = DV.mark(dve.tensor_tensor(ss[:, 0:1], ss[:, 0:1], ss[:, 1:2], ALU.add))
                    wait(dve, u)
                    root = inverse_root(ss[:, 0:1], 1.0 / D, EPS)
                u = DV.mark(dve.tensor_tensor(tmp[:, t, cols], b.t[:], gain[:, cols], ALU.mult))
                b.free = (u,)
            wait(dve, root, u)
            yield [DV.mark(dve.scalar_tensor_tensor(x[:, t, cols], tmp[:, t, cols], ss[:, 0:1], x[:, t, cols],
                                                    ALU.mult, ALU.add)) for _, cols in halves]

    mix_banks = [[pair_of(m0)[t], pair_of(m1)[t]] for t in range(TILES)]
    x_marks = list(post_norm(mix_banks, [(done0, done1[t][0]) for t in range(TILES)], bg[0], post_in,
                             tuple(merged.values())))
    done1 = done1[1][0]
    h4 = turn_and_cut(x, LEFT, lambda c: gains[:, 3, c:c + 1], [(m[0],) for m in x_marks], bank[4:6], free=(done1,))
    h4.update(turn_and_cut(x, RIGHT, lambda c: gains[:, 3, c:c + 1], [(m[1],) for m in x_marks],
                           (mix_banks[0][0], mix_banks[0][1])))
    r4_ok = norm_scale(3, x_marks)
    wait(act, r4_ok)
    wait(dve, r4_ok)
    ff2 = feed_forward(8, up_slab2, lambda i, c: a["w_down_2"][0][bass.ds((4 * i + c) * P, P), :], 4, True, h4,
                       row_scale[:, 3, :], 4, 4, lambda: None)

    acc_banks = [bank[4:6], bank[6:8]]
    stored = [Line(nc, ctx, f"stored{t}") for t in range(TILES)]
    for t, oks in enumerate(post_norm(acc_banks, ff2, bg[1], post2_in, ())):
        for half, ok in enumerate(oks):
            cols = slice(half * WIDE, (half + 1) * WIDE)
            wait(sp, ok)
            stored[t].mark(sp.dma_start(out[0, t * P:(t + 1) * P, cols], x[:, t, cols]), 16)
    wait(sp, *[Mark(line, line.n) for line in stored])


_INS = ["x", "meta_tokens", "attn_norm_g", "w_in", "a_q_norm_g", "a_k_norm_g", "b_q_norm_g", "b_k_norm_g",
        "b_lambda_q1", "b_lambda_k1", "b_lambda_q2", "b_lambda_k2", "b_subln_g", "w_out", "ffn_norm_g", "w_gate",
        "w_up", "w_down", "norm_mix_pre_2", "w_in_2", "b_gate_2", "ln_v_gain_2", "ln_v_bias_2", "w_spatial_2",
        "b_spatial_2", "w_branch_a_2", "w_branch_b_2", "w_out_2", "norm_mix_post_2", "norm_mlp_pre_2", "w_up_2",
        "w_down_2", "norm_mlp_post_2"]


def kernel(**inputs):
    import concourse.bacc as _bacc
    from concourse.bass_utils import run_bass_kernel_spmd as _run

    nc = _bacc.Bacc("TRN2", target_bir_lowering=False, num_devices=1)
    arrays = {name: np.ascontiguousarray(inputs[name]) for name in _INS}
    one, two = rope_tables()
    arrays.update(rope1=one, rope2=two, mask=masks(), ident=np.eye(P, dtype=np.float32))
    args = {n: nc.dram_tensor(f"in_{n}", v.shape, mybir.dt.from_np(v.dtype), kind="ExternalInput").ap()
            for n, v in arrays.items()}
    out = nc.dram_tensor("out_0", (1, SEQ, D), F32, kind="ExternalOutput").ap()
    program(nc, args, out)
    r = _run(nc, [{f"in_{n}": v for n, v in arrays.items()}], core_ids=[0])
    return r.results[0]["out_0"]
```
